# Optimizing a Trainium2 kernel written in Bass

```python
import math
import jax, jax.numpy as jnp
from jax import lax
import numpy as np

D_MODEL = 1024
BATCH = 1
SEQ = 512
DEPTH = 2

N_A_LAYERS = DEPTH // 2
N_B_LAYERS = DEPTH - N_A_LAYERS
EPS = 1e-6

A_HEADS = 8
A_DK = 128
A_DV = 256
A_QK_W = A_HEADS * A_DK
A_V_W = A_HEADS * A_DV
A_CONV_CH = 2 * A_QK_W + A_V_W
A_IN_W = A_CONV_CH + A_V_W + 2 * A_HEADS
CONV_W = 4
CHUNK = 64

B_Q_HEADS = 32
B_KV_HEADS = 4
B_GROUP = B_Q_HEADS // B_KV_HEADS
B_HD = 64
B_W = B_Q_HEADS * B_HD
B_KV_W = B_KV_HEADS * B_HD
WINDOW = 128
BLOCK = 128

N_BUCKETS = 32
MAX_DIST = 128


def rms_norm(x, g):
    xf = x.astype(jnp.float32)
    y = xf * lax.rsqrt(jnp.mean(xf * xf, axis=-1, keepdims=True) + EPS)
    return (y * g.astype(jnp.float32)).astype(x.dtype)

def l2_norm(x):
    xf = x.astype(jnp.float32)
    return xf * lax.rsqrt(jnp.sum(xf * xf, axis=-1, keepdims=True) + EPS)

def causal_depthwise_conv(x, w):
    c = x.shape[-1]
    return lax.conv_general_dilated(
        x, w[:, None, :].astype(x.dtype), window_strides=(1,),
        padding=[(CONV_W - 1, 0)], dimension_numbers=("NWC", "WIO", "NWC"),
        feature_group_count=c)

def chunk_gated_delta_rule(q, k, v, g, beta):
    B, T, H, _ = q.shape
    N = T // CHUNK

    def chunks(t):
        return t.reshape(B, N, CHUNK, H, -1).transpose(0, 1, 3, 2, 4)

    q, k, v = chunks(q), chunks(k), chunks(v)
    g = jnp.cumsum(g.reshape(B, N, CHUNK, H).transpose(0, 1, 3, 2), axis=-1)
    beta = beta.reshape(B, N, CHUNK, H).transpose(0, 1, 3, 2)

    tri = jnp.tril(jnp.ones((CHUNK, CHUNK), dtype=bool))
    strict = jnp.tril(jnp.ones((CHUNK, CHUNK), dtype=bool), -1)
    decay = jnp.exp(jnp.where(tri, g[..., :, None] - g[..., None, :], -jnp.inf))

    kk = jnp.einsum("bnhcd,bnhsd->bnhcs", k, k)
    lower = jnp.where(strict, beta[..., :, None] * kk * decay, 0.0)
    rhs = jnp.concatenate([v * beta[..., None], k * (beta * jnp.exp(g))[..., None]], axis=-1)
    sol = lax.linalg.triangular_solve(lower, rhs, left_side=True, lower=True, unit_diagonal=True)
    u, w = sol[..., :A_DV], sol[..., A_DV:]

    qk = jnp.einsum("bnhcd,bnhsd->bnhcs", q, k) * decay
    q_dec = q * jnp.exp(g)[..., None]
    k_dec = k * jnp.exp(g[..., -1:] - g)[..., None]
    g_last = jnp.exp(g[..., -1])

    def step(S, inp):
        qk_i, qd_i, kd_i, u_i, w_i, gl_i = inp
        v_new = u_i - jnp.einsum("bhck,bhkv->bhcv", w_i, S)
        o = jnp.einsum("bhck,bhkv->bhcv", qd_i, S) + jnp.einsum("bhcs,bhsv->bhcv", qk_i, v_new)
        S = S * gl_i[..., None, None] + jnp.einsum("bhck,bhcv->bhkv", kd_i, v_new)
        return S, o

    xs = tuple(t.swapaxes(0, 1) for t in (qk, q_dec, k_dec, u, w, g_last))
    S0 = jnp.zeros((B, H, A_DK, A_DV), jnp.float32)
    _, o = lax.scan(step, S0, xs)
    return o.transpose(1, 0, 3, 2, 4).reshape(B, T, H, A_DV)

def gated_deltanet_mixer(h, w_in, conv_w, a_log, dt_bias, o_gain, w_out):
    B, T, _ = h.shape
    proj = h @ w_in
    qkv, z, ab = jnp.split(proj, [A_CONV_CH, A_CONV_CH + A_V_W], axis=-1)
    qkv = jax.nn.silu(causal_depthwise_conv(qkv, conv_w))
    q, k, v = jnp.split(qkv, [A_QK_W, 2 * A_QK_W], axis=-1)
    q = l2_norm(q.reshape(B, T, A_HEADS, A_DK)) * (A_DK ** -0.5)
    k = l2_norm(k.reshape(B, T, A_HEADS, A_DK))
    v = v.reshape(B, T, A_HEADS, A_DV).astype(jnp.float32)
    b_logit, a_logit = jnp.split(ab.astype(jnp.float32), 2, axis=-1)
    beta = jax.nn.sigmoid(b_logit)
    g = -jnp.exp(a_log.astype(jnp.float32)) * jax.nn.softplus(a_logit + dt_bias.astype(jnp.float32))
    o = chunk_gated_delta_rule(q, k, v, g, beta)
    o = rms_norm(o, o_gain) * jax.nn.silu(z.reshape(B, T, A_HEADS, A_DV).astype(jnp.float32))
    return o.reshape(B, T, A_V_W).astype(h.dtype) @ w_out

def shared_kv(x, kv_norm, w_kv, k_gain):
    B, T, _ = x.shape
    nb = T // BLOCK
    kv = rms_norm(x, kv_norm) @ w_kv
    k, v = jnp.split(kv, 2, axis=-1)
    k = rms_norm(k.reshape(B, T, B_KV_HEADS, B_HD), k_gain)
    v = v.reshape(B, T, B_KV_HEADS, B_HD)

    def band(t):
        tb = t.reshape(B, nb, BLOCK, B_KV_HEADS, B_HD)
        prev = jnp.concatenate([jnp.zeros_like(tb[:, :1]), tb[:, :-1]], axis=1)
        return jnp.concatenate([prev, tb], axis=2)

    return band(k), band(v)

def t5_causal_bucket(dist):
    n = np.maximum(dist, 0)
    max_exact = N_BUCKETS // 2
    large = max_exact + (np.log(np.maximum(n, 1) / max_exact) / np.log(MAX_DIST / max_exact)
                         * (N_BUCKETS - max_exact)).astype(np.int64)
    large = np.minimum(large, N_BUCKETS - 1)
    return np.where(n < max_exact, n, large).astype(np.int32)

def band_bias_and_mask(rel_bias, seq):
    nb = seq // BLOCK
    qi = np.arange(BLOCK)[:, None]
    s = np.arange(2 * BLOCK)[None, :]
    dist = qi + BLOCK - s
    in_window = (dist >= 0) & (dist < WINDOW)
    bias = rel_bias.astype(jnp.float32)[jnp.asarray(t5_causal_bucket(dist))]
    bias = bias.transpose(2, 0, 1).reshape(B_KV_HEADS, B_GROUP, BLOCK, 2 * BLOCK)
    key_pos = np.arange(nb)[:, None] * BLOCK - BLOCK + s
    mask = in_window[None] & (key_pos >= 0)[:, None, :]
    return bias, jnp.asarray(mask)

def swa_sink_mixer(h, w_in, q_gain, sinks, w_out, k_band, v_band, bias, mask):
    B, T, _ = h.shape
    nb = T // BLOCK
    q, z = jnp.split(h @ w_in, 2, axis=-1)
    q = rms_norm(q.reshape(B, T, B_Q_HEADS, B_HD), q_gain) * (B_HD ** -0.5)
    q = q.reshape(B, nb, BLOCK, B_KV_HEADS, B_GROUP, B_HD)
    logits = jnp.einsum("bnqkgd,bnskd->bnkgqs", q, k_band).astype(jnp.float32) + bias
    logits = jnp.where(mask[None, :, None, None], logits, -jnp.inf)
    sink = sinks.astype(jnp.float32).reshape(B_KV_HEADS, B_GROUP)[..., None, None]
    m = jnp.maximum(jnp.max(logits, axis=-1, keepdims=True), sink)
    p = jnp.exp(logits - m)
    probs = p / (jnp.sum(p, axis=-1, keepdims=True) + jnp.exp(sink - m))
    o = jnp.einsum("bnkgqs,bnskd->bnqkgd", probs.astype(v_band.dtype), v_band)
    o = o.reshape(B, T, B_W) * jax.nn.silu(z)
    return o @ w_out

def first_inputs(seed: int = 0) -> dict:
    key = jax.random.key(seed)
    ks = jax.random.split(key, 20)
    f = jnp.float32
    D = D_MODEL
    nA, nB = N_A_LAYERS, N_B_LAYERS

    def nrm(k, shape, scale):
        return jax.random.normal(k, shape, f) * scale

    dt = jnp.exp(jax.random.uniform(ks[5], (nA, A_HEADS), f, math.log(1e-3), math.log(1e-1)))
    return {
        "x": nrm(ks[0], (BATCH, SEQ, D), 1.0),
        "a_norm": 1.0 + nrm(ks[1], (nA, D), 0.02),
        "a_w_in": nrm(ks[2], (nA, D, A_IN_W), D ** -0.5),
        "a_conv": nrm(ks[3], (nA, CONV_W, A_CONV_CH), CONV_W ** -0.5),
        "a_A_log": jnp.log(jax.random.uniform(ks[4], (nA, A_HEADS), f, 1.0, 16.0)),
        "a_dt_bias": dt + jnp.log(-jnp.expm1(-dt)),
        "a_o_gain": 1.0 + nrm(ks[6], (nA, A_DV), 0.02),
        "a_w_out": nrm(ks[7], (nA, A_V_W, D), A_V_W ** -0.5),
        "kv_norm": 1.0 + nrm(ks[8], (D,), 0.02),
        "w_kv": nrm(ks[9], (D, 2 * B_KV_W), D ** -0.5),
        "k_gain": 1.0 + nrm(ks[10], (B_HD,), 0.02),
        "rel_bias": nrm(ks[11], (N_BUCKETS, B_Q_HEADS), 0.5),
        "b_norm": 1.0 + nrm(ks[12], (nB, D), 0.02),
        "b_w_in": nrm(ks[13], (nB, D, 2 * B_W), D ** -0.5),
        "b_q_gain": 1.0 + nrm(ks[14], (nB, B_HD), 0.02),
        "b_sinks": nrm(ks[15], (nB, B_Q_HEADS), 0.5),
        "b_w_out": nrm(ks[16], (nB, B_W, D), B_W ** -0.5),
    }

def first_block(x, a_norm, a_w_in, a_conv, a_A_log, a_dt_bias, a_o_gain, a_w_out,
              kv_norm, w_kv, k_gain, rel_bias,
              b_norm, b_w_in, b_q_gain, b_sinks, b_w_out):
    bias, mask = band_bias_and_mask(rel_bias, x.shape[1])
    k_band = v_band = None
    for layer in range(DEPTH):
        if layer < N_A_LAYERS:
            i = layer
            x = x + gated_deltanet_mixer(rms_norm(x, a_norm[i]), a_w_in[i], a_conv[i], a_A_log[i],
                                         a_dt_bias[i], a_o_gain[i], a_w_out[i])
            if layer == N_A_LAYERS - 1:
                k_band, v_band = shared_kv(x, kv_norm, w_kv, k_gain)
        else:
            j = layer - N_A_LAYERS
            x = x + swa_sink_mixer(rms_norm(x, b_norm[j]), b_w_in[j], b_q_gain[j], b_sinks[j],
                                   b_w_out[j], k_band, v_band, bias, mask)
    return x


DEPTH_2 = 1

N_META = 16

D_MIX = D_MODEL
M_HEADS = 4
M_HEAD_DIM = (D_MIX // 2) // M_HEADS
M_WIDTH = M_HEADS * M_HEAD_DIM
F_HEADS = 8
F_HEAD_DIM = (D_MIX - M_WIDTH) // F_HEADS
F_WIDTH = F_HEADS * F_HEAD_DIM
Q_BLOCK = 128

PROJ_SIZES = (M_WIDTH, M_WIDTH, M_WIDTH, M_WIDTH, M_HEADS, M_HEADS, F_WIDTH, F_WIDTH, F_WIDTH, F_HEADS)
PROJ_DIM = 4 * M_WIDTH + 2 * M_HEADS + 3 * F_WIDTH + F_HEADS

PEER_HEADS = 8
N_KEYS = 128
N_EXPERTS = N_KEYS * N_KEYS
PEER_TOPK = 16
PEER_QDIM = 256
PEER_HALF = PEER_QDIM // 2
PEER_TOKEN_BLOCK = 128


def _rmsnorm(x, g):
    xf = x.astype(jnp.float32)
    y = xf * lax.rsqrt(jnp.mean(xf * xf, axis=-1, keepdims=True) + EPS)
    return (y * g.astype(jnp.float32)).astype(x.dtype)

def _proj_splits():
    out, acc = [], 0
    for s in PROJ_SIZES[:-1]:
        acc += s
        out.append(acc)
    return out

def _causal_dwconv(x, w):
    c = x.shape[-1]
    return lax.conv_general_dilated(
        x, w.astype(x.dtype)[:, None, :], window_strides=(1,),
        padding=[(CONV_W - 1, 0)], dimension_numbers=("NWC", "WIO", "NWC"),
        feature_group_count=c)

def _mlstm(q, k, v, o_pre, i_pre, f_pre, out_gain):
    f32 = jnp.float32
    B, L, _ = q.shape
    n_chunks = -(-L // CHUNK)
    pad = n_chunks * CHUNK - L

    def heads(t):
        t = jnp.pad(t.astype(f32), ((0, 0), (0, pad), (0, 0)))
        return t.reshape(B, n_chunks, CHUNK, M_HEADS, M_HEAD_DIM).transpose(1, 0, 3, 2, 4)

    def gates(t):
        t = jnp.pad(t.astype(f32), ((0, 0), (0, pad), (0, 0)))
        return t.reshape(B, n_chunks, CHUNK, M_HEADS).transpose(1, 0, 3, 2)

    qc = heads(q)
    kc = heads(k) * (M_HEAD_DIM ** -0.5)
    vc = heads(v)
    logi = gates(i_pre)
    logf = jax.nn.log_sigmoid(gates(f_pre))
    causal = jnp.asarray(np.tril(np.ones((CHUNK, CHUNK), dtype=bool)))

    def step(carry, inp):
        C, n, m = carry
        qb, kb, vb, li, lf = inp
        b = jnp.cumsum(lf, axis=-1)
        Dm = jnp.where(causal, b[..., :, None] - b[..., None, :] + li[..., None, :], -jnp.inf)
        m_inter = b + m[..., None]
        m_t = jnp.maximum(m_inter, jnp.max(Dm, axis=-1))
        S = jnp.einsum('bhtd,bhsd->bhts', qb, kb) * jnp.exp(Dm - m_t[..., None])
        w_inter = jnp.exp(m_inter - m_t)
        num = jnp.einsum('bhts,bhsd->bhtd', S, vb) + w_inter[..., None] * jnp.einsum('bhvk,bhtk->bhtv', C, qb)
        den = jnp.sum(S, axis=-1) + w_inter * jnp.einsum('bhk,bhtk->bht', n, qb)
        h = num / jnp.maximum(jnp.abs(den), jnp.exp(-m_t))[..., None]
        b_end = b[..., -1]
        g = b_end[..., None] - b + li
        m_new = jnp.maximum(b_end + m, jnp.max(g, axis=-1))
        decay = jnp.exp(b_end + m - m_new)
        wg = jnp.exp(g - m_new[..., None])
        C = decay[..., None, None] * C + jnp.einsum('bhs,bhsv,bhsk->bhvk', wg, vb, kb)
        n = decay[..., None] * n + jnp.einsum('bhs,bhsk->bhk', wg, kb)
        return (C, n, m_new), h

    init = (jnp.zeros((B, M_HEADS, M_HEAD_DIM, M_HEAD_DIM), f32),
            jnp.zeros((B, M_HEADS, M_HEAD_DIM), f32),
            jnp.zeros((B, M_HEADS), f32))
    _, h = lax.scan(step, init, (qc, kc, vc, logi, logf))
    h = h.transpose(1, 0, 3, 2, 4).reshape(B, n_chunks * CHUNK, M_HEADS, M_HEAD_DIM)[:, :L]
    h = _rmsnorm(h, out_gain.reshape(M_HEADS, M_HEAD_DIM)).reshape(B, L, M_WIDTH)
    h = h * jax.nn.sigmoid(o_pre.astype(f32))
    return h.astype(q.dtype)

def _forgetting_attention(q, k, v, f_pre, g_q, g_k):
    B, L, _ = q.shape

    def heads(t):
        return t.reshape(B, L, F_HEADS, F_HEAD_DIM).transpose(0, 2, 1, 3)

    qh = _rmsnorm(heads(q), g_q)
    kh = _rmsnorm(heads(k), g_k)
    vh = heads(v)
    c = jnp.cumsum(jax.nn.log_sigmoid(f_pre.astype(jnp.float32)), axis=1).transpose(0, 2, 1)
    scale = F_HEAD_DIM ** -0.5
    outs = []
    for start in range(0, L, Q_BLOCK):
        end = min(start + Q_BLOCK, L)
        logits = jnp.einsum('bhtd,bhsd->bhts', qh[:, :, start:end], kh[:, :, :end]).astype(jnp.float32) * scale
        logits = logits + c[:, :, start:end, None] - c[:, :, None, :end]
        mask = np.arange(start, end)[:, None] >= np.arange(end)[None, :]
        logits = jnp.where(mask, logits, -jnp.inf)
        p = jax.nn.softmax(logits, axis=-1).astype(vh.dtype)
        outs.append(jnp.einsum('bhts,bhsd->bhtd', p, vh[:, :, :end]))
    out = jnp.concatenate(outs, axis=2)
    return out.transpose(0, 2, 1, 3).reshape(B, L, F_WIDTH)

def _peer(x, w_query, sub_keys, u_emb, v_emb):
    B, L, D = x.shape
    T = B * L
    Tp = -(-T // PEER_TOKEN_BLOCK) * PEER_TOKEN_BLOCK
    xt = jnp.pad(x.reshape(T, D), ((0, Tp - T), (0, 0))).reshape(-1, PEER_TOKEN_BLOCK, D)
    keys32 = sub_keys.astype(jnp.float32)

    def block(xb):
        tb = xb.shape[0]
        qh = (xb @ w_query).astype(jnp.float32).reshape(tb, PEER_HEADS, 2, PEER_HALF)
        scores = jnp.einsum('thpc,hpnc->thpn', qh, keys32)
        val, idx = lax.top_k(scores, PEER_TOPK)
        cand = (val[:, :, 0, :, None] + val[:, :, 1, None, :]).reshape(tb, PEER_HEADS, PEER_TOPK * PEER_TOPK)
        cand_id = (idx[:, :, 0, :, None] * N_KEYS + idx[:, :, 1, None, :]).reshape(tb, PEER_HEADS, PEER_TOPK * PEER_TOPK)
        top_s, pos = lax.top_k(cand, PEER_TOPK)
        ids = jnp.take_along_axis(cand_id, pos, axis=-1).reshape(tb, PEER_HEADS * PEER_TOPK)
        gate = jax.nn.softmax(top_s, axis=-1).reshape(tb, PEER_HEADS * PEER_TOPK)
        u = u_emb[ids]
        act = jax.nn.gelu(jnp.einsum('ted,td->te', u, xb).astype(jnp.float32), approximate=False)
        w = (gate * act).astype(xb.dtype)
        return jnp.einsum('te,ted->td', w, v_emb[ids])

    out = lax.map(block, xt)
    return out.reshape(Tp, D)[:T].reshape(B, L, D)

def second_inputs(seed: int = 0) -> dict:
    key = jax.random.key(seed)
    ks = jax.random.split(key, 20)
    f32 = jnp.float32
    nrm = lambda k, shape, s: jax.random.normal(k, shape, f32) * s
    fbias_m = jnp.broadcast_to(jnp.linspace(3.0, 6.0, M_HEADS, dtype=f32), (DEPTH_2, M_HEADS))
    fbias_f = jnp.broadcast_to(jnp.linspace(2.0, 6.0, F_HEADS, dtype=f32), (DEPTH_2, F_HEADS))
    return {
        "x": nrm(ks[0], (BATCH, SEQ, D_MODEL), 1.0),
        "meta_tokens": nrm(ks[1], (N_META, D_MODEL), 1.0),
        "norm_mix": 1.0 + nrm(ks[2], (DEPTH_2, D_MODEL), 0.02),
        "w_in": nrm(ks[3], (DEPTH_2, D_MODEL, PROJ_DIM), D_MODEL ** -0.5),
        "conv_qk": nrm(ks[4], (DEPTH_2, CONV_W, 2 * M_WIDTH), CONV_W ** -0.5),
        "b_igate": nrm(ks[5], (DEPTH_2, M_HEADS), 0.1),
        "b_fgate_m": fbias_m + nrm(ks[6], (DEPTH_2, M_HEADS), 0.1),
        "m_out_norm": 1.0 + nrm(ks[7], (DEPTH_2, M_WIDTH), 0.02),
        "b_fgate_f": fbias_f + nrm(ks[8], (DEPTH_2, F_HEADS), 0.1),
        "f_q_norm": 1.0 + nrm(ks[9], (DEPTH_2, F_HEAD_DIM), 0.02),
        "f_k_norm": 1.0 + nrm(ks[10], (DEPTH_2, F_HEAD_DIM), 0.02),
        "w_out": nrm(ks[11], (DEPTH_2, D_MIX, D_MODEL), D_MIX ** -0.5),
        "norm_ffn": 1.0 + nrm(ks[12], (DEPTH_2, D_MODEL), 0.02),
        "peer_query": nrm(ks[13], (DEPTH_2, D_MODEL, PEER_HEADS * PEER_QDIM), D_MODEL ** -0.5),
        "peer_sub_keys": nrm(ks[14], (DEPTH_2, PEER_HEADS, 2, N_KEYS, PEER_HALF), PEER_HALF ** -0.5),
        "peer_u": nrm(ks[15], (DEPTH_2, N_EXPERTS, D_MODEL), D_MODEL ** -0.5),
        "peer_v": nrm(ks[16], (DEPTH_2, N_EXPERTS, D_MODEL), 0.1),
    }

def second_block(x, meta_tokens, norm_mix, w_in, conv_qk, b_igate, b_fgate_m, m_out_norm,
              b_fgate_f, f_q_norm, f_k_norm, w_out, norm_ffn, peer_query, peer_sub_keys,
              peer_u, peer_v):
    B = x.shape[0]
    meta = jnp.broadcast_to(meta_tokens.astype(x.dtype)[None], (B, N_META, D_MODEL))
    h_res = jnp.concatenate([meta, x], axis=1)
    splits = _proj_splits()
    for layer in range(DEPTH_2):
        hn = _rmsnorm(h_res, norm_mix[layer])
        z = hn @ w_in[layer]
        mq, mk, mv, mo, mi, mf, fq, fk, fv, ff = jnp.split(z, splits, axis=-1)
        qk = jax.nn.silu(_causal_dwconv(jnp.concatenate([mq, mk], axis=-1), conv_qk[layer]))
        mq, mk = jnp.split(qk, 2, axis=-1)
        y_m = _mlstm(mq, mk, mv, mo, mi + b_igate[layer], mf + b_fgate_m[layer], m_out_norm[layer])
        y_f = _forgetting_attention(fq, fk, fv, ff + b_fgate_f[layer], f_q_norm[layer], f_k_norm[layer])
        h_res = h_res + jnp.concatenate([y_m, y_f], axis=-1) @ w_out[layer]
        if layer == DEPTH_2 - 1:
            h_res = h_res[:, N_META:]
        h_res = h_res + _peer(_rmsnorm(h_res, norm_ffn[layer]), peer_query[layer],
                              peer_sub_keys[layer], peer_u[layer], peer_v[layer])
    return h_res


def setup_inputs(seed=0):
    out = dict(first_inputs(seed))
    for name, value in second_inputs(seed + 1).items():
        if name != "x":
            out[name + "_2"] = value
    return out


def reference(
    x, a_norm, a_w_in, a_conv, a_A_log, a_dt_bias, a_o_gain, a_w_out, kv_norm, w_kv, k_gain,
    rel_bias, b_norm, b_w_in, b_q_gain, b_sinks, b_w_out, meta_tokens_2, norm_mix_2, w_in_2,
    conv_qk_2, b_igate_2, b_fgate_m_2, m_out_norm_2, b_fgate_f_2, f_q_norm_2, f_k_norm_2,
    w_out_2, norm_ffn_2, peer_query_2, peer_sub_keys_2, peer_u_2, peer_v_2,
):
    x = first_block(
        x, a_norm, a_w_in, a_conv, a_A_log, a_dt_bias, a_o_gain, a_w_out, kv_norm, w_kv, k_gain,
        rel_bias, b_norm, b_w_in, b_q_gain, b_sinks, b_w_out,
    )
    return second_block(
        x, meta_tokens_2, norm_mix_2, w_in_2, conv_qk_2, b_igate_2, b_fgate_m_2, m_out_norm_2,
        b_fgate_f_2, f_q_norm_2, f_k_norm_2, w_out_2, norm_ffn_2, peer_query_2, peer_sub_keys_2,
        peer_u_2, peer_v_2,
    )


_drawn_inputs = setup_inputs


def setup_inputs(seed=0):
    import zlib

    import numpy as np

    out = dict(_drawn_inputs(seed))
    spreads = {}
    factors = {'a_norm': 2.738,
     'a_o_gain': 4.501,
     'kv_norm': 8.0,
     'k_gain': 8.0,
     'b_norm': 8.0,
     'b_q_gain': 8.0,
     'b_sinks': 64.0,
     'norm_mix_2': 20.936,
     'b_igate_2': 64.0,
     'm_out_norm_2': 64.0,
     'f_q_norm_2': 51.681,
     'f_k_norm_2': 55.971,
     'norm_ffn_2': 64.0,
     'conv_qk_2': 5.828,
     'peer_u_2': 2.865}
    for name, (base, spread) in spreads.items():
        noise = np.random.default_rng([zlib.crc32(name.encode()), seed]).standard_normal(out[name].shape)
        drawn = base * np.exp(spread * noise) if base else spread * noise
        out[name] = __import__('jax').numpy.asarray(drawn.astype(out[name].dtype))
    for name, factor in factors.items():
        out[name] = (out[name] * factor).astype(out[name].dtype)
    return out
```

```python
from contextlib import ExitStack

import numpy as np

import concourse.bass as bass
from concourse import mybir

F32 = mybir.dt.float32
U32 = mybir.dt.uint32
ACT = mybir.ActivationFunctionType
ALU = mybir.AluOpType
AX = mybir.AxisListType

P = 128
D = 1024
KD = D // P
T = 512
TT = T // P
EPS = 1e-6
NEG = -1e30

HA, DK, DV = 8, 128, 256
QKV_TILES = (2 * HA * DK + HA * DV) // P
HB, KVB, HD = 32, 4, 64
META = 16
T2 = T + META
HM, DM = 4, 128
HF, DF = 8, 64
PH, NK, TOPK = 8, 128, 16
SLOTS = PH * TOPK

C_IDENT, C_ONES, C_HALVES, C_LE, C_LEVEL = 0, 128, 256, 384, 512
LEVELS = 7
C_NEGDIAG = C_LEVEL + LEVELS * P
C_PAIR = C_NEGDIAG + P
C_IOTA = C_PAIR + 2
C_MHALF = C_IOTA + 16
C_FLIP = C_MHALF + 1
C_WIDTH = C_FLIP + P
R_SEL, R_BUCKET, R_WINDOW = 0, 8 * P, 8 * P + 384
R_WIDTH = R_WINDOW + 384
(V_ANORM, V_KVNORM, V_BNORM, V_NORM2, V_NORMF) = (0, 8, 16, 24, 32)
V_QGK = 40
V_FQK = 42
V_ALOG, V_DT, V_BI = 44, 45, 46
V_WIDTH = 47


def shape_constants():
    c = np.zeros((P, C_WIDTH), np.float32)
    s, t = np.arange(P)[:, None], np.arange(P)[None, :]
    c[:, C_IDENT:C_IDENT + P] = s == t
    c[:, C_ONES:C_ONES + P] = 1
    c[:, C_HALVES:C_HALVES + P] = s // 64 == t // 64
    c[:, C_LE:C_LE + P] = s <= t
    for n in range(LEVELS):
        b = 1 << n
        c[:, C_LEVEL + n * P:C_LEVEL + (n + 1) * P] = (s // (2 * b) == t // (2 * b)) & (s % (2 * b) < b) & (t % (2 * b) >= b)
    c[:, C_NEGDIAG:C_NEGDIAG + P] = np.where(t <= s, 0, NEG)
    c[:, C_PAIR:C_PAIR + 2] = s // 64 == np.arange(2)[None, :]
    c[:, C_IOTA:C_IOTA + 16] = np.arange(16)[None, :]
    c[:, C_MHALF] = -0.5
    c[:, C_FLIP:C_FLIP + P] = s + t == P - 1
    r = np.zeros((32, R_WIDTH), np.float32)
    for h in range(8):
        r[h, R_SEL + h * P:R_SEL + (h + 1) * P] = 1
    dist = 255 - np.arange(384)
    n = np.maximum(dist, 0)
    large = 16 + (np.log(np.maximum(n, 1) / 16) / np.log(128 / 16) * 16).astype(np.int64)
    bucket = np.where(n < 16, n, np.minimum(large, 31))
    r[:, R_BUCKET:R_BUCKET + 384] = np.arange(32)[:, None] == bucket[None, :]
    r[:, R_WINDOW:R_WINDOW + 384] = np.where((dist >= 0) & (dist < 128), 0, NEG)
    return c, r


class Chain:

    def __init__(self, eng, sem, base=0):
        self.eng, self.sem, self.base, self.n = eng, sem, base, 0

    def __call__(self, ins):
        ins.then_inc(self.sem, 1)
        self.n += 1
        self.eng.wait_ge(self.sem, self.base + self.n)


class Core:

    def __init__(self, nc, stack):
        self.nc, self.stack = nc, stack

    def keep(self, name, shape, dt=F32):
        return self.stack.enter_context(self.nc.sbuf_tensor(name, shape, dt))


def sb(nc, ctx, name, shape, dt=F32):
    return ctx.enter_context(nc.sbuf_tensor(name, shape, dt))


def banks(nc, ctx, name, n):
    return [ctx.enter_context(nc.psum_tensor(f"{name}{i}", [P, 512], F32)) for i in range(n)]


def stage_load(nc, core, a):
    loaded = nc.alloc_semaphore("loaded")
    with nc.Block() as block:
        @block.sync
        def _(sp):
            sp.dma_start(core.c[:, :], a["c128"]).then_inc(loaded, 16)
            sp.dma_start(core.r[:, :], a["c32"]).then_inc(loaded, 16)
            sp.dma_start(core.v[:, :], a["v128"]).then_inc(loaded, 16)
            sp.dma_start(core.x[:, :, :], a["x"].rearrange("(i p) d -> p i d", p=P)).then_inc(loaded, 16)
            sp.dma_start(core.ta[:, :, :], a["a_conv"]).then_inc(loaded, 16)
            sp.dma_start(core.tm[:, :, :], a["conv_qk_2"]).then_inc(loaded, 16)
            sp.dma_start(core.xm[:, :], a["meta"]).then_inc(loaded, 16)
            sp.wait_ge(loaded, 112)

        @block.vector
        def _(dve):
            nc.vector.memset(core.eps[:, 0:1], EPS)
            nc.vector.memset(core.eps[:, 1:2], 64 * EPS)


def stage_norm(nc, core, tag, tiles, gain, h_t, natural=None):
    sem = lambda n: nc.alloc_semaphore(f"{tag}_{n}")
    squared, meaned, rooted, scaled, turned, stored = map(sem, ("squared", "meaned", "rooted", "scaled", "turned", "stored"))
    ident = core.c[:, C_IDENT:C_IDENT + P]
    n = len(tiles)
    with ExitStack() as ctx:
        junk = sb(nc, ctx, f"{tag}_junk", [P, D])
        ss = sb(nc, ctx, f"{tag}_ss", [P, 3, n])
        xn = sb(nc, ctx, f"{tag}_xn", [P, 2, D]) if natural is None else None
        ps = banks(nc, ctx, f"{tag}_ps", 4)
        block = ctx.enter_context(nc.Block())
        where = [natural(i) if natural else xn[0:tiles[i][1], i % 2, :] for i in range(n)]

        @block.scalar
        def _(act):
            for i, (x, rows, _c) in enumerate(tiles):
                if i:
                    act.wait_ge(squared, i)
                nc.scalar.activation(junk[0:rows, :], x, ACT.Square, accum_out=ss[0:rows, 0, i:i + 1]).then_inc(squared, 1)
            for i, (x, rows, _c) in enumerate(tiles):
                act.wait_ge(rooted, i + 1)
                if natural is None and i >= 2:
                    act.wait_ge(turned, 2 * (i - 1))
                nc.scalar.activation(where[i], x, ACT.Copy, scale=ss[0:rows, 2, i:i + 1]).then_inc(scaled, 1)

        @block.gpsimd
        def _(pool):
            for i, (x, rows, _c) in enumerate(tiles):
                pool.wait_ge(meaned, i + 1)
                nc.gpsimd.tensor_tensor(ss[0:rows, 2, i:i + 1], ss[0:rows, 1, i:i + 1],
                                        core.c[0:rows, C_MHALF:C_MHALF + 1], ALU.pow).then_inc(rooted, 1)

        @block.tensor
        def _(pe):
            for i, (x, rows, _c) in enumerate(tiles):
                pe.wait_ge(scaled, i + 1)
                for half in range(2):
                    b = 2 * i + half
                    if b >= 4:
                        pe.wait_ge(stored, b - 3)
                    for k in range(4):
                        d = (4 * half + k) * P
                        last = nc.tensor.transpose(ps[b % 4][:, k * rows:(k + 1) * rows], where[i][:, d:d + P], ident[0:rows, 0:rows])
                    last.then_inc(turned, 1)

        @block.vector
        def _(dve):
            for i, (x, rows, _c) in enumerate(tiles):
                dve.wait_ge(squared, i + 1)
                nc.vector.tensor_scalar(ss[0:rows, 1, i:i + 1], ss[0:rows, 0, i:i + 1], 1.0 / D, EPS, ALU.mult, ALU.add).then_inc(meaned, 1)
            for i, (x, rows, col) in enumerate(tiles):
                for half in range(2):
                    b = 2 * i + half
                    dve.wait_ge(turned, b + 1)
                    k0 = 4 * half
                    nc.vector.tensor_tensor(h_t[:, k0:k0 + 4, col:col + rows],
                                            ps[b % 4][:, 0:4 * rows].rearrange("p (k t) -> p k t", k=4),
                                            core.v[:, gain + k0:gain + k0 + 4].unsqueeze(2).to_broadcast([P, 4, rows]),
                                            ALU.mult).then_inc(stored, 1)


def x_tiles(core):
    return [(core.x[:, i, :], P, i * P) for i in range(TT)]


def w_view(w, kt):
    return w.rearrange("(k p) n -> p k n", p=P)


def stage_proj_t(nc, core, tag, h_t, cols, w, n0, chunks, out, spans):
    loads = [nc.alloc_semaphore(f"{tag}_w{i}") for i in range(2)]
    done, free = (nc.alloc_semaphore(f"{tag}_{n}") for n in ("product", "bank_free"))
    ns = len(spans)
    with ExitStack() as ctx:
        wb = [sb(nc, ctx, f"{tag}_wb{i}", [P, KD, 512]) for i in range(2)]
        ps = banks(nc, ctx, f"{tag}_ps", 4)
        block = ctx.enter_context(nc.Block())
        wv = w_view(w, KD)

        @block.sync
        def _(sp):
            for b in range(2):
                sp.dma_start(wb[b][:, :, :], wv[:, :, n0 + 512 * b:n0 + 512 * b + 512]).then_inc(loads[b], 16)
            if chunks > 2:
                with sp.Fori(1, chunks // 2) as i:
                    for b in range(2):
                        sp.wait_ge(done, i * 8 * ns + (b - 1) * 4 * ns)
                        sp.dma_start(wb[b][:, :, :], wv[:, :, bass.ds(n0 + 512 * b + i * 1024, 512)]).then_inc(loads[b], 16)

        @block.tensor
        def _(pe):
            with pe.Fori(0, chunks // 2) as i:
                for b in range(2):
                    pe.wait_ge(loads[b], 16 * i + 16)
                    for j in range(4):
                        for si, (c0, cw) in enumerate(spans):
                            u = (b * 4 + j) * ns + si
                            pe.wait_ge(free, i * 8 * ns + u + 1)
                            for k in range(KD):
                                last = nc.tensor.matmul(ps[u % 4][:, 0:cw], wb[b][:, k, j * P:(j + 1) * P],
                                                        h_t[:, k, c0:c0 + cw], start=(k == 0), stop=(k == KD - 1))
                            last.then_inc(done, 1)

        @block.scalar
        def _(act):
            act.sem_inc(free, 4)
            with act.Fori(0, chunks // 2) as i:
                for j in range(8):
                    for si, (c0, cw) in enumerate(spans):
                        u = j * ns + si
                        act.wait_ge(done, i * 8 * ns + u + 1)
                        nc.scalar.activation(out[:, bass.ds(i * 8 + j, 1), c0:c0 + cw],
                                             ps[u % 4][:, 0:cw].unsqueeze(1), ACT.Copy).then_inc(free, 1)


def stage_proj_conv(nc, core, tag, h_t, w, n0, chunks, taps, out, spans, width):
    loads = [nc.alloc_semaphore(f"{tag}_w{i}") for i in range(2)]
    done, free, padded, conved, step, zeroed, activated = (
        nc.alloc_semaphore(f"{tag}_{n}") for n in ("product", "bank_free", "padded", "conved", "conv_step", "zeroed", "activated"))
    ns = len(spans)
    with ExitStack() as ctx:
        wb = [sb(nc, ctx, f"{tag}_wb{i}", [P, KD, 512]) for i in range(2)]
        xp = sb(nc, ctx, f"{tag}_xp", [P, 3 + width])
        y = sb(nc, ctx, f"{tag}_y", [P, width])
        ps = banks(nc, ctx, f"{tag}_ps", 4)
        block = ctx.enter_context(nc.Block())
        wv = w_view(w, KD)

        @block.sync
        def _(sp):
            for b in range(2):
                sp.dma_start(wb[b][:, :, :], wv[:, :, n0 + 512 * b:n0 + 512 * b + 512]).then_inc(loads[b], 16)
            if chunks > 2:
                with sp.Fori(1, chunks // 2) as i:
                    for b in range(2):
                        sp.wait_ge(done, i * 8 * ns + (b - 1) * 4 * ns)
                        sp.dma_start(wb[b][:, :, :], wv[:, :, bass.ds(n0 + 512 * b + i * 1024, 512)]).then_inc(loads[b], 16)

        @block.tensor
        def _(pe):
            with pe.Fori(0, chunks // 2) as i:
                for b in range(2):
                    pe.wait_ge(loads[b], 16 * i + 16)
                    for j in range(4):
                        for si, (c0, cw) in enumerate(spans):
                            u = (b * 4 + j) * ns + si
                            pe.wait_ge(free, i * 8 * ns + u + 1)
                            for k in range(KD):
                                last = nc.tensor.matmul(ps[u % 4][:, 0:cw], wb[b][:, k, j * P:(j + 1) * P],
                                                        h_t[:, k, c0:c0 + cw], start=(k == 0), stop=(k == KD - 1))
                            last.then_inc(done, 1)

        @block.scalar
        def _(act):
            act.sem_inc(free, 4)
            act.wait_ge(zeroed, 1)
            with act.Fori(0, chunks // 2) as i:
                for j in range(8):
                    for si, (c0, cw) in enumerate(spans):
                        u = j * ns + si
                        act.wait_ge(done, i * 8 * ns + u + 1)
                        nc.scalar.activation(xp[:, 3 + c0:3 + c0 + cw], ps[u % 4][:, 0:cw], ACT.Copy).then_inc(free, 1)
                    act.wait_ge(conved, i * 8 + j + 1)
                    nc.scalar.activation(out[:, bass.ds(i * 8 + j, 1), :], y[:, :].unsqueeze(1), ACT.Silu).then_inc(activated, 1)

        @block.vector
        def _(dve):
            nc.vector.memset(xp[:, 0:3], 0.0).then_inc(zeroed, 1)
            with dve.Fori(0, chunks // 2) as i:
                for j in range(8):
                    tap = lambda k: taps[:, bass.ds(i * 8 + j, 1), k]
                    dve.wait_ge(free, 4 + i * 8 * ns + (j + 1) * ns)
                    if j:
                        dve.wait_ge(activated, i * 8 + j)
                    nc.vector.tensor_scalar(y[:, :], xp[:, 3:3 + width], tap(3), None, ALU.mult).then_inc(step, 1)
                    for k in range(3):
                        dve.wait_ge(step, i * 24 + j * 3 + k + 1)
                        last = nc.vector.scalar_tensor_tensor(y[:, :], xp[:, k:k + width], tap(k), y[:, :], ALU.mult, ALU.add)
                        if k < 2:
                            last.then_inc(step, 1)
                    last.then_inc(conved, 1)


def stage_unit_rows(nc, core, tag, qk):
    squared, summed, rooted, inverted, scaled = (
        nc.alloc_semaphore(f"{tag}_{n}") for n in ("squared", "summed", "rooted", "inverted", "scaled"))
    with ExitStack() as ctx:
        sq = sb(nc, ctx, f"{tag}_sq", [P, 2, T])
        rt = sb(nc, ctx, f"{tag}_rt", [P, 2, T])
        iv = sb(nc, ctx, f"{tag}_iv", [P, 2, T])
        ps = banks(nc, ctx, f"{tag}_ps", 2)
        block = ctx.enter_context(nc.Block())
        tile = lambda i, b: qk[:, bass.ds(i + b * HA, 1), :]

        @block.scalar
        def _(act):
            with act.Fori(0, HA) as i:
                for b in range(2):
                    nc.scalar.activation(sq[:, b:b + 1, :], tile(i, b), ACT.Square).then_inc(squared, 1)
                for b in range(2):
                    act.wait_ge(summed, 2 * i + b + 1)
                    act.wait_ge(inverted, 2 * i + b + 1)
                    nc.scalar.activation(rt[:, b, :], ps[b][:, :], ACT.Sqrt, bias=core.eps[:, 0:1]).then_inc(rooted, 1)

        @block.tensor
        def _(pe):
            with pe.Fori(0, HA) as i:
                for b in range(2):
                    pe.wait_ge(squared, 2 * i + b + 1)
                    nc.tensor.matmul(ps[b][:, :], core.c[:, C_ONES:C_ONES + P], sq[:, b, :], start=True, stop=True).then_inc(summed, 1)

        @block.vector
        def _(dve):
            dve.sem_inc(inverted, 2)
            with dve.Fori(0, HA) as i:
                for b in range(2):
                    dve.wait_ge(rooted, 2 * i + b + 1)
                    nc.vector.reciprocal(iv[:, b, :], rt[:, b, :]).then_inc(inverted, 1)
                    dve.wait_ge(inverted, 2 * i + b + 3)
                    nc.vector.scalar_tensor_tensor(tile(i, b), tile(i, b), DK ** -0.5 if b == 0 else 1.0, iv[:, b:b + 1, :],
                                                   ALU.mult, ALU.mult).then_inc(scaled, 1)


def stage_delta_gates(nc, core, h_t, w, rows, cols):
    sem = lambda n: nc.alloc_semaphore(f"dg_{n}")
    loaded, zeroed, product, vdone, adone, turned = map(sem, ("loaded", "zeroed", "product", "vector_step", "scalar_step", "turned"))
    with ExitStack() as ctx:
        wg = sb(nc, ctx, "dg_w", [P, KD, 40])
        t = sb(nc, ctx, "dg_t", [P, 4, T])
        more = sb(nc, ctx, "dg_more", [8, 2, T])
        ea = sb(nc, ctx, "dg_ea", [P, 1])
        ps = banks(nc, ctx, "dg_ps", 2)
        block = ctx.enter_context(nc.Block())
        wv = w_view(w, KD)
        ab = QKV_TILES * P + HA * DV
        A = slice(32, 40)

        @block.sync
        def _(sp):
            sp.wait_ge(zeroed, 1)
            sp.dma_start(wg[:, :, 0:8], wv[:, :, ab:ab + 8]).then_inc(loaded, 16)
            sp.dma_start(wg[:, :, 32:40], wv[:, :, ab + 8:ab + 16]).then_inc(loaded, 16)

        @block.tensor
        def _(pe):
            pe.wait_ge(loaded, 32)
            for k in range(KD):
                last = nc.tensor.matmul(ps[0][0:40, :], wg[:, k, :], h_t[:, k, :], start=(k == 0), stop=(k == KD - 1))
            last.then_inc(product, 1)
            pe.wait_ge(vdone, 11)
            pe.wait_ge(adone, 6)
            for kind in range(4):
                src = rows[0:8, kind, :] if kind < 2 else more[:, kind - 2, :]
                for i in range(TT):
                    last = nc.tensor.transpose(ps[1][:, (kind * TT + i) * 8:(kind * TT + i) * 8 + 8],
                                               src[:, i * P:(i + 1) * P], core.c[0:8, C_IDENT:C_IDENT + 8])
            last.then_inc(turned, 1)

        @block.scalar
        def _(act):
            nc.scalar.activation(ea[A, :], core.v[A, V_ALOG:V_ALOG + 1], ACT.Exp).then_inc(adone, 1)
            act.wait_ge(vdone, 2)
            nc.scalar.activation(t[A, 1, :], t[A, 1, :], ACT.Exp, scale=-1.0).then_inc(adone, 1)
            act.wait_ge(adone, 2)
            nc.scalar.activation(t[A, 1, :], t[A, 1, :], ACT.Ln, bias=1.0).then_inc(adone, 1)
            act.wait_ge(vdone, 9)
            nc.scalar.activation(more[:, 0, :], rows[0:8, 0, :], ACT.Exp).then_inc(adone, 1)
            act.wait_ge(vdone, 10)
            nc.scalar.activation(more[:, 1, :], more[:, 1, :], ACT.Exp).then_inc(adone, 1)
            act.wait_ge(product, 1)
            nc.scalar.activation(rows[0:8, 1, :], ps[0][0:8, :], ACT.Sigmoid).then_inc(adone, 1)

        @block.vector
        def _(dve):
            nc.vector.memset(wg[:, :, :], 0.0).then_inc(zeroed, 1)
            then = Chain(dve, vdone)
            dve.wait_ge(product, 1)
            then(nc.vector.tensor_scalar(t[A, 0, :], ps[0][A, :], core.v[A, V_DT:V_DT + 1], None, ALU.add))
            then(nc.vector.scalar_tensor_tensor(t[A, 1, :], t[A, 0, :], -1.0, t[A, 0, :], ALU.mult, ALU.max))
            dve.wait_ge(adone, 3)
            then(nc.vector.scalar_tensor_tensor(t[A, 2, :], t[A, 0, :], 0.0, t[A, 1, :], ALU.max, ALU.add))
            then(nc.vector.tensor_scalar(t[A, 0, :], t[A, 2, :], ea[A, 0:1], -1.0, ALU.mult, ALU.mult))
            for i in range(TT):
                c = slice(i * P, (i + 1) * P)
                then(nc.vector.tensor_tensor_scan(t[A, 3, c], core.c[A, C_ONES:C_ONES + P], t[A, 0, c], 0.0, ALU.mult, ALU.add))
            then(nc.vector.tensor_copy(rows[0:8, 0, :], t[A, 3, :]))
            g = rows[0:8, 0, :].rearrange("p (i c) -> p i c", i=TT)
            then(nc.vector.tensor_tensor(more[:, 1, :].rearrange("p (i c) -> p i c", i=TT),
                                         g[:, :, P - 1:P].to_broadcast([8, TT, P]), g, ALU.subtract))
            dve.wait_ge(adone, 6)
            then(nc.vector.tensor_tensor(more[:, 0, :], more[:, 0, :], rows[0:8, 1, :], ALU.mult))
            dve.wait_ge(turned, 1)
            nc.vector.tensor_copy(cols[:, :, :, :], ps[1][:, 0:4 * TT * 8].rearrange("p (a i h) -> p a i h", a=4, i=TT))


def stage_delta_chunks(nc, core, qkv, rows, cols, ss):
    sem = lambda n: nc.alloc_semaphore(f"dc_{n}")
    (rowcast, exp_g, decayed, gramed, masked, weighted, qk_ready, qdec_ready, level_ready, x_ready, x_copied, mx_ready, m_ready,
     turned, turn_copied, kdec_ready, t_scaled, w_ready, w_copied, vnew_ready, vnew_copied, out_ready, out_read, s_ready,
     step, adj_ready) = map(sem, (
        "rowcast", "exp_g", "decayed", "gramed", "masked", "weighted", "qk_ready", "qdec_ready", "level_ready", "x_ready", "x_copied",
        "mx_ready", "m_ready", "turned", "turn_copied", "kdec_ready", "t_scaled", "w_ready", "w_copied", "vnew_ready", "vnew_copied",
        "out_ready", "out_read", "s_ready", "step", "adjusted"))
    ident = core.c[:, C_IDENT:C_IDENT + P]
    q_t = lambda h: qkv[:, h, :]
    k_t = lambda h: qkv[:, HA + h, :]
    v_t = lambda h, j: qkv[:, 2 * HA + 2 * h + j, :]
    o_h = lambda h: qkv[:, 2 * HA + 2 * h:2 * HA + 2 * h + 2, :].rearrange("p j (a d) -> p (j a) d", a=2)
    w4 = lambda ap: ap.rearrange("p (i c) -> p i c", i=TT)
    PAIRS = [(2 * p, 2 * p + 1) for p in range(HA // 2)]
    with ExitStack() as ctx:
        two = lambda name, n=T: [sb(nc, ctx, f"dc_{name}{j}", [P, n]) for j in range(2)]
        dec, at, em, m, mt, xs = two("dec"), two("at"), two("em"), two("m"), two("mt"), two("xs")
        lv = two("lv", 2 * T)
        tb, tbg, kn, kd, wt, qd, qk, eg = (two(n) for n in ("tb", "tbg", "kn", "kd", "wt", "qd", "qk", "eg"))
        vn, vnew, st, junk = two("vn", TT * DV), two("vnew", DV), two("st", DV), two("junk", DV)
        ba, bb, bc, bd = (banks(nc, ctx, f"dc_p{n}", 2) for n in "abcd")
        block = ctx.enter_context(nc.Block())

        @block.tensor
        def _(pe):
            def turn(h, n):
                j = h % 2
                if n == 0:
                    pe.wait_ge(qk_ready, h + 1)
                else:
                    pe.wait_ge(turn_copied, h // 2 * 6 + 2 * (n - 1) + j + 1)
                src = k_t(h) if n == 0 else v_t(h, n - 1)
                for i in range(TT):
                    last = nc.tensor.transpose(bd[j][:, i * P:(i + 1) * P], src[:, i * P:(i + 1) * P], ident)
                last.then_inc(turned, 1)

            for pair in PAIRS:
                for h in pair:
                    j = h % 2
                    if h >= 2:
                        pe.wait_ge(s_ready, 6 * (h // 2))
                        pe.wait_ge(vnew_copied, 8 * (h // 2))
                        pe.wait_ge(out_read, 8 * (h // 2))
                        pe.wait_ge(turn_copied, 6 * (h // 2))
                    sel = core.r[0:8, R_SEL + h * P:R_SEL + (h + 1) * P]
                    nc.tensor.matmul(ba[j][:, :], sel, rows[0:8, 0, :], start=True, stop=True)
                    nc.tensor.matmul(bb[j][:, :], sel, rows[0:8, 1, :], start=True, stop=True).then_inc(rowcast, 1)
                    for bank, rhs in ((bc, k_t(h)), (bd, q_t(h))):
                        for i in range(TT):
                            c = slice(i * P, (i + 1) * P)
                            last = nc.tensor.matmul(bank[j][:, c], k_t(h)[:, c], rhs[:, c], start=True, stop=True)
                    last.then_inc(gramed, 1)
                for n in range(LEVELS):
                    for h in pair:
                        j = h % 2
                        pe.wait_ge(level_ready, h // 2 * 2 * LEVELS + 2 * n + j + 1)
                        pe.wait_ge(m_ready, h // 2 * 2 * (LEVELS + 1) + 2 * n + j + 1)
                        if n == 0:
                            pe.wait_ge(exp_g, 2 * h + 2)
                            pe.wait_ge(decayed, h + 1)
                        for i in range(TT):
                            c = slice(i * P, (i + 1) * P)
                            last = nc.tensor.matmul(ba[j][:, c], lv[j][:, n % 2 * T + i * P:n % 2 * T + (i + 1) * P], m[j][:, c],
                                                    start=True, stop=True)
                        last.then_inc(x_ready, 1)
                    for h in pair:
                        j = h % 2
                        if n in (1, 3, 5):
                            turn(h, n // 2)
                        pe.wait_ge(x_copied, h // 2 * 2 * LEVELS + 2 * n + j + 1)
                        for i in range(TT):
                            c = slice(i * P, (i + 1) * P)
                            if n < LEVELS - 1:
                                nc.tensor.matmul(bb[j][:, c], mt[j][:, c], xs[j][:, c], start=True, stop=True)
                            last = nc.tensor.matmul(bc[j][:, c], xs[j][:, c], mt[j][:, c], start=True, stop=True)
                        last.then_inc(mx_ready, 1)
                for h in pair:
                    j = h % 2
                    pe.wait_ge(t_scaled, h + 1)
                    pe.wait_ge(turn_copied, h // 2 * 6 + 4 + j + 1)
                    for i in range(TT):
                        c = slice(i * P, (i + 1) * P)
                        last = nc.tensor.matmul(ba[j][:, c], kn[j][:, c], tbg[j][:, c], start=True, stop=True)
                    last.then_inc(w_ready, 1)
                for i in range(TT):
                    c = slice(i * P, (i + 1) * P)
                    for h in pair:
                        j = h % 2
                        if i:
                            pe.wait_ge(s_ready, h // 2 * 6 + (i - 1) * 2 + j + 1)
                        last = nc.tensor.matmul(bb[j][:, 0:DV], tb[j][:, c], vn[j][:, i * DV:(i + 1) * DV], start=True, stop=i == 0)
                        if i:
                            last = nc.tensor.matmul(bb[j][:, 0:DV], wt[j][:, c], st[j][:, :], start=False, stop=True)
                        last.then_inc(vnew_ready, 1)
                    for h in pair:
                        j = h % 2
                        pe.wait_ge(vnew_copied, h // 2 * 8 + 2 * i + j + 1)
                        if i:
                            pe.wait_ge(out_read, h // 2 * 8 + 2 * (i - 1) + j + 1)
                            nc.tensor.matmul(bc[j][:, 0:DV], qd[j][:, c], st[j][:, :], start=True, stop=False)
                        else:
                            pe.wait_ge(w_copied, h + 1)
                            pe.wait_ge(qdec_ready, h + 1)
                            pe.wait_ge(kdec_ready, h + 1)
                        last = nc.tensor.matmul(bc[j][:, 0:DV], qk[j][:, c], vnew[j][:, :], start=i == 0, stop=True)
                        if i < TT - 1:
                            last = nc.tensor.matmul(ba[j][:, 0:DV], kd[j][:, c], vnew[j][:, :], start=True, stop=True)
                        last.then_inc(out_ready, 1)

        @block.scalar
        def _(act):
            for pair in PAIRS:
                for h in pair:
                    j = h % 2
                    act.wait_ge(decayed, h + 1)
                    if h >= 2:
                        act.wait_ge(s_ready, 6 * (h // 2))
                    nc.scalar.activation(eg[j][:, :], ba[j][:, :], ACT.Exp).then_inc(exp_g, 1)
                    nc.scalar.activation(dec[j][:, :], dec[j][:, :], ACT.Exp).then_inc(exp_g, 1)
                for n in range(LEVELS):
                    for h in pair:
                        j = h % 2
                        act.wait_ge(x_ready, h // 2 * 2 * LEVELS + 2 * n + j + 1)
                        nc.scalar.activation(xs[j][:, :], ba[j][:, :], ACT.Copy).then_inc(x_copied, 1)
                    for h in pair:
                        j = h % 2
                        if n in (1, 3, 5):
                            act.wait_ge(turned, h // 2 * 6 + (n // 2) * 2 + j + 1)
                            dst = kn[j][:, :] if n == 1 else w4v(vn[j], DV)[:, :, (n // 2 - 1) * P:(n // 2) * P]
                            nc.scalar.activation(dst, bd[j][:, :] if n == 1 else w4(bd[j][:, :]), ACT.Copy).then_inc(turn_copied, 1)
                for h in pair:
                    j = h % 2
                    act.wait_ge(w_ready, h + 1)
                    nc.scalar.activation(wt[j][:, :], ba[j][:, :], ACT.Copy, scale=-1.0).then_inc(w_copied, 1)
                for i in range(TT):
                    for h in pair:
                        j = h % 2
                        act.wait_ge(vnew_ready, h // 2 * 8 + 2 * i + j + 1)
                        nc.scalar.activation(vnew[j][:, :], bb[j][:, 0:DV], ACT.Copy).then_inc(vnew_copied, 1)
                    for h in pair:
                        j = h % 2
                        act.wait_ge(out_ready, h // 2 * 8 + 2 * i + j + 1)
                        nc.scalar.activation(o_h(h)[:, i, :], bc[j][:, 0:DV], ACT.Copy)
                        nc.scalar.activation(junk[j][:, :], bc[j][:, 0:DV], ACT.Square, accum_out=ss[:, i, h:h + 1]).then_inc(out_read, 1)

        @block.gpsimd
        def _(pool):
            for pair in PAIRS:
                for h in pair:
                    j = h % 2
                    pool.wait_ge(exp_g, 2 * h + 2)
                    nc.gpsimd.tensor_tensor(w4(em[j][:, :]), w4(dec[j][:, :]),
                                            core.c[:, C_LE:C_LE + P].unsqueeze(1).to_broadcast([P, TT, P]), ALU.mult).then_inc(masked, 1)
                for n in range(LEVELS):
                    for h in pair:
                        j = h % 2
                        if n == 0:
                            pool.wait_ge(weighted, h + 1)
                        if n >= 2:
                            pool.wait_ge(x_ready, h // 2 * 2 * LEVELS + 2 * (n - 2) + j + 1)
                        elif h >= 2:
                            pool.wait_ge(x_ready, h // 2 * 2 * LEVELS)
                        lo = C_LEVEL + n * P
                        nc.gpsimd.tensor_tensor(w4(lv[j][:, n % 2 * T:n % 2 * T + T]), w4(at[j][:, :]),
                                                core.c[:, lo:lo + P].unsqueeze(1).to_broadcast([P, TT, P]), ALU.mult).then_inc(level_ready, 1)
                for h in pair:
                    j = h % 2
                    pool.wait_ge(turn_copied, h // 2 * 6 + j + 1)
                    if h >= 2:
                        pool.wait_ge(out_ready, 8 * (h // 2))
                    nc.gpsimd.tensor_tensor(w4(kd[j][:, :]), w4(kn[j][:, :]), cols[:, 3, :, h:h + 1].to_broadcast([P, TT, P]),
                                            ALU.mult).then_inc(kdec_ready, 1)

        @block.vector
        def _(dve):
            eye = ident.unsqueeze(1).to_broadcast([P, TT, P])
            for pair in PAIRS:
                for h in pair:
                    j = h % 2
                    dve.wait_ge(rowcast, h + 1)
                    if h >= 2:
                        dve.wait_ge(masked, h - 1)
                    for i in range(TT):
                        c = slice(i * P, (i + 1) * P)
                        last = nc.vector.tensor_scalar(dec[j][:, c], ba[j][:, c], cols[:, 0, i, h:h + 1], 0.0, ALU.subtract, ALU.min)
                    last.then_inc(decayed, 1)
                    nc.vector.tensor_copy(w4(m[j][:, :]), eye)
                    nc.vector.tensor_copy(w4(mt[j][:, :]), eye).then_inc(m_ready, 1)
                for h in pair:
                    j = h % 2
                    dve.wait_ge(gramed, h + 1)
                    dve.wait_ge(exp_g, 2 * h + 2)
                    nc.vector.tensor_tensor(at[j][:, :], bc[j][:, :], dec[j][:, :], ALU.mult).then_inc(step, 1)
                    dve.wait_ge(step, h + 1)
                    nc.vector.tensor_tensor(at[j][:, :], bb[j][:, :], at[j][:, :], ALU.mult).then_inc(weighted, 1)
                    dve.wait_ge(masked, h + 1)
                    nc.vector.tensor_tensor(qk[j][:, :], bd[j][:, :], em[j][:, :], ALU.mult).then_inc(qk_ready, 1)
                    nc.vector.tensor_tensor(qd[j][:, :], q_t(h), eg[j][:, :], ALU.mult).then_inc(qdec_ready, 1)
                for n in range(LEVELS):
                    for h in pair:
                        j = h % 2
                        dve.wait_ge(mx_ready, h // 2 * 2 * LEVELS + 2 * n + j + 1)
                        if n < LEVELS - 1:
                            nc.vector.tensor_tensor(m[j][:, :], m[j][:, :], bb[j][:, :], ALU.subtract)
                        nc.vector.tensor_tensor(mt[j][:, :], mt[j][:, :], bc[j][:, :], ALU.subtract).then_inc(m_ready, 1)
                for h in pair:
                    j = h % 2
                    dve.wait_ge(m_ready, h // 2 * 2 * (LEVELS + 1) + 2 * LEVELS + j + 1)
                    nc.vector.tensor_tensor(w4(tb[j][:, :]), w4(mt[j][:, :]), cols[:, 1, :, h:h + 1].to_broadcast([P, TT, P]), ALU.mult)
                    nc.vector.tensor_tensor(w4(tbg[j][:, :]), w4(mt[j][:, :]), cols[:, 2, :, h:h + 1].to_broadcast([P, TT, P]),
                                            ALU.mult).then_inc(t_scaled, 1)
                for i in range(TT - 1):
                    for h in pair:
                        j = h % 2
                        dve.wait_ge(out_ready, h // 2 * 8 + 2 * i + j + 1)
                        if i:
                            dve.wait_ge(s_ready, h // 2 * 6 + (i - 1) * 2 + j + 1)
                            last = nc.vector.scalar_tensor_tensor(st[j][:, :], st[j][:, :], eg[j][:, i * P + P - 1:i * P + P],
                                                                  ba[j][:, 0:DV], ALU.mult, ALU.add)
                        else:
                            last = nc.vector.tensor_copy(st[j][:, :], ba[j][:, 0:DV])
                        last.then_inc(s_ready, 1)


def w4v(buf, n):
    return buf[:, :].rearrange("p (i d) -> p i d", d=n)


def open_core(nc, stack, a):
    core = Core(nc, stack)
    core.c = core.keep("c128_sb", [P, C_WIDTH])
    core.r = core.keep("c32_sb", [32, R_WIDTH])
    core.v = core.keep("v128_sb", [P, V_WIDTH])
    core.x = core.keep("x_sb", [P, TT, D])
    core.eps = core.keep("eps_sb", [P, 2])
    core.xm = core.keep("meta_sb", [META, D])
    core.one = core.keep("one_sb", [P, T2])
    core.ta = core.keep("taps_a_sb", [P, QKV_TILES, 4])
    core.tm = core.keep("taps_m_sb", [P, 2 * HM, 4])
    return core


def stage_proj_n(nc, core, tag, h_t, kt, tiles, w, chunks, engine, emit):
    loads = [nc.alloc_semaphore(f"{tag}_w{i}") for i in range(2)]
    product, taken = (nc.alloc_semaphore(f"{tag}_{n}") for n in ("product", "taken"))
    width = max(cw for _, cw in chunks)
    nt = len(tiles)
    with ExitStack() as ctx:
        wb = [sb(nc, ctx, f"{tag}_wb{i}", [P, kt, width]) for i in range(min(2, len(chunks)))]
        ps = banks(nc, ctx, f"{tag}_ps", 4)
        block = ctx.enter_context(nc.Block())
        wv = w_view(w, kt)

        @block.sync
        def _(sp):
            for c, (c0, cw) in enumerate(chunks):
                if c >= 2:
                    sp.wait_ge(product, (c - 1) * nt)
                sp.dma_start(wb[c % 2][:, :, 0:cw], wv[:, :, c0:c0 + cw]).then_inc(loads[c % 2], 16)

        @block.tensor
        def _(pe):
            for c, (c0, cw) in enumerate(chunks):
                pe.wait_ge(loads[c % 2], 16 * (c // 2 + 1))
                for i, (rows, col) in enumerate(tiles):
                    u = c * nt + i
                    if u >= 4:
                        pe.wait_ge(taken, u - 3)
                    for k in range(kt):
                        last = nc.tensor.matmul(ps[u % 4][0:rows, 0:cw], h_t[:, k, col:col + rows], wb[c % 2][:, k, 0:cw],
                                                start=(k == 0), stop=(k == kt - 1))
                    last.then_inc(product, 1)

        def take(eng):
            for c, (c0, cw) in enumerate(chunks):
                for i, (rows, col) in enumerate(tiles):
                    u = c * nt + i
                    eng.wait_ge(product, u + 1)
                    emit(c, i, ps[u % 4][0:rows, 0:cw]).then_inc(taken, 1)

        if engine == "scalar":
            @block.scalar
            def _(act):
                take(act)
        else:
            @block.vector
            def _(dve):
                take(dve)


X_COLS = [(P, i * P) for i in range(TT)]


def add_to_x(nc, core, width=512):
    def emit(c, i, product):
        x = core.x[:, i, c * width:(c + 1) * width]
        return nc.vector.tensor_tensor(x, x, product, ALU.add)
    return emit


def stage_delta_out(nc, core, h_t, w, z0, o, ss, gain, o_t):
    sem = lambda n: nc.alloc_semaphore(f"do_{n}")
    loads = [sem("w0"), sem("w1")]
    meaned, rooted, product, gated, normed, mixed, step, turned, taken = map(
        sem, ("meaned", "rooted", "product", "gated", "normed", "mixed", "step", "turned", "taken"))
    with ExitStack() as ctx:
        wb = [sb(nc, ctx, f"do_wb{i}", [P, KD, 512]) for i in range(2)]
        rstd = sb(nc, ctx, "do_rstd", [P, 2, TT * HA])
        sil = sb(nc, ctx, "do_sil", [P, 2, 512])
        on = sb(nc, ctx, "do_on", [P, 2, 512])
        gb = sb(nc, ctx, "do_gain", [P, DV])
        ps, pt = banks(nc, ctx, "do_ps", 2), banks(nc, ctx, "do_pt", 2)
        block = ctx.enter_context(nc.Block())
        wv = w_view(w, KD)
        U = 4 * TT

        @block.sync
        def _(sp):
            sp.dma_start(gb[:, :], gain.partition_broadcast(P)).then_inc(loads[0], 16)
            for c in range(4):
                if c >= 2:
                    sp.wait_ge(product, (c - 1) * TT)
                sp.dma_start(wb[c % 2][:, :, :], wv[:, :, z0 + c * 512:z0 + (c + 1) * 512]).then_inc(loads[c % 2], 16)

        @block.tensor
        def _(pe):
            def turn(u):
                pe.wait_ge(mixed, u + 1)
                if u >= 2:
                    pe.wait_ge(taken, u - 1)
                for k in range(4):
                    last = nc.tensor.transpose(pt[u % 2][:, k * P:(k + 1) * P], on[:, u % 2, k * P:(k + 1) * P],
                                               core.c[:, C_IDENT:C_IDENT + P])
                last.then_inc(turned, 1)
            for u in range(U):
                c, i = divmod(u, TT)
                if i == 0:
                    pe.wait_ge(loads[c % 2], 16 * (c // 2 + 1) + 16 * (c % 2 == 0))
                if u >= 2:
                    pe.wait_ge(gated, u - 1)
                for k in range(KD):
                    last = nc.tensor.matmul(ps[u % 2][:, :], h_t[:, k, i * P:(i + 1) * P], wb[c % 2][:, k, :],
                                            start=(k == 0), stop=(k == KD - 1))
                last.then_inc(product, 1)
                if u:
                    turn(u - 1)
            turn(U - 1)

        @block.gpsimd
        def _(pool):
            pool.wait_ge(meaned, 1)
            nc.gpsimd.tensor_tensor(rstd[:, 1, :], rstd[:, 0, :], core.c[:, C_MHALF:C_MHALF + 1].to_broadcast([P, TT * HA]),
                                    ALU.pow).then_inc(rooted, 1)

        @block.scalar
        def _(act):
            for u in range(U):
                act.wait_ge(product, u + 1)
                if u >= 2:
                    act.wait_ge(mixed, u - 1)
                nc.scalar.activation(sil[:, u % 2, :], ps[u % 2][:, :], ACT.Silu).then_inc(gated, 1)

        @block.vector
        def _(dve):
            nc.vector.tensor_scalar(rstd[:, 0, :], ss.rearrange("p i h -> p (i h)"), 1.0 / DV, EPS, ALU.mult, ALU.add).then_inc(meaned, 1)
            dve.wait_ge(rooted, 1)
            dve.wait_ge(loads[0], 32)

            def store(u):
                c, i = divmod(u, TT)
                dve.wait_ge(turned, u + 1)
                nc.vector.tensor_copy(o_t[:, 4 * c:4 * c + 4, i * P:(i + 1) * P],
                                      pt[u % 2][:, :].rearrange("p (k t) -> p k t", k=4)).then_inc(taken, 1)
            for u in range(U):
                c, i = divmod(u, TT)
                if u >= 2:
                    dve.wait_ge(turned, u - 1)
                for j in range(2):
                    h = 2 * c + j
                    nc.vector.scalar_tensor_tensor(on[:, u % 2, j * DV:(j + 1) * DV], o[:, h, i, :],
                                                   rstd[:, 1, i * HA + h:i * HA + h + 1], gb[:, :],
                                                   ALU.mult, ALU.mult).then_inc(step, 1)
                dve.wait_ge(step, 2 * u + 2)
                dve.wait_ge(gated, u + 1)
                nc.vector.tensor_tensor(on[:, u % 2, :], on[:, u % 2, :], sil[:, u % 2, :], ALU.mult).then_inc(mixed, 1)
                if u:
                    store(u - 1)
            store(U - 1)


def stage_shared_k(nc, core, kv, k_t):
    sem = lambda n: nc.alloc_semaphore(f"sk_{n}")
    squared, step, meaned, rooted, normed, turned, taken, gained = map(
        sem, ("squared", "step", "meaned", "rooted", "normed", "turned", "taken", "gained"))
    KW = KVB * HD
    with ExitStack() as ctx:
        sq = sb(nc, ctx, "sk_sq", [P, TT, KW])
        r = sb(nc, ctx, "sk_r", [P, 3, TT * KVB])
        kn = sb(nc, ctx, "sk_kn", [P, TT, KVB, 2, HD])
        g = sb(nc, ctx, "sk_g", [P, 1])
        ps = banks(nc, ctx, "sk_ps", 4)
        block = ctx.enter_context(nc.Block())

        @block.scalar
        def _(act):
            nc.scalar.activation(sq[:, :, :], kv[:, :, 0:KW], ACT.Square).then_inc(squared, 1)

        @block.gpsimd
        def _(pool):
            pool.wait_ge(meaned, 1)
            nc.gpsimd.tensor_tensor(r[:, 2, :], r[:, 1, :], core.c[:, C_MHALF:C_MHALF + 1].to_broadcast([P, TT * KVB]),
                                    ALU.pow).then_inc(rooted, 1)

        @block.tensor
        def _(pe):
            pe.wait_ge(normed, TT)
            for h in range(KVB):
                for i in range(TT):
                    last = nc.tensor.transpose(ps[h][:, i * P:(i + 1) * P], kn[:, i, h, :, :].rearrange("p a d -> p (a d)"),
                                               core.c[:, C_IDENT:C_IDENT + P])
                last.then_inc(turned, 1)

        @block.vector
        def _(dve):
            nc.vector.tensor_tensor(g[:, :], core.v[:, V_QGK:V_QGK + 1], core.v[:, V_QGK + 1:V_QGK + 2], ALU.mult).then_inc(gained, 1)
            dve.wait_ge(squared, 1)
            nc.vector.tensor_reduce(r[:, 0, :], sq[:, :, :].rearrange("p i (h d) -> p (i h) d", d=HD), AX.X, ALU.add).then_inc(step, 1)
            dve.wait_ge(step, 1)
            nc.vector.tensor_scalar(r[:, 1, :], r[:, 0, :], 1.0 / HD, EPS, ALU.mult, ALU.add).then_inc(meaned, 1)
            dve.wait_ge(rooted, 1)
            for i in range(TT):
                nc.vector.tensor_tensor(kn[:, i, :, :, :], kv[:, i, 0:KW].rearrange("p (h d) -> p h d", d=HD).unsqueeze(2).to_broadcast([P, KVB, 2, HD]),
                                        r[:, 2, i * KVB:(i + 1) * KVB].unsqueeze(2).unsqueeze(3).to_broadcast([P, KVB, 2, HD]),
                                        ALU.mult).then_inc(normed, 1)
            dve.wait_ge(gained, 1)
            for h in range(KVB):
                dve.wait_ge(turned, h + 1)
                nc.vector.tensor_scalar(k_t[:, h, :], ps[h][:, :], g[:, 0:1], None, ALU.mult).then_inc(taken, 1)


def stage_head_scale(nc, core, tag, q_t, tiles, cols, out, scale2):
    sem = lambda n: nc.alloc_semaphore(f"{tag}_{n}")
    squared, summed, rooted, inverted, scaled = map(sem, ("squared", "summed", "rooted", "inverted", "scaled"))
    w = len(cols) * 2 * tiles
    with ExitStack() as ctx:
        sq = sb(nc, ctx, f"{tag}_sq", [P, 2, T])
        rt = sb(nc, ctx, f"{tag}_rt", [P, w])
        ps = banks(nc, ctx, f"{tag}_ps", 1)[0]
        block = ctx.enter_context(nc.Block())

        @block.scalar
        def _(act):
            for n in range(tiles):
                if n >= 2:
                    act.wait_ge(summed, n - 1)
                nc.scalar.activation(sq[:, n % 2, :], q_t[:, n, :], ACT.Square).then_inc(squared, 1)
            act.wait_ge(summed, tiles)
            nc.scalar.activation(rt[:, :], ps[:, 0:w], ACT.Sqrt, bias=core.eps[:, 1:2]).then_inc(rooted, 1)

        @block.tensor
        def _(pe):
            for n in range(tiles):
                pe.wait_ge(squared, n + 1)
                for i, c in enumerate(cols):
                    at = (i * tiles + n) * 2
                    last = nc.tensor.matmul(ps[:, at:at + 2], sq[:, n % 2, c:c + P], core.c[:, C_PAIR:C_PAIR + 2], start=True, stop=True)
                last.then_inc(summed, 1)

        @block.vector
        def _(dve):
            dve.wait_ge(rooted, 1)
            nc.vector.reciprocal(out.rearrange("p i h -> p (i h)"), rt[:, :]).then_inc(inverted, 1)
            if scale2 != 1:
                dve.wait_ge(inverted, 1)
                nc.vector.tensor_scalar(out.rearrange("p i h -> p (i h)"), out.rearrange("p i h -> p (i h)"), scale2, None, ALU.mult).then_inc(scaled, 1)


def stage_bias(nc, core, rel_bias, scratch, bias):
    sem = lambda n: nc.alloc_semaphore(f"rb_{n}")
    loaded, product, masked, stored, back, flipped, copied = map(sem, ("loaded", "product", "masked", "stored", "back", "flipped", "copied"))
    with ExitStack() as ctx:
        rb = sb(nc, ctx, "rb_in", [32, HB])
        row = sb(nc, ctx, "rb_row", [HB, 384])
        shifted = sb(nc, ctx, "rb_shifted", [P, HB, 256])
        ps = banks(nc, ctx, "rb_ps", 1)[0]
        turn = banks(nc, ctx, "rb_turn", 4)
        block = ctx.enter_context(nc.Block())

        @block.sync
        def _(sp):
            sp.dma_start(rb[:, :], rel_bias).then_inc(loaded, 16)
            sp.wait_ge(masked, 1)
            sp.dma_start(scratch, row[:, :]).then_inc(stored, 16)
            sp.wait_ge(stored, 16)
            with nc.allow_non_contiguous_dma("rows shifted by one"):
                for h in range(0, HB, 8):
                    src = bass.AP(scratch.tensor, h * 384, [[1, P], [384, 8], [1, 256]])
                    sp.dma_start(shifted[:, h:h + 8, :], src).then_inc(back, 16)

        @block.tensor
        def _(pe):
            pe.wait_ge(loaded, 16)
            nc.tensor.matmul(ps[0:HB, 0:384], rb[:, :], core.r[:, R_BUCKET:R_BUCKET + 384], start=True, stop=True).then_inc(product, 1)
            pe.wait_ge(back, 64)
            for i in range(HB // 2):
                if i >= 4:
                    pe.wait_ge(copied, i - 3)
                nc.tensor.matmul(turn[i % 4][:, :], core.c[:, C_FLIP:C_FLIP + P], shifted[:, 2 * i:2 * i + 2, :],
                                 start=True, stop=True).then_inc(flipped, 1)

        @block.vector
        def _(dve):
            dve.wait_ge(product, 1)
            nc.vector.tensor_tensor(row[:, :], ps[0:HB, 0:384], core.r[:, R_WINDOW:R_WINDOW + 384], ALU.add).then_inc(masked, 1)
            for i in range(HB // 2):
                dve.wait_ge(flipped, i + 1)
                nc.vector.tensor_copy(bias[:, 2 * i:2 * i + 2, :], turn[i % 4][:, :].rearrange("p (h s) -> p h s", h=2)).then_inc(copied, 1)


def stage_window_attention(nc, core, q_t, k_t, kv, rq, bias, sinks, z):
    sem = lambda n: nc.alloc_semaphore(f"wa_{n}")
    (loaded, scored, biased, step, shifted, expd, sunk, turned, act_taken, dve_taken, summed, mixed, weighted) = map(sem, (
        "loaded", "scored", "biased", "step", "shifted", "expd", "sunk", "turned", "scalar_taken", "vector_taken", "summed", "mixed", "weighted"))
    ident = core.c[:, C_IDENT:C_IDENT + P]
    G = HB // 4
    U = [(n, g) for n in range(TT) for g in range(G)]
    with ExitStack() as ctx:
        lg = sb(nc, ctx, "wa_lg", [P, 2, 4, 256])
        pt = sb(nc, ctx, "wa_pt", [P, 4, 2, P])
        sm = sb(nc, ctx, "wa_sm", [P, 2, 8, 4])
        snk = sb(nc, ctx, "wa_snk", [P, HB])
        tmp = sb(nc, ctx, "wa_tmp", [P, 256])
        sc = [banks(nc, ctx, f"wa_sc{e}", 2) for e in range(2)]
        tp = banks(nc, ctx, "wa_tp", 2)
        po = banks(nc, ctx, "wa_po", 2)
        block = ctx.enter_context(nc.Block())
        first = lambda n: P if n == 0 else 0
        col = lambda u, k, e=slice(0, 4): sm[:, u % 2, k, e]

        @block.sync
        def _(sp):
            sp.dma_start(snk[:, :], sinks.partition_broadcast(P)).then_inc(loaded, 16)

        @block.tensor
        def _(pe):
            def scores(u):
                n, g = U[u]
                s0 = first(n)
                if u >= 2:
                    pe.wait_ge(biased, u - 1)
                for e in range(4):
                    half = slice(64 * (e % 2), 64 * (e % 2) + 64)
                    last = nc.tensor.matmul(sc[e % 2][u % 2][:, e // 2 * 256 + s0:e // 2 * 256 + 256],
                                            q_t[half, 2 * g + e // 2, n * P:(n + 1) * P],
                                            k_t[half, g // 2, n * P + s0 - P:(n + 1) * P], start=True, stop=True)
                last.then_inc(scored, 1)
            scores(0)
            for u, (n, g) in enumerate(U):
                if u + 1 < len(U):
                    scores(u + 1)
                blocks = range(1 if n == 0 else 0, 2)
                for p in range(2):
                    pe.wait_ge(expd, 2 * u + p + 1)
                    if u:
                        pe.wait_ge((act_taken, dve_taken)[p], u)
                    for e in (2 * p, 2 * p + 1):
                        for b in blocks:
                            last = nc.tensor.transpose(tp[p][:, (e % 2 * 2 + b) * P:(e % 2 * 2 + b + 1) * P],
                                                       lg[:, u % 2, e, b * P:(b + 1) * P], ident)
                    last.then_inc(turned, 1)
                if u >= 2:
                    pe.wait_ge(weighted, u - 1)
                for e in range(4):
                    if e % 2 == 0:
                        pe.wait_ge((act_taken, dve_taken)[e // 2], u + 1)
                    for b in blocks:
                        last = nc.tensor.matmul(po[u % 2][:, e * HD:(e + 1) * HD], pt[:, e, b, :],
                                                kv[:, n - 1 + b, (KVB + g // 2) * HD:(KVB + g // 2 + 1) * HD],
                                                start=(b == blocks[0]), stop=(b == 1))
                last.then_inc(mixed, 1)

        @block.scalar
        def _(act):
            for u, (n, g) in enumerate(U):
                s0 = first(n)
                act.wait_ge(shifted, u + 1)
                for e in range(4):
                    last = nc.scalar.activation(lg[:, u % 2, e, s0:256], lg[:, u % 2, e, s0:256], ACT.Exp,
                                                bias=col(u, 2, slice(e, e + 1)), accum_out=col(u, 4, slice(e, e + 1)))
                    if e % 2:
                        last.then_inc(expd, 1)
                nc.scalar.activation(col(u, 5), col(u, 3), ACT.Exp).then_inc(sunk, 1)
                act.wait_ge(turned, 2 * u + 1)
                if u:
                    act.wait_ge(mixed, u)
                nc.scalar.activation(pt[:, 0:2, first(n) // P:2, :], tp[0][:, :].rearrange("p (e b t) -> p e b t", e=2, b=2)[:, :, first(n) // P:2, :],
                                     ACT.Copy).then_inc(act_taken, 1)

        @block.vector
        def _(dve):
            then = Chain(dve, step)

            def logits(u):
                n, g = U[u]
                s0 = first(n)
                dve.wait_ge(scored, u + 1)
                if u >= 2:
                    dve.wait_ge(turned, 2 * (u - 1))
                for e in range(4):
                    h = 4 * g + e
                    last = nc.vector.scalar_tensor_tensor(lg[:, u % 2, e, s0:256], sc[e % 2][u % 2][:, e // 2 * 256 + s0:e // 2 * 256 + 256],
                                                          rq[:, n, h:h + 1], bias[:, h, s0:256], ALU.mult, ALU.add)
                last.then_inc(biased, 1)
                dve.wait_ge(biased, u + 1)
                sk = snk[:, 4 * g:4 * g + 4]
                then(nc.vector.tensor_reduce(col(u, 0), lg[:, u % 2, :, s0:256], AX.X, ALU.max))
                then(nc.vector.tensor_tensor(col(u, 1), col(u, 0), sk, ALU.max))
                nc.vector.tensor_scalar(col(u, 2), col(u, 1), -1.0, None, ALU.mult)
                nc.vector.tensor_tensor(col(u, 3), sk, col(u, 1), ALU.subtract).then_inc(shifted, 1)
            dve.wait_ge(loaded, 16)
            logits(0)
            for u, (n, g) in enumerate(U):
                if u + 1 < len(U):
                    logits(u + 1)
                dve.wait_ge(turned, 2 * u + 2)
                if u:
                    dve.wait_ge(mixed, u)
                nc.vector.tensor_copy(pt[:, 2:4, first(n) // P:2, :], tp[1][:, :].rearrange("p (e b t) -> p e b t", e=2, b=2)[:, :, first(n) // P:2, :]).then_inc(dve_taken, 1)
                dve.wait_ge(sunk, u + 1)
                then(nc.vector.tensor_tensor(col(u, 6), col(u, 4), col(u, 5), ALU.add))
                then(nc.vector.reciprocal(col(u, 7), col(u, 6)))
                dve.wait_ge(mixed, u + 1)
                then(nc.vector.tensor_tensor(tmp[:, :].rearrange("p (e d) -> p e d", e=4), po[u % 2][:, 0:256].rearrange("p (e d) -> p e d", e=4),
                                             sm[:, u % 2, 7, :].unsqueeze(2).to_broadcast([P, 4, HD]), ALU.mult))
                zz = z[:, n, g * 256:(g + 1) * 256]
                nc.vector.tensor_tensor(zz, zz, tmp[:, :], ALU.mult).then_inc(weighted, 1)


def stage_turn(nc, core, tag, src, n, out):
    turned, taken = [nc.alloc_semaphore(f"{tag}_turned{i}") for i in range(2)], [nc.alloc_semaphore(f"{tag}_taken{i}") for i in range(2)]
    with ExitStack() as ctx:
        ps = banks(nc, ctx, f"{tag}_ps", 4)
        block = ctx.enter_context(nc.Block())

        @block.tensor
        def _(pe):
            for k in range(n):
                if k >= 4:
                    pe.wait_ge(taken[k % 2], k // 2 - 1)
                for i in range(TT):
                    last = nc.tensor.transpose(ps[k % 4][:, i * P:(i + 1) * P], src[:, i, k * P:(k + 1) * P], core.c[:, C_IDENT:C_IDENT + P])
                last.then_inc(turned[k % 2], 1)

        @block.scalar
        def _(act):
            for k in range(0, n, 2):
                act.wait_ge(turned[0], k // 2 + 1)
                nc.scalar.activation(out[:, k, :], ps[k % 4][:, :], ACT.Copy).then_inc(taken[0], 1)

        @block.vector
        def _(dve):
            for k in range(1, n, 2):
                dve.wait_ge(turned[1], k // 2 + 1)
                nc.vector.tensor_copy(out[:, k, :], ps[k % 4][:, :]).then_inc(taken[1], 1)


def first_block(nc, core, a, scratch):
    silu_to = lambda dst: (lambda c, i, product: nc.scalar.activation(dst[:, i, c * 512:(c + 1) * 512], product, ACT.Silu))
    with ExitStack() as ctx:
        h = sb(nc, ctx, "h_t", [P, KD, T])
        with ExitStack() as c2:
            qkv = sb(nc, c2, "qkv_t", [P, QKV_TILES, T])
            rows = sb(nc, c2, "gate_rows", [8, 2, T])
            cols = sb(nc, c2, "gate_cols", [P, 4, TT, HA])
            ss = sb(nc, c2, "o_squares", [P, TT, HA])
            stage_norm(nc, core, "na", x_tiles(core), V_ANORM, h)
            stage_proj_conv(nc, core, "pa", h, a["a_w_in"], 0, 8, core.ta, qkv, [(0, T)], T)
            stage_unit_rows(nc, core, "ua", qkv)
            stage_delta_gates(nc, core, h, a["a_w_in"], rows, cols)
            stage_delta_chunks(nc, core, qkv, rows, cols, ss)
            o = qkv[:, 2 * HA:, :].rearrange("p (h j) (a d) -> p h (j a) d", j=2, a=2)
            stage_delta_out(nc, core, h, a["a_w_in"], QKV_TILES * P, o, ss[:, :, :], a["a_o_gain"], qkv[:, 0:2 * HA, :])
            stage_proj_n(nc, core, "oa", qkv[:, 0:2 * HA, :], HA * DV // P, X_COLS, a["a_w_out"], [(0, 512), (512, 512)], "vector", add_to_x(nc, core))
        kv = sb(nc, ctx, "kv", [P, TT, 2 * KVB * HD])
        k_t = sb(nc, ctx, "k_t", [P, KVB, T])
        q_t = sb(nc, ctx, "q_t", [P, HB * HD // P, T])
        z = sb(nc, ctx, "z", [P, TT, HB * HD])
        rq = sb(nc, ctx, "rq", [P, TT, HB])
        stage_norm(nc, core, "nk", x_tiles(core), V_KVNORM, h)
        stage_proj_n(nc, core, "pk", h, KD, X_COLS, a["w_kv"], [(0, 512)], "scalar",
                     lambda c, i, product: nc.scalar.activation(kv[:, i, :], product, ACT.Copy))
        stage_shared_k(nc, core, kv, k_t)
        stage_norm(nc, core, "nb", x_tiles(core), V_BNORM, h)
        stage_proj_t(nc, core, "pq", h, T, a["b_w_in"], 0, 4, q_t, [(0, T)])
        stage_proj_n(nc, core, "pz", h, KD, X_COLS, a["b_w_in"], [(HB * HD + c * 512, 512) for c in range(4)], "scalar", silu_to(z))
        stage_head_scale(nc, core, "hq", q_t, HB * HD // P, [i * P for i in range(TT)], rq[:, :, :], 1)
        with ExitStack() as c2:
            bias = sb(nc, c2, "bias", [P, HB, 256])
            stage_bias(nc, core, a["rel_bias"], scratch, bias)
            stage_window_attention(nc, core, q_t, k_t, kv, rq, bias, a["b_sinks"], z)
        stage_turn(nc, core, "tb", z, HB * HD // P, q_t)
        stage_proj_n(nc, core, "ob", q_t, HB * HD // P, X_COLS, a["b_w_out"], [(0, 512), (512, 512)], "vector", add_to_x(nc, core))


S_TILES = [(META, 0, 0)] + [(P, META + P * i, P * i) for i in range(TT)]
HALF2 = T2 // 2
MQ, MV, MO, MI, MF, FQ, FV, FF = 0, 1024, 1536, 2048, 2052, 2056, 3080, 3592


def stage_mix_gates(nc, core, h_t, w, mrow, acol, emcol, negc):
    sem = lambda n: nc.alloc_semaphore(f"mg_{n}")
    zeroed, loaded, product, vstep, astep, turned, cast, cast_taken = map(
        sem, ("zeroed", "loaded", "product", "vector_step", "scalar_step", "turned", "cast", "cast_taken"))
    G = 72
    with ExitStack() as ctx:
        wg = sb(nc, ctx, "mg_w", [P, KD, G])
        t = [sb(nc, ctx, f"mg_t{i}", [G, T2]) for i in range(4)]
        b = sb(nc, ctx, "mg_b", [HM, T2])
        am = sb(nc, ctx, "mg_am", [HM, 2, T2])
        nc8 = sb(nc, ctx, "mg_nc", [HF, T2])
        ps = banks(nc, ctx, "mg_ps", 2)
        pt = banks(nc, ctx, "mg_pt", 1)[0]
        pc = banks(nc, ctx, "mg_pc", 4)
        block = ctx.enter_context(nc.Block())
        wv = w_view(w, KD)

        @block.sync
        def _(sp):
            sp.wait_ge(zeroed, 1)
            for dst, src, n in ((0, MI, HM), (32, MF, HM), (64, FF, HF)):
                with nc.allow_non_contiguous_dma("a few gate columns"):
                    sp.dma_start(wg[:, :, dst:dst + n], wv[:, :, src:src + n]).then_inc(loaded, 16)

        @block.tensor
        def _(pe):
            pe.wait_ge(loaded, 48)
            for half in range(2):
                for k in range(KD):
                    last = nc.tensor.matmul(ps[half][0:G, 0:HALF2], wg[:, k, :], h_t[:, k, half * HALF2:(half + 1) * HALF2],
                                            start=(k == 0), stop=(k == KD - 1))
            last.then_inc(product, 1)
            pe.wait_ge(vstep, 10)
            pe.wait_ge(astep, 3)
            for j, (rows, c, _t) in enumerate(S_TILES):
                nc.tensor.transpose(pt[0:rows, j * 4:j * 4 + 4], am[:, 0, c:c + rows], core.c[0:HM, C_IDENT:C_IDENT + HM])
            for i in range(TT):
                c = META + i * P
                last = nc.tensor.transpose(pt[:, 32 + i * 4:36 + i * 4], am[:, 1, c:c + P], core.c[0:HM, C_IDENT:C_IDENT + HM])
            last.then_inc(turned, 1)
            for u in range(2 * HF):
                h, half = divmod(u, 2)
                if u >= 4:
                    pe.wait_ge(cast_taken, u - 3)
                nc.tensor.matmul(pc[u % 4][:, 0:HALF2], core.r[0:HF, R_SEL + h * P:R_SEL + (h + 1) * P],
                                 nc8[:, half * HALF2:(half + 1) * HALF2], start=True, stop=True).then_inc(cast, 1)

        @block.scalar
        def _(act):
            act.wait_ge(vstep, 3)
            nc.scalar.activation(t[1][:, :], t[1][:, :], ACT.Exp, scale=-1.0).then_inc(astep, 1)
            act.wait_ge(astep, 1)
            nc.scalar.activation(t[1][:, :], t[1][:, :], ACT.Ln, bias=1.0).then_inc(astep, 1)
            act.wait_ge(vstep, 10)
            nc.scalar.activation(am[:, 1, :], am[:, 1, :], ACT.Exp, scale=-1.0).then_inc(astep, 1)
            for u in range(2 * HF):
                h, half = divmod(u, 2)
                act.wait_ge(cast, u + 1)
                nc.scalar.activation(negc[:, h, half * HALF2:(half + 1) * HALF2], pc[u % 4][:, 0:HALF2], ACT.Copy).then_inc(cast_taken, 1)

        @block.vector
        def _(dve):
            nc.vector.memset(wg[:, :, :], 0.0).then_inc(zeroed, 1)
            then = Chain(dve, vstep)
            dve.wait_ge(product, 1)
            for half in range(2):
                then(nc.vector.tensor_scalar(t[0][:, half * HALF2:(half + 1) * HALF2], ps[half][0:G, 0:HALF2], core.v[0:G, V_BI:V_BI + 1], None, ALU.add))
            then(nc.vector.scalar_tensor_tensor(t[1][:, :], t[0][:, :], -1.0, t[0][:, :], ALU.mult, ALU.max))
            dve.wait_ge(astep, 2)
            then(nc.vector.scalar_tensor_tensor(t[2][:, :], t[0][:, :], 0.0, t[1][:, :], ALU.min, ALU.subtract))
            then(nc.vector.tensor_tensor_scan(t[3][:, :], core.one[0:G, :], t[2][:, :], 0.0, ALU.mult, ALU.add))
            then(nc.vector.tensor_copy(b[:, :], t[3][32:32 + HM, :]))
            then(nc.vector.tensor_scalar(nc8[:, :], t[3][64:64 + HF, :], -1.0, None, ALU.mult))
            then(nc.vector.tensor_tensor(am[:, 0, :], t[0][0:HM, :], b[:, :], ALU.subtract))
            then(nc.vector.tensor_tensor_scan(mrow[:, :], am[:, 0, :], am[:, 0, :], 0.0, ALU.max, ALU.max))
            then(nc.vector.tensor_tensor(am[:, 1, :], b[:, :], mrow[:, :], ALU.add))
            dve.wait_ge(turned, 1)
            nc.vector.tensor_copy(acol[:, 1:, :], pt[:, 4:20].rearrange("p (j h) -> p j h", h=4))
            nc.vector.tensor_copy(acol[0:META, 0, :], pt[0:META, 0:4])
            nc.vector.tensor_copy(emcol[:, :, :], pt[:, 32:48].rearrange("p (j h) -> p j h", h=4))


def stage_mlstm(nc, core, qk, v, mrow, acol, nd):
    sem = lambda n: nc.alloc_semaphore(f"ml_{n}")
    cast, shifted, expd, masked, scored, weighted, mixed, taken = map(
        sem, ("cast", "shifted", "expd", "masked", "scored", "weighted", "mixed", "taken"))
    offs, o = [], 0
    for j, (rows, c, t0) in enumerate(S_TILES):
        offs.append(o)
        o += T - t0
    N = len(S_TILES)
    with ExitStack() as ctx:
        ew = sb(nc, ctx, "ml_ew", [P, 2, o])
        pm = banks(nc, ctx, "ml_pm", 2)
        psc = banks(nc, ctx, "ml_ps", 4)
        po = banks(nc, ctx, "ml_po", 2)
        block = ctx.enter_context(nc.Block())
        e = lambda h, j, a=0, n=None: ew[0:S_TILES[j][0], h % 2, offs[j] + a:offs[j] + (T - S_TILES[j][2] if n is None else a + n)]

        @block.tensor
        def _(pe):
            for h in range(HM):
                if h >= 2:
                    pe.wait_ge(shifted, N * (h - 1))
                nc.tensor.matmul(pm[h % 2][:, :], core.r[0:HM, R_SEL + h * P:R_SEL + (h + 1) * P], mrow[:, META:], start=True, stop=True).then_inc(cast, 1)
                for j, (rows, c, t0) in enumerate(S_TILES):
                    u = h * N + j
                    if u >= 4:
                        pe.wait_ge(weighted, u - 3)
                    nc.tensor.matmul(psc[u % 4][0:rows, 0:T - t0], qk[:, HM + h, c:c + rows], qk[:, h, META + t0:T2], start=True, stop=True).then_inc(scored, 1)
                for i in range(TT):
                    u = h * TT + i
                    if u >= 2:
                        pe.wait_ge(taken, u - 1)
                    pe.wait_ge(weighted, h * N + i + 2)
                    for j in range(i + 2):
                        rows, c, t0 = S_TILES[j]
                        last = nc.tensor.matmul(po[u % 2][:, 0:DM + 1], e(h, j, i * P - t0, P), v[0:rows, j, h, :], start=(j == 0), stop=(j == i + 1))
                    last.then_inc(mixed, 1)

        @block.vector
        def _(dve):
            for h in range(HM):
                dve.wait_ge(cast, h + 1)
                if h >= 2:
                    dve.wait_ge(mixed, TT * (h - 1))
                for j, (rows, c, t0) in enumerate(S_TILES):
                    nc.vector.tensor_scalar(e(h, j), pm[h % 2][0:rows, t0:T], acol[0:rows, j, h:h + 1], 0.0, ALU.subtract, ALU.max).then_inc(shifted, 1)
                for j, (rows, c, t0) in enumerate(S_TILES):
                    u = h * N + j
                    dve.wait_ge(scored, u + 1)
                    dve.wait_ge(expd, u + 1)
                    if j:
                        dve.wait_ge(masked, h * TT + j)
                    nc.vector.scalar_tensor_tensor(e(h, j), psc[u % 4][0:rows, 0:T - t0], DM ** -0.5, e(h, j), ALU.mult, ALU.mult).then_inc(weighted, 1)

        @block.scalar
        def _(act):
            for h in range(HM):
                for j in range(N):
                    act.wait_ge(shifted, h * N + j + 1)
                    nc.scalar.activation(e(h, j), e(h, j), ACT.Exp, scale=-1.0).then_inc(expd, 1)
                for i in range(TT):
                    u = h * TT + i
                    act.wait_ge(mixed, u + 1)
                    nc.scalar.activation(nd[:, i, h, :], po[u % 2][:, 0:DM + 1], ACT.Copy).then_inc(taken, 1)

        @block.gpsimd
        def _(pool):
            for h in range(HM):
                for j in range(1, N):
                    pool.wait_ge(expd, h * N + j + 1)
                    nc.gpsimd.tensor_tensor(e(h, j, 0, P), e(h, j, 0, P), core.c[:, C_LE:C_LE + P], ALU.mult).then_inc(masked, 1)


def stage_mlstm_out(nc, core, nd, emcol, so, gain, y):
    sem = lambda n: nc.alloc_semaphore(f"mo_{n}")
    loaded, step, divided, squared, meaned, rooted = map(sem, ("loaded", "step", "divided", "squared", "meaned", "rooted"))
    with ExitStack() as ctx:
        gb = sb(nc, ctx, "mo_gain", [P, HM * DM])
        r = sb(nc, ctx, "mo_r", [P, 6, TT * HM])
        sq = sb(nc, ctx, "mo_sq", [P, TT, HM * DM])
        block = ctx.enter_context(nc.Block())
        th = lambda k: r[:, k, :].rearrange("p (i h) -> p i h", h=HM)
        wide = lambda k: th(k).unsqueeze(3).to_broadcast([P, TT, HM, DM])
        yh = y[:, :, 0:HM * DM].rearrange("p i (h d) -> p i h d", h=HM)
        ym = y[:, :, 0:HM * DM]

        @block.sync
        def _(sp):
            sp.dma_start(gb[:, :], gain.partition_broadcast(P)).then_inc(loaded, 16)

        @block.scalar
        def _(act):
            act.wait_ge(divided, 1)
            nc.scalar.activation(sq[:, :, :], ym, ACT.Square).then_inc(squared, 1)

        @block.gpsimd
        def _(pool):
            pool.wait_ge(meaned, 1)
            nc.gpsimd.tensor_tensor(r[:, 5, :], r[:, 4, :], core.c[:, C_MHALF:C_MHALF + 1].to_broadcast([P, TT * HM]), ALU.pow).then_inc(rooted, 1)

        @block.vector
        def _(dve):
            then = Chain(dve, step)
            den = nd[:, :, :, DM]
            then(nc.vector.scalar_tensor_tensor(th(0), den, -1.0, den, ALU.mult, ALU.max))
            then(nc.vector.tensor_tensor(th(1), th(0), emcol, ALU.max))
            then(nc.vector.reciprocal(r[:, 2, :], r[:, 1, :]))
            nc.vector.tensor_tensor(yh, nd[:, :, :, 0:DM], wide(2), ALU.mult).then_inc(divided, 1)
            dve.wait_ge(squared, 1)
            then(nc.vector.tensor_reduce(r[:, 3, :], sq[:, :, :].rearrange("p i (h d) -> p (i h) d", h=HM), AX.X, ALU.add))
            nc.vector.tensor_scalar(r[:, 4, :], r[:, 3, :], 1.0 / DM, EPS, ALU.mult, ALU.add).then_inc(meaned, 1)
            dve.wait_ge(rooted, 1)
            then(nc.vector.tensor_tensor(yh, yh, wide(5), ALU.mult))
            dve.wait_ge(loaded, 16)
            then(nc.vector.tensor_tensor(ym, ym, gb[:, :].unsqueeze(1).to_broadcast([P, TT, HM * DM]), ALU.mult))
            then(nc.vector.tensor_tensor(ym, ym, so[:, :, :], ALU.mult))


def stage_key_scale(nc, core, k_t):
    sem = lambda n: nc.alloc_semaphore(f"ks_{n}")
    gained, squared, summed, rooted, inverted, scaled = map(sem, ("gained", "squared", "summed", "rooted", "inverted", "scaled"))
    with ExitStack() as ctx:
        g = sb(nc, ctx, "ks_g", [P, 1])
        sq = sb(nc, ctx, "ks_sq", [P, 4, HALF2])
        rt = sb(nc, ctx, "ks_rt", [P, 4, HALF2])
        ps = banks(nc, ctx, "ks_ps", 4)
        block = ctx.enter_context(nc.Block())
        part = lambda u: k_t[:, u // 2, u % 2 * HALF2:(u % 2 + 1) * HALF2]
        N = 8

        @block.scalar
        def _(act):
            for b in range(0, N, 4):
                for u in range(b, b + 4):
                    if u >= 4:
                        act.wait_ge(summed, u - 3)
                    nc.scalar.activation(sq[:, u % 4, :], part(u), ACT.Square).then_inc(squared, 1)
                for u in range(b, b + 4):
                    act.wait_ge(summed, u + 1)
                    if u >= 4:
                        act.wait_ge(scaled, u - 3)
                    nc.scalar.activation(rt[:, u % 4, :], ps[u % 4][:, 0:HALF2], ACT.Sqrt, bias=core.eps[:, 0:1], scale=1.0 / DF).then_inc(rooted, 1)

        @block.tensor
        def _(pe):
            for u in range(N):
                pe.wait_ge(squared, u + 1)
                if u >= 4:
                    pe.wait_ge(rooted, u - 3)
                nc.tensor.matmul(ps[u % 4][:, 0:HALF2], core.c[:, C_HALVES:C_HALVES + P], sq[:, u % 4, :], start=True, stop=True).then_inc(summed, 1)

        @block.vector
        def _(dve):
            nc.vector.tensor_tensor(g[:, :], core.v[:, V_FQK:V_FQK + 1], core.v[:, V_FQK + 1:V_FQK + 2], ALU.mult).then_inc(gained, 1)
            dve.wait_ge(gained, 1)
            for u in range(N):
                dve.wait_ge(rooted, u + 1)
                nc.vector.reciprocal(rt[:, u % 4, :], rt[:, u % 4, :]).then_inc(inverted, 1)
                dve.wait_ge(inverted, u + 1)
                nc.vector.scalar_tensor_tensor(part(u), part(u), g[:, 0:1], rt[:, u % 4, :], ALU.mult, ALU.mult).then_inc(scaled, 1)


def stage_forgetting_attention(nc, core, qk, v, rq, negc, y):
    sem = lambda n: nc.alloc_semaphore(f"fa_{n}")
    (scored, biased, step, shifted, expd, turned_a, turned_b, act_taken, dve_taken, mixed, weighted) = map(sem, (
        "scored", "biased", "step", "shifted", "expd", "turned_a", "turned_b", "scalar_taken", "vector_taken", "mixed", "weighted"))
    ident = core.c[:, C_IDENT:C_IDENT + P]
    U = [(h, i) for h in range(HF) for i in range(TT)]
    nb = lambda u: sum(1 for w in range(u + 1) if U[w][1] >= 2)
    with ExitStack() as ctx:
        lg = sb(nc, ctx, "fa_lg", [P, 2, T2])
        pt = sb(nc, ctx, "fa_pt", [P, 5, P])
        sm = sb(nc, ctx, "fa_sm", [P, 2, 4])
        sc = [banks(nc, ctx, f"fa_sc{e}", 2) for e in range(2)]
        tp = banks(nc, ctx, "fa_tp", 2)
        po = banks(nc, ctx, "fa_po", 2)
        block = ctx.enter_context(nc.Block())
        width = lambda i: META + P * (i + 1)
        col = lambda u, k: sm[:, u % 2, k:k + 1]

        @block.tensor
        def _(pe):
            def scores(u):
                h, i = U[u]
                half, hw = slice(64 * (h % 2), 64 * (h % 2) + 64), width(i) // 2
                if u >= 2:
                    pe.wait_ge(biased, u - 1)
                for p in range(2):
                    last = nc.tensor.matmul(sc[p][u % 2][:, 0:hw], qk[half, h // 2, META + i * P:META + (i + 1) * P],
                                            qk[half, 4 + h // 2, p * hw:(p + 1) * hw], start=True, stop=True)
                last.then_inc(scored, 1)
            scores(0)
            for u, (h, i) in enumerate(U):
                if u + 1 < len(U):
                    scores(u + 1)
                pe.wait_ge(expd, u + 1)
                if u:
                    pe.wait_ge(act_taken, u)
                for j in range(min(3, i + 2)):
                    rows, c, _t = S_TILES[j]
                    last = nc.tensor.transpose(tp[0][0:rows, j * P:(j + 1) * P], lg[:, u % 2, c:c + rows], ident)
                last.then_inc(turned_a, 1)
                if i >= 2:
                    if nb(u) > 1:
                        pe.wait_ge(dve_taken, nb(u) - 1)
                    for j in range(3, i + 2):
                        rows, c, _t = S_TILES[j]
                        last = nc.tensor.transpose(tp[1][:, (j - 3) * P:(j - 2) * P], lg[:, u % 2, c:c + rows], ident)
                    last.then_inc(turned_b, 1)
                if u >= 2:
                    pe.wait_ge(weighted, u - 1)
                pe.wait_ge(act_taken, u + 1)
                if i >= 2:
                    pe.wait_ge(dve_taken, nb(u))
                for j in range(i + 2):
                    rows, c, _t = S_TILES[j]
                    last = nc.tensor.matmul(po[u % 2][:, 0:DF], pt[0:rows, j, :], v[0:rows, j, h * DF:(h + 1) * DF], start=(j == 0), stop=(j == i + 1))
                last.then_inc(mixed, 1)

        @block.scalar
        def _(act):
            for u, (h, i) in enumerate(U):
                act.wait_ge(shifted, u + 1)
                nc.scalar.activation(lg[:, u % 2, 0:width(i)], lg[:, u % 2, 0:width(i)], ACT.Exp, bias=col(u, 1), accum_out=col(u, 2)).then_inc(expd, 1)
                act.wait_ge(turned_a, u + 1)
                if u:
                    act.wait_ge(mixed, u)
                nc.scalar.activation(pt[0:META, 0, :], tp[0][0:META, 0:P], ACT.Copy)
                n = min(2, i + 1)
                nc.scalar.activation(pt[:, 1:1 + n, :], tp[0][:, P:P + n * P].rearrange("p (j t) -> p j t", t=P), ACT.Copy).then_inc(act_taken, 1)

        @block.vector
        def _(dve):
            then = Chain(dve, step)

            def logits(u):
                h, i = U[u]
                hw, w = width(i) // 2, width(i)
                dve.wait_ge(scored, u + 1)
                if u >= 2:
                    dve.wait_ge(mixed, u - 1)
                for p in range(2):
                    c = slice(p * hw, (p + 1) * hw)
                    last = nc.vector.scalar_tensor_tensor(lg[:, u % 2, c], sc[p][u % 2][:, 0:hw], rq[:, i, h:h + 1], negc[:, h, c], ALU.mult, ALU.add)
                last.then_inc(biased, 1)
                dve.wait_ge(biased, u + 1)
                then(nc.vector.tensor_tensor(lg[:, u % 2, w - P:w], lg[:, u % 2, w - P:w], core.c[:, C_NEGDIAG:C_NEGDIAG + P], ALU.add))
                then(nc.vector.tensor_reduce(col(u, 0), lg[:, u % 2, 0:w], AX.X, ALU.max))
                nc.vector.tensor_scalar(col(u, 1), col(u, 0), -1.0, None, ALU.mult).then_inc(shifted, 1)
            logits(0)
            for u, (h, i) in enumerate(U):
                if u + 1 < len(U):
                    logits(u + 1)
                if i >= 2:
                    dve.wait_ge(turned_b, nb(u))
                    dve.wait_ge(mixed, u)
                    nc.vector.tensor_copy(pt[:, 3:i + 2, :], tp[1][:, 0:(i - 1) * P].rearrange("p (j t) -> p j t", t=P)).then_inc(dve_taken, 1)
                dve.wait_ge(expd, u + 1)
                then(nc.vector.reciprocal(col(u, 3), col(u, 2)))
                dve.wait_ge(mixed, u + 1)
                nc.vector.tensor_scalar(y[:, i, HM * DM + h * DF:HM * DM + (h + 1) * DF], po[u % 2][:, 0:DF], col(u, 3), None, ALU.mult).then_inc(weighted, 1)


def mixers(nc, core, a):
    tiles = [(core.xm[:, :], META, 0)] + [(core.x[:, i, :], P, META + i * P) for i in range(TT)]
    with ExitStack() as ctx:
        h = sb(nc, ctx, "h2_t", [P, KD, T2])
        mqk = sb(nc, ctx, "mqk_t", [P, 2 * HM, T2])
        fqk = sb(nc, ctx, "fqk_t", [P, 8, T2])
        vm = sb(nc, ctx, "vm", [P, 5, HM, DM + 1])
        vf = sb(nc, ctx, "vf", [P, 5, HF * DF])
        so = sb(nc, ctx, "so", [P, TT, HM * DM])
        y = sb(nc, ctx, "y", [P, TT, D])
        mrow = sb(nc, ctx, "m_row", [HM, T2])
        acol = sb(nc, ctx, "a_col", [P, 5, HM])
        emcol = sb(nc, ctx, "em_col", [P, TT, HM])
        rq = sb(nc, ctx, "rq2", [P, TT, HF])
        with nc.Block() as block:
            @block.vector
            def _(dve):
                nc.vector.memset(vm[:, :, :, DM:DM + 1], 1.0)
                nc.vector.memset(core.one[:, :], 1.0)
        stage_norm(nc, core, "n2", tiles, V_NORM2, h)
        w = a["w_in_2"]
        stage_proj_conv(nc, core, "pm", h, w, MQ, 2, core.tm, mqk, [(0, HALF2), (HALF2, HALF2)], T2)
        stage_proj_t(nc, core, "pf", h, T2, w, FQ, 2, fqk, [(0, HALF2), (HALF2, HALF2)])

        def values(c, j, product):
            rows = S_TILES[j][0]
            if c == 0:
                return nc.scalar.activation(vm[0:rows, j, :, 0:DM], product.rearrange("p (h d) -> p h d", h=HM), ACT.Copy)
            return nc.scalar.activation(vf[0:rows, j, :], product, ACT.Copy)
        stage_proj_n(nc, core, "pv", h, KD, [(rows, c) for rows, c, _ in S_TILES], w, [(MV, 512), (FV, 512)], "scalar", values)
        stage_proj_n(nc, core, "po", h, KD, [(P, META + i * P) for i in range(TT)], w, [(MO, 512)], "scalar",
                     lambda c, i, product: nc.scalar.activation(so[:, i, :], product, ACT.Sigmoid))
        with ExitStack() as c2:
            negc = sb(nc, c2, "negc", [P, HF, T2])
            stage_mix_gates(nc, core, h, w, mrow, acol, emcol, negc)
            with ExitStack() as c3:
                nd = sb(nc, c3, "nd", [P, TT, HM, DM + 1])
                stage_mlstm(nc, core, mqk, vm, mrow, acol, nd)
                stage_mlstm_out(nc, core, nd, emcol[:, :, :], so, a["m_out_norm_2"], y)
            stage_head_scale(nc, core, "hf", fqk[:, 0:4, META:], 4, [i * P for i in range(TT)], rq[:, :, :], 1)
            stage_key_scale(nc, core, fqk[:, 4:8, :])
            stage_forgetting_attention(nc, core, fqk, vf, rq, negc, y)
        y_t = h[:, :, 0:T]
        stage_turn(nc, core, "t2", y, KD, y_t)
        stage_proj_n(nc, core, "o2", y_t, KD, X_COLS, a["w_out_2"], [(0, 512), (512, 512)], "vector", add_to_x(nc, core))


def stage_topk(nc, core, q_t, keys, ids, gate):
    sem = lambda n: nc.alloc_semaphore(f"tk_{n}")
    scored, copied, step, shifted, expd, searched = map(sem, ("scored", "copied", "step", "shifted", "expd", "searched"))
    N2 = 2 * PH
    with ExitStack() as ctx:
        sc = sb(nc, ctx, "tk_sc", [P, N2, NK])
        sc2 = sb(nc, ctx, "tk_sc2", [P, N2, NK])
        cd = sb(nc, ctx, "tk_cd", [P, PH, 256])
        cd2 = sb(nc, ctx, "tk_cd2", [P, PH, 256])
        eq = sb(nc, ctx, "tk_eq", [P, PH, 16, 16])
        vv = sb(nc, ctx, "tk_vv", [P, N2, TOPK])
        ii = sb(nc, ctx, "tk_ii", [P, N2, TOPK], U32)
        fi = sb(nc, ctx, "tk_fi", [P, N2, TOPK])
        ts = sb(nc, ctx, "tk_ts", [P, PH, TOPK])
        tp = sb(nc, ctx, "tk_tp", [P, PH, TOPK], U32)
        hl = sb(nc, ctx, "tk_hl", [P, 2, SLOTS], U32)
        hf = sb(nc, ctx, "tk_hf", [P, 2, SLOTS])
        pick = sb(nc, ctx, "tk_pick", [P, 3, SLOTS])
        ex = sb(nc, ctx, "tk_ex", [P, PH, TOPK])
        den = sb(nc, ctx, "tk_den", [P, 2, PH])
        ps = banks(nc, ctx, "tk_ps", 4)
        block = ctx.enter_context(nc.Block())

        @block.tensor
        def _(pe):
            for i in range(TT):
                for b in range(4):
                    if i:
                        pe.wait_ge(copied, (i - 1) * 4 + b + 1)
                    for n in range(4):
                        last = nc.tensor.matmul(ps[b][:, n * NK:(n + 1) * NK], q_t[:, b * 4 + n, i * P:(i + 1) * P], keys[:, b * 4 + n, :], start=True, stop=True)
                    last.then_inc(scored, 1)

        @block.scalar
        def _(act):
            for i in range(TT):
                if i:
                    act.wait_ge(searched, i)
                for b in range(4):
                    act.wait_ge(scored, i * 4 + b + 1)
                    nc.scalar.activation(sc[:, b * 4:b * 4 + 4, :], ps[b][:, :].rearrange("p (n k) -> p n k", n=4), ACT.Copy).then_inc(copied, 1)
                act.wait_ge(shifted, i + 1)
                nc.scalar.activation(ex[:, :, :], ex[:, :, :], ACT.Exp).then_inc(expd, 1)

        @block.vector
        def _(dve):
            then = Chain(dve, step)

            def top16(n, scores, rest, values, index, done=None):
                for r in range(n):
                    last = nc.vector.max(values(r, 0), scores(r))
                then(last)
                for r in range(n):
                    nc.vector.max_index(index(r, 0), values(r, 0), scores(r))
                    last = nc.vector.match_replace(rest(r), values(r, 0), scores(r), -3.0e38)
                then(last) if done is None else last.then_inc(done, 1)
                if done is not None:
                    dve.wait_ge(done, i + 1)
                for r in range(n):
                    last = nc.vector.max(values(r, 1), rest(r))
                then(last)
                for r in range(n):
                    last = nc.vector.max_index(index(r, 1), values(r, 1), rest(r))
                then(last)

            for i in range(TT):
                dve.wait_ge(copied, 4 * i + 4)
                top16(N2, lambda r: sc[:, r, :], lambda r: sc2[:, r, :], lambda r, k: vv[:, r, 8 * k:8 * k + 8],
                      lambda r, k: ii[:, r, 8 * k:8 * k + 8], searched)
                pair = lambda ap, k: ap[:, :, :].rearrange("p (h two) k -> p h two k", two=2)[:, :, k, :]
                nc.vector.tensor_copy(fi[:, :, :], ii[:, :, :])
                then(nc.vector.tensor_tensor(cd[:, :, :].rearrange("p h (i j) -> p h i j", i=16),
                                             pair(vv, 0).unsqueeze(3).to_broadcast([P, PH, 16, 16]),
                                             pair(vv, 1).unsqueeze(2).to_broadcast([P, PH, 16, 16]), ALU.add))
                top16(PH, lambda r: cd[:, r, :], lambda r: cd2[:, r, :], lambda r, k: ts[:, r, 8 * k:8 * k + 8],
                      lambda r, k: tp[:, r, 8 * k:8 * k + 8])
                flat = tp[:, :, :].rearrange("p h k -> p (h k)")
                nc.vector.tensor_tensor(ex[:, :, :], ts[:, :, :], ts[:, :, 0:1].to_broadcast([P, PH, TOPK]), ALU.subtract).then_inc(shifted, 1)
                nc.vector.tensor_scalar(hl[:, 0, :], flat, 4, None, ALU.logical_shift_right)
                then(nc.vector.tensor_scalar(hl[:, 1, :], flat, 15, None, ALU.bitwise_and))
                then(nc.vector.tensor_copy(hf[:, :, :], hl[:, :, :]))
                for k in range(2):
                    e3 = eq[:, :, :, :].rearrange("p h k i -> p (h k) i")
                    then(nc.vector.tensor_tensor(e3, hf[:, k, :].unsqueeze(2).to_broadcast([P, SLOTS, 16]),
                                                 core.c[:, C_IOTA:C_IOTA + 16].unsqueeze(1).to_broadcast([P, SLOTS, 16]), ALU.is_equal))
                    then(nc.vector.tensor_tensor(eq[:, :, :, :], eq[:, :, :, :], pair(fi, k).unsqueeze(2).to_broadcast([P, PH, 16, 16]), ALU.mult))
                    then(nc.vector.tensor_reduce(pick[:, k, :], e3, AX.X, ALU.add))
                then(nc.vector.scalar_tensor_tensor(pick[:, 2, :], pick[:, 0, :], float(NK), pick[:, 1, :], ALU.mult, ALU.add))
                nc.vector.tensor_copy(ids[:, i, :], pick[:, 2, :])
                dve.wait_ge(expd, i + 1)
                then(nc.vector.tensor_reduce(den[:, 0, :], ex[:, :, :], AX.X, ALU.add))
                then(nc.vector.reciprocal(den[:, 1, :], den[:, 0, :]))
                then(nc.vector.tensor_tensor(gate[:, i, :].rearrange("p (h k) -> p h k", h=PH), ex[:, :, :],
                                             den[:, 1, :].unsqueeze(2).to_broadcast([P, PH, TOPK]), ALU.mult))


RING = 8
ROUNDS = SLOTS // (2 * RING)


def stage_experts(nc, core, xn, gain, ids, gate, u_emb, v_emb, out):
    sem = lambda n: nc.alloc_semaphore(f"ex_{n}")
    two = lambda n: [sem(f"{n}{i}") for i in range(2)]
    staged, u_in, v_in, dotted, gelud, weighed, spread, mixed = map(
        two, ("staged", "u_loaded", "v_loaded", "dotted", "gelud", "weighed", "spread", "mixed"))
    gained, zeroed, opened, closed, copied, stored, gloaded, passed = map(sem, (
        "gained", "zeroed", "opened", "closed", "copied", "stored", "gain_loaded", "wait_passed"))
    ident = core.c[:, C_IDENT:C_IDENT + P]
    with ExitStack() as ctx:
        ur = [[sb(nc, ctx, f"ex_u{b}_{r}", [P, D]) for r in range(RING)] for b in range(2)]
        vr = [[sb(nc, ctx, f"ex_v{b}_{r}", [P, D]) for r in range(RING)] for b in range(2)]
        stg = [[sb(nc, ctx, f"ex_stage{b}_{s}", [P, RING], U32) for s in "uv"] for b in range(2)]
        dot, gel, wgt = ([sb(nc, ctx, f"ex_{n}{b}", [P, RING]) for b in range(2)] for n in ("dot", "gel", "wgt"))
        diag = [sb(nc, ctx, f"ex_diag{b}", [P, RING, P]) for b in range(2)]
        gb = sb(nc, ctx, "ex_gain", [P, D])
        zero = sb(nc, ctx, "ex_zero", [P, P])
        ob = sb(nc, ctx, "ex_out", [P, D])
        acc = [[ctx.enter_context(nc.psum_tensor(f"ex_acc{b}{i}", [P, 512], F32)) for i in range(2)] for b in range(2)]
        block = ctx.enter_context(nc.Block())
        at = lambda tile, i: tile * ROUNDS + i

        @block.sync
        def _(sp):
            sp.dma_start(gb[:, :], gain.partition_broadcast(P)).then_inc(gloaded, 16)
            for tile in range(TT):
                sp.wait_ge(copied, tile + 1)
                sp.dma_start(out[tile * P:(tile + 1) * P, :], ob[:, :]).then_inc(stored, 16)
            sp.wait_ge(stored, 16 * TT)

        @block.gpsimd
        def _(pool):
            for tile in range(TT):
                with pool.Fori(0, ROUNDS) as i:
                    for b in range(2):
                        for s, (free, rows, table, loaded) in enumerate(((dotted, ur, u_emb, u_in), (mixed, vr, v_emb, v_in))):
                            pool.wait_ge(free[b], at(tile, i) + 1)
                            pool.sem_inc(passed, 1)
                            nc.gpsimd.tensor_copy(stg[b][s][:, :], ids[:, tile, bass.ds(i * 2 * RING + b * RING, RING)]).then_inc(staged[b], 1)
                            pool.wait_ge(staged[b], at(tile, i) * 2 + s + 1)
                            pool.sem_inc(passed, 1)
                            for r in range(RING):
                                nc.gpsimd.indirect_dma_start(out=rows[b][r][:, :], out_offset=None, in_=table,
                                                             in_offset=bass.IndirectOffsetOnAxis(ap=stg[b][s][:, r:r + 1], axis=0)).then_inc(loaded[b], 16)

        @block.vector
        def _(dve):
            for b in range(2):
                dve.sem_inc(dotted[b], 1)
            nc.vector.memset(zero[:, :], 0.0).then_inc(zeroed, 1)
            dve.wait_ge(gloaded, 16)
            for tile in range(TT):
                last = nc.vector.tensor_tensor(xn[:, tile, :], xn[:, tile, :], gb[:, :], ALU.mult)
            last.then_inc(gained, 1)
            dve.wait_ge(gained, 1)
            for tile in range(TT):
                with dve.Fori(0, ROUNDS) as i:
                    for b in range(2):
                        dve.wait_ge(u_in[b], (at(tile, i) + 1) * 16 * RING)
                        for r in range(RING):
                            last = nc.vector.tensor_tensor_reduce(ur[b][r][:, :], ur[b][r][:, :], xn[:, tile, :], 1.0, 0.0,
                                                                  ALU.mult, ALU.add, dot[b][:, r:r + 1])
                        last.then_inc(dotted[b], 1)
                        dve.wait_ge(gelud[b], at(tile, i) + 1)
                        nc.vector.tensor_tensor(wgt[b][:, :], gel[b][:, :], gate[:, tile, bass.ds(i * 2 * RING + b * RING, RING)],
                                                ALU.mult).then_inc(weighed[b], 1)

        @block.scalar
        def _(act):
            for tile in range(TT):
                with act.Fori(0, ROUNDS) as i:
                    for b in range(2):
                        act.wait_ge(dotted[b], at(tile, i) + 2)
                        nc.scalar.activation(gel[b][:, :], dot[b][:, :], ACT.Gelu).then_inc(gelud[b], 1)
                        act.wait_ge(weighed[b], at(tile, i) + 1)
                        act.wait_ge(mixed[b], at(tile, i) + 1)
                        for r in range(RING):
                            last = nc.scalar.activation(diag[b][:, r, :], ident, ACT.Copy, scale=wgt[b][:, r:r + 1])
                        last.then_inc(spread[b], 1)
                act.wait_ge(closed, tile + 1)
                if tile:
                    act.wait_ge(stored, 16 * tile)
                for half in range(2):
                    last = nc.scalar.activation(ob[:, half * 512:(half + 1) * 512], acc[tile % 2][half][:, :], ACT.Copy)
                last.then_inc(copied, 1)

        @block.tensor
        def _(pe):
            for b in range(2):
                pe.sem_inc(mixed[b], 1)
            pe.wait_ge(zeroed, 1)
            for tile in range(TT):
                if tile >= 2:
                    pe.wait_ge(copied, tile - 1)
                for half in range(2):
                    nc.tensor.matmul(acc[tile % 2][half][:, :], ident, core.x[:, tile, half * 512:(half + 1) * 512], start=True, stop=False,
                                     skip_group_check=True)
                with pe.Fori(0, ROUNDS) as i:
                    for b in range(2):
                        pe.wait_ge(v_in[b], (at(tile, i) + 1) * 16 * RING)
                        pe.wait_ge(spread[b], at(tile, i) + 1)
                        for r in range(RING):
                            for half in range(2):
                                last = nc.tensor.matmul(acc[tile % 2][half][:, :], diag[b][:, r, :], vr[b][r][:, half * 512:(half + 1) * 512],
                                                        start=False, stop=False, skip_group_check=True)
                        last.then_inc(mixed[b], 1)
                for half in range(2):
                    last = nc.tensor.matmul(acc[tile % 2][half][:, :], zero[:, :], core.x[:, tile, half * 512:(half + 1) * 512],
                                            start=False, stop=True, skip_group_check=True)
                last.then_inc(closed, 1)


def peer(nc, core, a, out):
    with ExitStack() as ctx:
        xn = sb(nc, ctx, "xn", [P, TT, D])
        ids = sb(nc, ctx, "expert_ids", [P, TT, SLOTS], U32)
        gate = sb(nc, ctx, "expert_gates", [P, TT, SLOTS])
        with ExitStack() as c2:
            h = sb(nc, c2, "h3_t", [P, KD, T])
            q_t = sb(nc, c2, "query_t", [P, 2 * PH, T])
            keys = sb(nc, c2, "keys", [P, 2 * PH, NK])
            loaded = nc.alloc_semaphore("keys_loaded")
            with nc.Block() as block:
                @block.sync
                def _(sp):
                    sp.dma_start(keys[:, :, :], a["keys"]).then_inc(loaded, 16)
                    sp.wait_ge(loaded, 16)
            stage_norm(nc, core, "nf", x_tiles(core), V_NORMF, h, natural=lambda i: xn[:, i, :])
            stage_proj_t(nc, core, "pp", h, T, a["peer_query"], 0, 4, q_t, [(0, T)])
            stage_topk(nc, core, q_t, keys, ids, gate)
        stage_experts(nc, core, xn, a["norm_ffn_2"], ids, gate, a["peer_u"], a["peer_v"], out)


def build(nc, a, scratch, out):
    with ExitStack() as stack:
        core = open_core(nc, stack, a)
        stage_load(nc, core, a)
        for part in (lambda: first_block(nc, core, a, scratch), lambda: mixers(nc, core, a), lambda: peer(nc, core, a, out)):
            before = nc.snapshot_sems()
            part()
            nc.clear_and_free_semaphores(nc.allocated_since(before))
            nc.all_engine_barrier()


def _columns(v):
    return np.reshape(v, (KD, P)).T


def _layout(i):
    consts, rows = shape_constants()
    v = np.zeros((P, V_WIDTH), np.float32)
    for name, at in (("a_norm", V_ANORM), ("kv_norm", V_KVNORM), ("b_norm", V_BNORM), ("norm_mix_2", V_NORM2), ("norm_ffn_2", V_NORMF)):
        v[:, at:at + KD] = _columns(i[name])
    for name, at in (("b_q_gain", V_QGK), ("k_gain", V_QGK + 1), ("f_q_norm_2", V_FQK), ("f_k_norm_2", V_FQK + 1)):
        v[0:HD, at] = v[HD:P, at] = np.reshape(i[name], HD)
    v[32:32 + HA, V_ALOG] = i["a_A_log"][0]
    v[32:32 + HA, V_DT] = i["a_dt_bias"][0]
    v[0:HM, V_BI] = i["b_igate_2"][0]
    v[32:32 + HM, V_BI] = i["b_fgate_m_2"][0]
    v[64:64 + HF, V_BI] = i["b_fgate_f_2"][0]
    taps = lambda w: np.transpose(np.reshape(w, (4, -1, P)), (2, 1, 0))
    return {
        "c128": consts, "c32": rows, "v128": v, "x": i["x"][0], "meta": i["meta_tokens_2"],
        "a_w_in": i["a_w_in"][0], "a_conv": taps(i["a_conv"][0]), "a_o_gain": i["a_o_gain"][0], "a_w_out": i["a_w_out"][0],
        "w_kv": i["w_kv"], "rel_bias": i["rel_bias"], "b_w_in": i["b_w_in"][0], "b_sinks": i["b_sinks"][0], "b_w_out": i["b_w_out"][0],
        "w_in_2": i["w_in_2"][0], "conv_qk_2": taps(i["conv_qk_2"][0]), "m_out_norm_2": i["m_out_norm_2"][0], "w_out_2": i["w_out_2"][0],
        "norm_ffn_2": i["norm_ffn_2"][0], "peer_query": i["peer_query_2"][0],
        "keys": np.transpose(np.reshape(i["peer_sub_keys_2"][0], (2 * PH, NK, P)), (2, 0, 1)),
        "peer_u": i["peer_u_2"][0], "peer_v": i["peer_v_2"][0],
    }


def kernel(**inputs):
    import concourse.bacc as bacc
    from concourse.bass_utils import run_bass_kernel_spmd

    nc = bacc.Bacc("TRN2", target_bir_lowering=False, num_devices=1)
    arrays, a = {}, {}
    for name, value in _layout({k: np.asarray(v) for k, v in inputs.items()}).items():
        arrays[f"in_{name}"] = np.ascontiguousarray(value)
        a[name] = nc.dram_tensor(f"in_{name}", value.shape, F32, kind="ExternalInput").ap()
    scratch = nc.dram_tensor("bias_rows", (HB, 384), F32, kind="Internal").ap()
    out = nc.dram_tensor("out_0", (T, D), F32, kind="ExternalOutput").ap()
    build(nc, a, scratch, out)
    r = run_bass_kernel_spmd(nc, [arrays], core_ids=[0])
    return r.results[0]["out_0"].reshape(1, T, D)
```

```python
from contextlib import ExitStack

import numpy as np

import concourse.bass as bass
from concourse import mybir

F32 = mybir.dt.float32
U32 = mybir.dt.uint32
F32R = mybir.dt.float32r
ACT = mybir.ActivationFunctionType
ALU = mybir.AluOpType
AX = mybir.AxisListType

P = 128
D = 1024
KD = D // P
T = 512
TT = T // P
EPS = 1e-6
NEG = -1e30

HA, DK, DV = 8, 128, 256
QKV_TILES = (2 * HA * DK + HA * DV) // P
HB, KVB, HD = 32, 4, 64
META = 16
T2 = T + META
HM, DM = 4, 128
HF, DF = 8, 64
PH, NK, TOPK = 8, 128, 16
SLOTS = PH * TOPK

C_IDENT, C_ONES, C_HALVES, C_LE, C_LEVEL = 0, 128, 256, 384, 512
LEVELS = 7
C_NEGDIAG = C_LEVEL + LEVELS * P
C_PAIR = C_NEGDIAG + P
C_IOTA = C_PAIR + 2
C_MHALF = C_IOTA + 16
C_FLIP = C_MHALF + 1
C_WIDTH = C_FLIP + P
R_SEL, R_BUCKET, R_WINDOW = 0, 8 * P, 8 * P + 384
R_WIDTH = R_WINDOW + 384
R_KEPT = R_BUCKET
(V_ANORM, V_KVNORM, V_BNORM, V_NORM2, V_NORMF) = (0, 8, 16, 24, 32)
V_QGK = 40
V_FQK = 42
V_ALOG, V_DT, V_BI = 44, 45, 46
V_WIDTH = 47


def shape_constants():
    c = np.zeros((P, C_WIDTH), np.float32)
    s, t = np.arange(P)[:, None], np.arange(P)[None, :]
    c[:, C_IDENT:C_IDENT + P] = s == t
    c[:, C_ONES:C_ONES + P] = 1
    c[:, C_HALVES:C_HALVES + P] = s // 64 == t // 64
    c[:, C_LE:C_LE + P] = s <= t
    for n in range(LEVELS):
        b = 1 << n
        c[:, C_LEVEL + n * P:C_LEVEL + (n + 1) * P] = (s // (2 * b) == t // (2 * b)) & (s % (2 * b) < b) & (t % (2 * b) >= b)
    c[:, C_NEGDIAG:C_NEGDIAG + P] = np.where(t <= s, 0, NEG)
    c[:, C_PAIR:C_PAIR + 2] = s // 64 == np.arange(2)[None, :]
    c[:, C_IOTA:C_IOTA + 16] = np.arange(16)[None, :]
    c[:, C_MHALF] = -0.5
    c[:, C_FLIP:C_FLIP + P] = s + t == P - 1
    r = np.zeros((32, R_WIDTH), np.float32)
    for h in range(8):
        r[h, R_SEL + h * P:R_SEL + (h + 1) * P] = 1
    dist = 255 - np.arange(384)
    n = np.maximum(dist, 0)
    large = 16 + (np.log(np.maximum(n, 1) / 16) / np.log(128 / 16) * 16).astype(np.int64)
    bucket = np.where(n < 16, n, np.minimum(large, 31))
    r[:, R_BUCKET:R_BUCKET + 384] = np.arange(32)[:, None] == bucket[None, :]
    r[:, R_WINDOW:R_WINDOW + 384] = np.where((dist >= 0) & (dist < 128), 0, NEG)
    return c, r


class Chain:

    def __init__(self, eng, sem, base=0):
        self.eng, self.sem, self.base, self.n = eng, sem, base, 0

    def __call__(self, ins):
        ins.then_inc(self.sem, 1)
        self.n += 1
        self.eng.wait_ge(self.sem, self.base + self.n)


class Core:

    def __init__(self, nc, stack):
        self.nc, self.stack = nc, stack

    def keep(self, name, shape, dt=F32):
        return self.stack.enter_context(self.nc.sbuf_tensor(name, shape, dt))


def sb(nc, ctx, name, shape, dt=F32, side=None):
    return ctx.enter_context(nc.sbuf_tensor(name, shape, dt, side=side))


def sb_parts(nc, ctx, name, shape, side=None):
    return [sb(nc, ctx, f"{name}_{part}", shape, F32R, side) for part in ("hi", "lo")]


def matmul_parts(nc, out, lhs, rhs, start, stop):
    nc.tensor.matmul(out, lhs[0], rhs[0], start=start, stop=False)
    nc.tensor.matmul(out, lhs[0], rhs[1], start=False, stop=False)
    return nc.tensor.matmul(out, lhs[1], rhs[0], start=False, stop=stop)


def banks(nc, ctx, name, n):
    return [ctx.enter_context(nc.psum_tensor(f"{name}{i}", [P, 512], F32)) for i in range(n)]


def stage_load(nc, core, a):
    loaded = nc.alloc_semaphore("loaded")
    with nc.Block() as block:
        @block.sync
        def _(sp):
            sp.dma_start(core.c[:, :], a["c128"]).then_inc(loaded, 16)
            sp.dma_start(core.r[:, :], a["c32"][:, 0:R_KEPT]).then_inc(loaded, 16)
            sp.dma_start(core.v[:, :], a["v128"]).then_inc(loaded, 16)
            sp.dma_start(core.x[:, :, :], a["x"].rearrange("(i p) d -> p i d", p=P)).then_inc(loaded, 16)
            sp.dma_start(core.ta[:, :, :], a["a_conv"]).then_inc(loaded, 16)
            sp.dma_start(core.tm[:, :, :], a["conv_qk_2"]).then_inc(loaded, 16)
            core.ring.first(sp)
            sp.wait_ge(loaded, 96)

        @block.vector
        def _(dve):
            nc.vector.memset(core.eps[:, 0:1], EPS)
            nc.vector.memset(core.eps[:, 1:2], 64 * EPS)


def stage_norm(nc, core, tag, tiles, gain, h_t, natural=None, whole=None):
    sem = lambda n: nc.alloc_semaphore(f"{tag}_{n}")
    squared, meaned, rooted, scaled, turned, stored, hi_ready, split = map(sem, (
        "squared", "meaned", "rooted", "scaled", "turned", "stored", "hi_ready", "split"))
    ident = core.c[:, C_IDENT:C_IDENT + P]
    n = len(tiles)
    with ExitStack() as ctx:
        junk = sb(nc, ctx, f"{tag}_junk", [P, D])
        ss = sb(nc, ctx, f"{tag}_ss", [P, 3, n])
        xn = sb(nc, ctx, f"{tag}_xn", [P, 2, D]) if natural is None else None
        ring = sb(nc, ctx, f"{tag}_full", [P, 2, 4 * P]) if whole is None else None
        ps = banks(nc, ctx, f"{tag}_ps", 4)
        block = ctx.enter_context(nc.Block())

        def full(b):
            rows, col = tiles[b // 2][1:]
            if whole is not None:
                return whole[:, 4 * (b % 2):4 * (b % 2) + 4, col:col + rows]
            return ring[:, b % 2, 0:4 * rows].rearrange("p (k t) -> p k t", k=4)
        where = [natural(i) if natural else xn[0:tiles[i][1], i % 2, :] for i in range(n)]

        @block.scalar
        def _(act):
            for i, (x, rows, _c) in enumerate(tiles):
                if i:
                    act.wait_ge(squared, i)
                nc.scalar.activation(junk[0:rows, :], x, ACT.Square, accum_out=ss[0:rows, 0, i:i + 1]).then_inc(squared, 1)
            def hi_part(b):
                if h_t is None:
                    return
                rows, col = tiles[b // 2][1:]
                act.wait_ge(stored, b + 1)
                nc.scalar.activation(h_t[0][:, 4 * (b % 2):4 * (b % 2) + 4, col:col + rows],
                                     full(b), ACT.Copy).then_inc(hi_ready, 1)

            for i, (x, rows, _c) in enumerate(tiles):
                act.wait_ge(rooted, i + 1)
                if natural is None and i >= 2:
                    act.wait_ge(turned, 2 * (i - 1))
                nc.scalar.activation(where[i], x, ACT.Copy, scale=ss[0:rows, 2, i:i + 1]).then_inc(scaled, 1)
                if i:
                    hi_part(2 * i - 2)
                    hi_part(2 * i - 1)
            hi_part(2 * n - 2)
            hi_part(2 * n - 1)

        @block.gpsimd
        def _(pool):
            for i, (x, rows, _c) in enumerate(tiles):
                pool.wait_ge(meaned, i + 1)
                nc.gpsimd.tensor_tensor(ss[0:rows, 2, i:i + 1], ss[0:rows, 1, i:i + 1],
                                        core.c[0:rows, C_MHALF:C_MHALF + 1], ALU.pow).then_inc(rooted, 1)

        @block.tensor
        def _(pe):
            for i, (x, rows, _c) in enumerate(tiles):
                pe.wait_ge(scaled, i + 1)
                for half in range(2):
                    b = 2 * i + half
                    if b >= 4:
                        pe.wait_ge(stored, b - 3)
                    for k in range(4):
                        d = (4 * half + k) * P
                        last = nc.tensor.transpose(ps[b % 4][:, k * rows:(k + 1) * rows], where[i][:, d:d + P], ident[0:rows, 0:rows])
                    last.then_inc(turned, 1)

        @block.vector
        def _(dve):
            for i, (x, rows, _c) in enumerate(tiles):
                dve.wait_ge(squared, i + 1)
                nc.vector.tensor_scalar(ss[0:rows, 1, i:i + 1], ss[0:rows, 0, i:i + 1], 1.0 / D, EPS, ALU.mult, ALU.add).then_inc(meaned, 1)
            def lo_part(b):
                if h_t is None:
                    return
                rows, col = tiles[b // 2][1:]
                where = (slice(None), slice(4 * (b % 2), 4 * (b % 2) + 4), slice(col, col + rows))
                dve.wait_ge(hi_ready, b + 1)
                nc.vector.tensor_tensor(h_t[1][where], full(b),
                                        h_t[0][where].bitcast(F32), ALU.subtract).then_inc(split, 1)

            for b in range(2 * n):
                rows = tiles[b // 2][1]
                k0 = 4 * (b % 2)
                dve.wait_ge(turned, b + 1)
                if b >= 2 and whole is None:
                    dve.wait_ge(split, b - 1)
                nc.vector.tensor_tensor(full(b),
                                        ps[b % 4][:, 0:4 * rows].rearrange("p (k t) -> p k t", k=4),
                                        core.v[:, gain + k0:gain + k0 + 4].unsqueeze(2).to_broadcast([P, 4, rows]),
                                        ALU.mult).then_inc(stored, 1)
                if b:
                    lo_part(b - 1)
            lo_part(2 * n - 1)


def x_tiles(core):
    return [(core.x[:, i, :], P, i * P) for i in range(TT)]


def w_view(w, kt):
    return w.rearrange("(k p) n -> p k n", p=P)


class Weights:

    def __init__(self, w, kt, n0=None, chunks=None, groups=None):
        self.view, self.n0, self.groups, self.parts = w_view(w, kt), n0, groups, kt // 4
        self.k, self.n = (KD, 256) if groups is None else (4, 512)
        self.chunks = chunks if groups is None else len(groups) * self.parts

    def source(self, c):
        if self.groups is None:
            return self.view[:, :, bass.ds(self.n0 + 256 * c, 256)]
        group, part = divmod(c, self.parts)
        return self.view[:, 4 * part:4 * part + 4, self.groups[group]:self.groups[group] + 512]

    def shaped(self, chunk):
        return chunk[:, :].rearrange("p (k n) -> p k n", k=self.k)


class Ring:

    def __init__(self, nc, core, plan):
        self.raw = [core.keep(f"weights_raw{b}", [P, 2048]) for b in range(2)]
        self.loaded = [nc.alloc_semaphore(f"weights_loaded{b}") for b in range(2)]
        self.plan, self.at, self.filled = plan, -1, 0

    def order(self, sp, w, c, b):
        sp.dma_start(w.shaped(self.raw[b]), w.source(c)).then_inc(self.loaded[b], 16)

    def first(self, sp):
        for b in range(2):
            self.order(sp, self.plan[0], b, b)

    def take(self):
        if self.at >= 0:
            self.filled += self.plan[self.at].chunks // 2
        self.at += 1
        return self.plan[self.at]


class Split:

    def __init__(self, nc, core, ctx, tag):
        self.nc, self.ring, self.w = nc, core.ring, core.ring.take()
        self.base = self.ring.filled
        self.after = self.ring.plan[self.ring.at + 1] if self.ring.at + 1 < len(self.ring.plan) else None
        self.hi, self.lo = ([sb(nc, ctx, f"{tag}_w_{part}{b}", [P, 2048], F32R) for b in range(2)] for part in ("hi", "lo"))
        self.hi_ready, self.ready = nc.alloc_semaphore(f"{tag}_w_hi"), nc.alloc_semaphore(f"{tag}_w_split")

    def parts(self, b):
        return self.w.shaped(self.hi[b]), self.w.shaped(self.lo[b])

    def loads(self, sp):
        w = self.w
        if w.groups is None and w.chunks > 2:
            with sp.Fori(1, w.chunks // 2) as i:
                for b in range(2):
                    sp.wait_ge(self.ready, 2 * i + b - 1)
                    self.ring.order(sp, w, 2 * i + b, b)
        else:
            for c in range(2, w.chunks):
                sp.wait_ge(self.ready, c - 1)
                self.ring.order(sp, w, c, c % 2)
        if self.after is not None:
            for b in range(2):
                sp.wait_ge(self.ready, w.chunks - 1 + b)
                self.ring.order(sp, self.after, b, b)

    def split_hi(self, eng, i, b):
        eng.wait_ge(self.ring.loaded[b], 16 * (self.base + i) + 16)
        if eng is self.nc.scalar:
            self.nc.scalar.activation(self.hi[b][:, :], self.ring.raw[b][:, :], ACT.Copy).then_inc(self.hi_ready, 1)
        else:
            self.nc.vector.tensor_copy(self.hi[b][:, :], self.ring.raw[b][:, :]).then_inc(self.hi_ready, 1)

    def split_lo(self, pool):
        with pool.Fori(0, self.w.chunks // 2) as i:
            for b in range(2):
                pool.wait_ge(self.hi_ready, 2 * i + b + 1)
                self.nc.gpsimd.tensor_tensor(self.lo[b][:, :], self.ring.raw[b][:, :], self.hi[b][:, :].bitcast(F32),
                                             ALU.subtract).then_inc(self.ready, 1)


def products_t(nc, pe, split, h_t, spans, ps, done, free):
    ns = len(spans)
    with pe.Fori(0, split.w.chunks // 2) as i:
        for b in range(2):
            pe.wait_ge(split.ready, 2 * i + b + 1)
            hi, lo = split.parts(b)
            for j in range(2):
                for si, (c0, cw) in enumerate(spans):
                    u = (b * 2 + j) * ns + si
                    pe.wait_ge(free, i * 4 * ns + u + 1)
                    for k in range(KD):
                        last = matmul_parts(nc, ps[u % 4][:, 0:cw], (hi[:, k, j * P:(j + 1) * P], lo[:, k, j * P:(j + 1) * P]),
                                            (h_t[0][:, k, c0:c0 + cw], h_t[1][:, k, c0:c0 + cw]), k == 0, k == KD - 1)
                    last.then_inc(done, 1)


def stage_proj_t(nc, core, tag, h_t, out, spans):
    done, free = (nc.alloc_semaphore(f"{tag}_{n}") for n in ("product", "bank_free"))
    ns = len(spans)
    with ExitStack() as ctx:
        split = Split(nc, core, ctx, tag)
        pairs = split.w.chunks // 2
        ps = banks(nc, ctx, f"{tag}_ps", 4)
        block = ctx.enter_context(nc.Block())

        @block.sync
        def _(sp):
            split.loads(sp)

        @block.gpsimd
        def _(pool):
            split.split_lo(pool)

        @block.tensor
        def _(pe):
            products_t(nc, pe, split, h_t, spans, ps, done, free)

        @block.vector
        def _(dve):
            for b in range(2):
                split.split_hi(dve, 0, b)
            if pairs > 1:
                with dve.Fori(1, pairs) as i:
                    for b in range(2):
                        dve.wait_ge(done, i * 4 * ns + (b - 1) * 2 * ns)
                        split.split_hi(dve, i, b)

        @block.scalar
        def _(act):
            act.sem_inc(free, 4)
            with act.Fori(0, pairs) as i:
                for j in range(4):
                    for si, (c0, cw) in enumerate(spans):
                        u = j * ns + si
                        act.wait_ge(done, i * 4 * ns + u + 1)
                        nc.scalar.activation(out[:, bass.ds(i * 4 + j, 1), c0:c0 + cw],
                                             ps[u % 4][:, 0:cw].unsqueeze(1), ACT.Copy).then_inc(free, 1)


def stage_proj_conv(nc, core, tag, h_t, taps, out, spans, width):
    done, free, conved, step, zeroed, activated = (
        nc.alloc_semaphore(f"{tag}_{n}") for n in ("product", "bank_free", "conved", "conv_step", "zeroed", "activated"))
    ns = len(spans)
    with ExitStack() as ctx:
        split = Split(nc, core, ctx, tag)
        pairs = split.w.chunks // 2
        xp = sb(nc, ctx, f"{tag}_xp", [P, 2, 3 + width])
        y = sb(nc, ctx, f"{tag}_y", [P, 2, width])
        ps = banks(nc, ctx, f"{tag}_ps", 4)
        block = ctx.enter_context(nc.Block())

        @block.sync
        def _(sp):
            split.loads(sp)

        @block.gpsimd
        def _(pool):
            split.split_lo(pool)

        @block.tensor
        def _(pe):
            products_t(nc, pe, split, h_t, spans, ps, done, free)

        @block.scalar
        def _(act):
            def tiles(i, last):
                for j in range(4):
                    for si, (c0, cw) in enumerate(spans):
                        u = j * ns + si
                        act.wait_ge(done, i * 4 * ns + u + 1)
                        if si == 0:
                            act.wait_ge(conved, i * 4 + j + 1)
                        nc.scalar.activation(xp[:, j % 2, 3 + c0:3 + c0 + cw], ps[u % 4][:, 0:cw], ACT.Copy).then_inc(free, 1)
                    if j % 2 and not last:
                        split.split_hi(act, i + 1, j // 2)
                    act.wait_ge(conved, i * 4 + j + 3)
                    nc.scalar.activation(out[:, bass.ds(i * 4 + j, 1), :], y[:, j % 2:j % 2 + 1, :], ACT.Silu).then_inc(activated, 1)

            act.sem_inc(free, 4)
            for b in range(2):
                split.split_hi(act, 0, b)
            act.wait_ge(zeroed, 1)
            if pairs > 1:
                with act.Fori(0, pairs - 1) as i:
                    tiles(i, False)
            tiles(pairs - 1, True)

        @block.vector
        def _(dve):
            dve.sem_inc(conved, 2)
            dve.sem_inc(activated, 2)
            nc.vector.memset(xp[:, :, 0:3], 0.0).then_inc(zeroed, 1)
            with dve.Fori(0, pairs) as i:
                for j in range(4):
                    tap = lambda k: taps[:, bass.ds(i * 4 + j, 1), k]
                    row, to = xp[:, j % 2, :], y[:, j % 2, :]
                    dve.wait_ge(free, 4 + i * 4 * ns + (j + 1) * ns)
                    dve.wait_ge(activated, i * 4 + j + 1)
                    nc.vector.tensor_scalar(to, row[:, 3:3 + width], tap(3), None, ALU.mult).then_inc(step, 1)
                    for k in range(3):
                        dve.wait_ge(step, i * 12 + j * 3 + k + 1)
                        last = nc.vector.scalar_tensor_tensor(to, row[:, k:k + width], tap(k), to, ALU.mult, ALU.add)
                        if k < 2:
                            last.then_inc(step, 1)
                    last.then_inc(conved, 1)


def stage_unit_rows(nc, core, tag, qk):
    squared, summed, rooted, inverted, scaled = (
        nc.alloc_semaphore(f"{tag}_{n}") for n in ("squared", "summed", "rooted", "inverted", "scaled"))
    with ExitStack() as ctx:
        sq = sb(nc, ctx, f"{tag}_sq", [P, 2, T])
        rt = sb(nc, ctx, f"{tag}_rt", [P, 2, T])
        iv = sb(nc, ctx, f"{tag}_iv", [P, 2, T])
        ps = banks(nc, ctx, f"{tag}_ps", 2)
        block = ctx.enter_context(nc.Block())
        tile = lambda i, b: qk[:, bass.ds(i + b * HA, 1), :]

        @block.scalar
        def _(act):
            with act.Fori(0, HA) as i:
                for b in range(2):
                    nc.scalar.activation(sq[:, b:b + 1, :], tile(i, b), ACT.Square).then_inc(squared, 1)
                for b in range(2):
                    act.wait_ge(summed, 2 * i + b + 1)
                    act.wait_ge(inverted, 2 * i + b + 1)
                    nc.scalar.activation(rt[:, b, :], ps[b][:, :], ACT.Sqrt, bias=core.eps[:, 0:1]).then_inc(rooted, 1)

        @block.tensor
        def _(pe):
            with pe.Fori(0, HA) as i:
                for b in range(2):
                    pe.wait_ge(squared, 2 * i + b + 1)
                    nc.tensor.matmul(ps[b][:, :], core.c[:, C_ONES:C_ONES + P], sq[:, b, :], start=True, stop=True).then_inc(summed, 1)

        @block.vector
        def _(dve):
            dve.sem_inc(inverted, 2)
            with dve.Fori(0, HA) as i:
                for b in range(2):
                    dve.wait_ge(rooted, 2 * i + b + 1)
                    nc.vector.reciprocal(iv[:, b, :], rt[:, b, :]).then_inc(inverted, 1)
                    dve.wait_ge(inverted, 2 * i + b + 3)
                    nc.vector.scalar_tensor_tensor(tile(i, b), tile(i, b), DK ** -0.5 if b == 0 else 1.0, iv[:, b:b + 1, :],
                                                   ALU.mult, ALU.mult).then_inc(scaled, 1)


GATE_COLS = 72


def split_small(nc, dve, w, parts, split):
    nc.vector.tensor_copy(parts[0][:, :, :], w[:, :, :]).then_inc(split, 1)
    dve.wait_ge(split, 1)
    nc.vector.tensor_tensor(parts[1][:, :, :], w[:, :, :], parts[0][:, :, :].bitcast(F32), ALU.subtract).then_inc(split, 1)


def stage_delta_gates(nc, core, h_t, w, rows, cols):
    sem = lambda n: nc.alloc_semaphore(f"dg_{n}")
    loaded, zeroed, product, vdone, adone, turned, split = map(sem, (
        "loaded", "zeroed", "product", "vector_step", "scalar_step", "turned", "weights_split"))
    with ExitStack() as ctx:
        wg = sb(nc, ctx, "dg_w", [P, KD, GATE_COLS])
        wp = sb_parts(nc, ctx, "dg_wp", [P, KD, GATE_COLS])
        t = sb(nc, ctx, "dg_t", [P, 4, T])
        more = sb(nc, ctx, "dg_more", [8, 2, T])
        ea = sb(nc, ctx, "dg_ea", [P, 1])
        ps = banks(nc, ctx, "dg_ps", 2)
        block = ctx.enter_context(nc.Block())
        wv = w_view(w, KD)
        ab = QKV_TILES * P + HA * DV
        A = slice(32, 40)

        @block.sync
        def _(sp):
            sp.wait_ge(zeroed, 1)
            sp.dma_start(wg[:, :, 0:8], wv[:, :, ab:ab + 8]).then_inc(loaded, 16)
            sp.dma_start(wg[:, :, 32:40], wv[:, :, ab + 8:ab + 16]).then_inc(loaded, 16)

        @block.tensor
        def _(pe):
            pe.wait_ge(split, 2)
            for k in range(KD):
                last = matmul_parts(nc, ps[0][0:GATE_COLS, :], (wp[0][:, k, :], wp[1][:, k, :]), (h_t[0][:, k, :], h_t[1][:, k, :]),
                                    k == 0, k == KD - 1)
            last.then_inc(product, 1)
            pe.wait_ge(vdone, 11)
            pe.wait_ge(adone, 6)
            for kind in range(4):
                src = rows[0:8, kind, :] if kind < 2 else more[:, kind - 2, :]
                for i in range(TT):
                    last = nc.tensor.transpose(ps[1][:, (kind * TT + i) * 8:(kind * TT + i) * 8 + 8],
                                               src[:, i * P:(i + 1) * P], core.c[0:8, C_IDENT:C_IDENT + 8])
            last.then_inc(turned, 1)

        @block.scalar
        def _(act):
            nc.scalar.activation(ea[A, :], core.v[A, V_ALOG:V_ALOG + 1], ACT.Exp).then_inc(adone, 1)
            act.wait_ge(vdone, 2)
            nc.scalar.activation(t[A, 1, :], t[A, 1, :], ACT.Exp, scale=-1.0).then_inc(adone, 1)
            act.wait_ge(adone, 2)
            nc.scalar.activation(t[A, 1, :], t[A, 1, :], ACT.Ln, bias=1.0).then_inc(adone, 1)
            act.wait_ge(vdone, 9)
            nc.scalar.activation(more[:, 0, :], rows[0:8, 0, :], ACT.Exp).then_inc(adone, 1)
            act.wait_ge(vdone, 10)
            nc.scalar.activation(more[:, 1, :], more[:, 1, :], ACT.Exp).then_inc(adone, 1)
            act.wait_ge(product, 1)
            nc.scalar.activation(rows[0:8, 1, :], ps[0][0:8, :], ACT.Sigmoid).then_inc(adone, 1)

        @block.vector
        def _(dve):
            nc.vector.memset(wg[:, :, :], 0.0).then_inc(zeroed, 1)
            dve.wait_ge(loaded, 32)
            split_small(nc, dve, wg, wp, split)
            then = Chain(dve, vdone)
            dve.wait_ge(product, 1)
            then(nc.vector.tensor_scalar(t[A, 0, :], ps[0][A, :], core.v[A, V_DT:V_DT + 1], None, ALU.add))
            then(nc.vector.scalar_tensor_tensor(t[A, 1, :], t[A, 0, :], -1.0, t[A, 0, :], ALU.mult, ALU.max))
            dve.wait_ge(adone, 3)
            then(nc.vector.scalar_tensor_tensor(t[A, 2, :], t[A, 0, :], 0.0, t[A, 1, :], ALU.max, ALU.add))
            then(nc.vector.tensor_scalar(t[A, 0, :], t[A, 2, :], ea[A, 0:1], -1.0, ALU.mult, ALU.mult))
            for i in range(TT):
                c = slice(i * P, (i + 1) * P)
                then(nc.vector.tensor_tensor_scan(t[A, 3, c], core.c[A, C_ONES:C_ONES + P], t[A, 0, c], 0.0, ALU.mult, ALU.add))
            then(nc.vector.tensor_copy(rows[0:8, 0, :], t[A, 3, :]))
            g = rows[0:8, 0, :].rearrange("p (i c) -> p i c", i=TT)
            then(nc.vector.tensor_tensor(more[:, 1, :].rearrange("p (i c) -> p i c", i=TT),
                                         g[:, :, P - 1:P].to_broadcast([8, TT, P]), g, ALU.subtract))
            dve.wait_ge(adone, 6)
            then(nc.vector.tensor_tensor(more[:, 0, :], more[:, 0, :], rows[0:8, 1, :], ALU.mult))
            dve.wait_ge(turned, 1)
            nc.vector.tensor_copy(cols[:, :, :, :], ps[1][:, 0:4 * TT * 8].rearrange("p (a i h) -> p a i h", a=4, i=TT))


def stage_delta_chunks(nc, core, qk_in, v, rows, cols, ss):
    sem = lambda n: nc.alloc_semaphore(f"dc_{n}")
    (rowcast, exp_g, decayed, gramed, masked, weighted, qk_ready, qdec_ready, level_ready, x_ready, x_copied, mx_ready, m_ready,
     turned, turn_copied, kdec_ready, t_scaled, w_ready, w_copied, vnew_ready, vnew_copied, out_ready, out_read, s_ready,
     step, adj_ready) = map(sem, (
        "rowcast", "exp_g", "decayed", "gramed", "masked", "weighted", "qk_ready", "qdec_ready", "level_ready", "x_ready", "x_copied",
        "mx_ready", "m_ready", "turned", "turn_copied", "kdec_ready", "t_scaled", "w_ready", "w_copied", "vnew_ready", "vnew_copied",
        "out_ready", "out_read", "s_ready", "step", "adjusted"))
    ident = core.c[:, C_IDENT:C_IDENT + P]
    q_t = lambda h: qk_in[:, h, :]
    k_t = lambda h: qk_in[:, HA + h, :]
    v_t = lambda h, j: v[:, 2 * h + j, :]
    o_h = lambda h: v[:, 2 * h:2 * h + 2, :].rearrange("p j (a d) -> p (j a) d", a=2)
    w4 = lambda ap: ap.rearrange("p (i c) -> p i c", i=TT)
    PAIRS = [(2 * p, 2 * p + 1) for p in range(HA // 2)]
    with ExitStack() as ctx:
        two = lambda name, n=T: [sb(nc, ctx, f"dc_{name}{j}", [P, n]) for j in range(2)]
        dec, at, em, m, mt, xs = two("dec"), two("at"), two("em"), two("m"), two("mt"), two("xs")
        lv = two("lv", 2 * T)
        tb, tbg, kn, kd, wt, qd, qk, eg = (two(n) for n in ("tb", "tbg", "kn", "kd", "wt", "qd", "qk", "eg"))
        vn, vnew, st, junk = two("vn", TT * DV), two("vnew", DV), two("st", DV), two("junk", DV)
        ba, bb, bc, bd = (banks(nc, ctx, f"dc_p{n}", 2) for n in "abcd")
        block = ctx.enter_context(nc.Block())

        @block.tensor
        def _(pe):
            def turn(h, n):
                j = h % 2
                if n == 0:
                    pe.wait_ge(qk_ready, h + 1)
                else:
                    pe.wait_ge(turn_copied, h // 2 * 6 + 2 * (n - 1) + j + 1)
                src = k_t(h) if n == 0 else v_t(h, n - 1)
                for i in range(TT):
                    last = nc.tensor.transpose(bd[j][:, i * P:(i + 1) * P], src[:, i * P:(i + 1) * P], ident)
                last.then_inc(turned, 1)

            for pair in PAIRS:
                for h in pair:
                    j = h % 2
                    if h >= 2:
                        pe.wait_ge(s_ready, 6 * (h // 2))
                        pe.wait_ge(vnew_copied, 8 * (h // 2))
                        pe.wait_ge(out_read, 8 * (h // 2))
                        pe.wait_ge(turn_copied, 6 * (h // 2))
                    sel = core.r[0:8, R_SEL + h * P:R_SEL + (h + 1) * P]
                    nc.tensor.matmul(ba[j][:, :], sel, rows[0:8, 0, :], start=True, stop=True)
                    nc.tensor.matmul(bb[j][:, :], sel, rows[0:8, 1, :], start=True, stop=True).then_inc(rowcast, 1)
                    for bank, rhs in ((bc, k_t(h)), (bd, q_t(h))):
                        for i in range(TT):
                            c = slice(i * P, (i + 1) * P)
                            last = nc.tensor.matmul(bank[j][:, c], k_t(h)[:, c], rhs[:, c], start=True, stop=True)
                    last.then_inc(gramed, 1)
                for n in range(LEVELS):
                    for h in pair:
                        j = h % 2
                        pe.wait_ge(level_ready, h // 2 * 2 * LEVELS + 2 * n + j + 1)
                        pe.wait_ge(m_ready, h // 2 * 2 * (LEVELS + 1) + 2 * n + j + 1)
                        if n == 0:
                            pe.wait_ge(exp_g, 2 * h + 2)
                            pe.wait_ge(decayed, h + 1)
                        for i in range(TT):
                            c = slice(i * P, (i + 1) * P)
                            last = nc.tensor.matmul(ba[j][:, c], lv[j][:, n % 2 * T + i * P:n % 2 * T + (i + 1) * P], m[j][:, c],
                                                    start=True, stop=True)
                        last.then_inc(x_ready, 1)
                    for h in pair:
                        j = h % 2
                        if n in (1, 3, 5):
                            turn(h, n // 2)
                        pe.wait_ge(x_copied, h // 2 * 2 * LEVELS + 2 * n + j + 1)
                        for i in range(TT):
                            c = slice(i * P, (i + 1) * P)
                            if n < LEVELS - 1:
                                nc.tensor.matmul(bb[j][:, c], mt[j][:, c], xs[j][:, c], start=True, stop=True)
                            last = nc.tensor.matmul(bc[j][:, c], xs[j][:, c], mt[j][:, c], start=True, stop=True)
                        last.then_inc(mx_ready, 1)
                for h in pair:
                    j = h % 2
                    pe.wait_ge(t_scaled, h + 1)
                    pe.wait_ge(turn_copied, h // 2 * 6 + 4 + j + 1)
                    for i in range(TT):
                        c = slice(i * P, (i + 1) * P)
                        last = nc.tensor.matmul(ba[j][:, c], kn[j][:, c], tbg[j][:, c], start=True, stop=True)
                    last.then_inc(w_ready, 1)
                for i in range(TT):
                    c = slice(i * P, (i + 1) * P)
                    for h in pair:
                        j = h % 2
                        if i:
                            pe.wait_ge(s_ready, h // 2 * 6 + (i - 1) * 2 + j + 1)
                        last = nc.tensor.matmul(bb[j][:, 0:DV], tb[j][:, c], vn[j][:, i * DV:(i + 1) * DV], start=True, stop=i == 0)
                        if i:
                            last = nc.tensor.matmul(bb[j][:, 0:DV], wt[j][:, c], st[j][:, :], start=False, stop=True)
                        last.then_inc(vnew_ready, 1)
                    for h in pair:
                        j = h % 2
                        pe.wait_ge(vnew_copied, h // 2 * 8 + 2 * i + j + 1)
                        if i:
                            pe.wait_ge(out_read, h // 2 * 8 + 2 * (i - 1) + j + 1)
                            nc.tensor.matmul(bc[j][:, 0:DV], qd[j][:, c], st[j][:, :], start=True, stop=False)
                        else:
                            pe.wait_ge(w_copied, h + 1)
                            pe.wait_ge(qdec_ready, h + 1)
                            pe.wait_ge(kdec_ready, h + 1)
                        last = nc.tensor.matmul(bc[j][:, 0:DV], qk[j][:, c], vnew[j][:, :], start=i == 0, stop=True)
                        if i < TT - 1:
                            last = nc.tensor.matmul(ba[j][:, 0:DV], kd[j][:, c], vnew[j][:, :], start=True, stop=True)
                        last.then_inc(out_ready, 1)

        @block.scalar
        def _(act):
            for pair in PAIRS:
                for h in pair:
                    j = h % 2
                    act.wait_ge(decayed, h + 1)
                    if h >= 2:
                        act.wait_ge(s_ready, 6 * (h // 2))
                    nc.scalar.activation(eg[j][:, :], ba[j][:, :], ACT.Exp).then_inc(exp_g, 1)
                    nc.scalar.activation(dec[j][:, :], dec[j][:, :], ACT.Exp).then_inc(exp_g, 1)
                for n in range(LEVELS):
                    for h in pair:
                        j = h % 2
                        act.wait_ge(x_ready, h // 2 * 2 * LEVELS + 2 * n + j + 1)
                        nc.scalar.activation(xs[j][:, :], ba[j][:, :], ACT.Copy).then_inc(x_copied, 1)
                    for h in pair:
                        j = h % 2
                        if n in (1, 3, 5):
                            act.wait_ge(turned, h // 2 * 6 + (n // 2) * 2 + j + 1)
                            dst = kn[j][:, :] if n == 1 else w4v(vn[j], DV)[:, :, (n // 2 - 1) * P:(n // 2) * P]
                            nc.scalar.activation(dst, bd[j][:, :] if n == 1 else w4(bd[j][:, :]), ACT.Copy).then_inc(turn_copied, 1)
                for h in pair:
                    j = h % 2
                    act.wait_ge(w_ready, h + 1)
                    nc.scalar.activation(wt[j][:, :], ba[j][:, :], ACT.Copy, scale=-1.0).then_inc(w_copied, 1)
                for i in range(TT):
                    for h in pair:
                        j = h % 2
                        act.wait_ge(vnew_ready, h // 2 * 8 + 2 * i + j + 1)
                        nc.scalar.activation(vnew[j][:, :], bb[j][:, 0:DV], ACT.Copy).then_inc(vnew_copied, 1)
                    for h in pair:
                        j = h % 2
                        act.wait_ge(out_ready, h // 2 * 8 + 2 * i + j + 1)
                        nc.scalar.activation(o_h(h)[:, i, :], bc[j][:, 0:DV], ACT.Copy)
                        nc.scalar.activation(junk[j][:, :], bc[j][:, 0:DV], ACT.Square, accum_out=ss[:, i, h:h + 1]).then_inc(out_read, 1)

        @block.gpsimd
        def _(pool):
            for pair in PAIRS:
                for h in pair:
                    j = h % 2
                    pool.wait_ge(exp_g, 2 * h + 2)
                    nc.gpsimd.tensor_tensor(w4(em[j][:, :]), w4(dec[j][:, :]),
                                            core.c[:, C_LE:C_LE + P].unsqueeze(1).to_broadcast([P, TT, P]), ALU.mult).then_inc(masked, 1)
                for n in range(LEVELS):
                    for h in pair:
                        j = h % 2
                        if n == 0:
                            pool.wait_ge(weighted, h + 1)
                        if n >= 2:
                            pool.wait_ge(x_ready, h // 2 * 2 * LEVELS + 2 * (n - 2) + j + 1)
                        elif h >= 2:
                            pool.wait_ge(x_ready, h // 2 * 2 * LEVELS)
                        lo = C_LEVEL + n * P
                        nc.gpsimd.tensor_tensor(w4(lv[j][:, n % 2 * T:n % 2 * T + T]), w4(at[j][:, :]),
                                                core.c[:, lo:lo + P].unsqueeze(1).to_broadcast([P, TT, P]), ALU.mult).then_inc(level_ready, 1)
                for h in pair:
                    j = h % 2
                    pool.wait_ge(turn_copied, h // 2 * 6 + j + 1)
                    if h >= 2:
                        pool.wait_ge(out_ready, 8 * (h // 2))
                    nc.gpsimd.tensor_tensor(w4(kd[j][:, :]), w4(kn[j][:, :]), cols[:, 3, :, h:h + 1].to_broadcast([P, TT, P]),
                                            ALU.mult).then_inc(kdec_ready, 1)

        @block.vector
        def _(dve):
            eye = ident.unsqueeze(1).to_broadcast([P, TT, P])
            for pair in PAIRS:
                for h in pair:
                    j = h % 2
                    dve.wait_ge(rowcast, h + 1)
                    if h >= 2:
                        dve.wait_ge(masked, h - 1)
                    for i in range(TT):
                        c = slice(i * P, (i + 1) * P)
                        last = nc.vector.tensor_scalar(dec[j][:, c], ba[j][:, c], cols[:, 0, i, h:h + 1], 0.0, ALU.subtract, ALU.min)
                    last.then_inc(decayed, 1)
                    nc.vector.tensor_copy(w4(m[j][:, :]), eye)
                    nc.vector.tensor_copy(w4(mt[j][:, :]), eye).then_inc(m_ready, 1)
                for h in pair:
                    j = h % 2
                    dve.wait_ge(gramed, h + 1)
                    dve.wait_ge(exp_g, 2 * h + 2)
                    nc.vector.tensor_tensor(at[j][:, :], bc[j][:, :], dec[j][:, :], ALU.mult).then_inc(step, 1)
                    dve.wait_ge(step, h + 1)
                    nc.vector.tensor_tensor(at[j][:, :], bb[j][:, :], at[j][:, :], ALU.mult).then_inc(weighted, 1)
                    dve.wait_ge(masked, h + 1)
                    nc.vector.tensor_tensor(qk[j][:, :], bd[j][:, :], em[j][:, :], ALU.mult).then_inc(qk_ready, 1)
                    nc.vector.tensor_tensor(qd[j][:, :], q_t(h), eg[j][:, :], ALU.mult).then_inc(qdec_ready, 1)
                for n in range(LEVELS):
                    for h in pair:
                        j = h % 2
                        dve.wait_ge(mx_ready, h // 2 * 2 * LEVELS + 2 * n + j + 1)
                        if n < LEVELS - 1:
                            nc.vector.tensor_tensor(m[j][:, :], m[j][:, :], bb[j][:, :], ALU.subtract)
                        nc.vector.tensor_tensor(mt[j][:, :], mt[j][:, :], bc[j][:, :], ALU.subtract).then_inc(m_ready, 1)
                for h in pair:
                    j = h % 2
                    dve.wait_ge(m_ready, h // 2 * 2 * (LEVELS + 1) + 2 * LEVELS + j + 1)
                    nc.vector.tensor_tensor(w4(tb[j][:, :]), w4(mt[j][:, :]), cols[:, 1, :, h:h + 1].to_broadcast([P, TT, P]), ALU.mult)
                    nc.vector.tensor_tensor(w4(tbg[j][:, :]), w4(mt[j][:, :]), cols[:, 2, :, h:h + 1].to_broadcast([P, TT, P]),
                                            ALU.mult).then_inc(t_scaled, 1)
                for i in range(TT - 1):
                    for h in pair:
                        j = h % 2
                        dve.wait_ge(out_ready, h // 2 * 8 + 2 * i + j + 1)
                        if i:
                            dve.wait_ge(s_ready, h // 2 * 6 + (i - 1) * 2 + j + 1)
                            last = nc.vector.scalar_tensor_tensor(st[j][:, :], st[j][:, :], eg[j][:, i * P + P - 1:i * P + P],
                                                                  ba[j][:, 0:DV], ALU.mult, ALU.add)
                        else:
                            last = nc.vector.tensor_copy(st[j][:, :], ba[j][:, 0:DV])
                        last.then_inc(s_ready, 1)


def w4v(buf, n):
    return buf[:, :].rearrange("p (i d) -> p i d", d=n)


def open_core(nc, stack, a):
    core = Core(nc, stack)
    core.c = core.keep("c128_sb", [P, C_WIDTH])
    core.r = core.keep("c32_sb", [32, R_KEPT])
    core.v = core.keep("v128_sb", [P, V_WIDTH])
    core.x = core.keep("x_sb", [P, TT, D])
    core.eps = core.keep("eps_sb", [P, 2])
    core.ta = core.keep("taps_a_sb", [P, QKV_TILES, 4])
    core.tm = core.keep("taps_m_sb", [P, 2 * HM, 4])
    core.ring = Ring(nc, core, weights_plan(a))
    return core


def products_n(nc, pe, w, split, h_t, tiles, ps, c, free, done, spent, finished=None, h_ready=None):
    group, part = divmod(c, w.parts)
    nt = len(tiles)
    pe.wait_ge(split.ready, c + 1)
    if h_ready is not None and group == 0:
        pe.wait_ge(h_ready, part + 1)
    hi, lo = split.parts(c % 2)
    for i, (rows, col) in enumerate(tiles):
        u = group * nt + i
        if part == 0:
            free(u)
        for k in range(4):
            kk = 4 * part + k
            last = matmul_parts(nc, ps[u % len(ps)][:, :], (h_t[0][:, kk, col:col + P], h_t[1][:, kk, col:col + P]),
                                (hi[:, k, :], lo[:, k, :]), kk == 0, kk == 4 * w.parts - 1)
        if part == w.parts - 1:
            last.then_inc(done, 1)
            if finished is not None:
                finished(u)
    if part < w.parts - 1:
        last.then_inc(spent, 1)


def wait_spent(eng, w, c, nt, done, spent):
    group, part = divmod(c, w.parts)
    if part == w.parts - 1:
        eng.wait_ge(done, (group + 1) * nt)
    else:
        eng.wait_ge(spent, group * (w.parts - 1) + part + 1)


def split_whole(nc, dve, whole, parts, n, hi_ready, split):
    for i in range(n):
        k = slice(4 * i, 4 * i + 4)
        nc.vector.tensor_copy(parts[0][:, k, :], whole[:, k, :]).then_inc(hi_ready, 1)
        dve.wait_ge(hi_ready, i + 1)
        nc.vector.tensor_tensor(parts[1][:, k, :], whole[:, k, :], parts[0][:, k, :].bitcast(F32), ALU.subtract).then_inc(split, 1)


def stage_proj_n(nc, core, tag, h_t, tiles, engine, emit, whole=None):
    product, taken, spent, h_hi, h_split = (nc.alloc_semaphore(f"{tag}_{n}") for n in ("product", "taken", "spent", "h_hi", "h_split"))
    nt = len(tiles)
    with ExitStack() as ctx:
        split = Split(nc, core, ctx, tag)
        w = split.w
        if whole is not None:
            h_t = sb_parts(nc, ctx, f"{tag}_h", [P, 4 * w.parts, T])
        ps = banks(nc, ctx, f"{tag}_ps", 8)
        block = ctx.enter_context(nc.Block())

        @block.sync
        def _(sp):
            split.loads(sp)

        @block.gpsimd
        def _(pool):
            split.split_lo(pool)

        @block.tensor
        def _(pe):
            def free(u):
                if u >= 8:
                    pe.wait_ge(taken, u - 7)
            for c in range(w.chunks):
                products_n(nc, pe, w, split, h_t, tiles, ps, c, free, product, spent, h_ready=None if whole is None else h_split)

        def take(eng):
            for g in range(w.chunks // w.parts):
                for i, (rows, col) in enumerate(tiles):
                    u = g * nt + i
                    eng.wait_ge(product, u + 1)
                    emit(g, i, ps[u % 8][0:rows, :]).then_inc(taken, 1)

        def split_hi(eng):
            for c in range(w.chunks):
                if c >= 2:
                    wait_spent(eng, w, c - 2, nt, product, spent)
                split.split_hi(eng, c // 2, c % 2)

        @block.scalar
        def _(act):
            if engine == "scalar":
                take(act)
            else:
                split_hi(act)

        @block.vector
        def _(dve):
            if whole is not None:
                split_whole(nc, dve, whole, h_t, w.parts, h_hi, h_split)
            if engine == "scalar":
                split_hi(dve)
            else:
                take(dve)


X_COLS = [(P, i * P) for i in range(TT)]


def add_to_x(nc, core, width=512):
    def emit(c, i, product):
        x = core.x[:, i, c * width:(c + 1) * width]
        return nc.vector.tensor_tensor(x, x, product, ALU.add)
    return emit


def stage_delta_out(nc, core, whole, o, ss, gain, o_t):
    sem = lambda n: nc.alloc_semaphore(f"do_{n}")
    gain_loaded, spent, h_hi, h_split = map(sem, ("gain_loaded", "spent", "h_hi", "h_split"))
    meaned, rooted, product, gated, normed, mixed, step, turned, taken = map(
        sem, ("meaned", "rooted", "product", "gated", "normed", "mixed", "step", "turned", "taken"))
    with ExitStack() as ctx:
        split = Split(nc, core, ctx, "do")
        h_t = sb_parts(nc, ctx, "do_h", [P, KD, T])
        rstd = sb(nc, ctx, "do_rstd", [P, 2, TT * HA])
        sil = sb(nc, ctx, "do_sil", [P, 2, 512])
        on = sb(nc, ctx, "do_on", [P, 2, 512])
        gb = sb(nc, ctx, "do_gain", [P, DV])
        ps, pt = banks(nc, ctx, "do_ps", 6), banks(nc, ctx, "do_pt", 2)
        block = ctx.enter_context(nc.Block())
        w = split.w
        U = 4 * TT

        @block.sync
        def _(sp):
            sp.dma_start(gb[:, :], gain.partition_broadcast(P)).then_inc(gain_loaded, 16)
            split.loads(sp)

        @block.tensor
        def _(pe):
            def turn(u):
                pe.wait_ge(mixed, u + 1)
                if u >= 2:
                    pe.wait_ge(taken, u - 1)
                for k in range(4):
                    last = nc.tensor.transpose(pt[u % 2][:, k * P:(k + 1) * P], on[:, u % 2, k * P:(k + 1) * P],
                                               core.c[:, C_IDENT:C_IDENT + P])
                last.then_inc(turned, 1)
            def free(u):
                if u >= 6:
                    pe.wait_ge(gated, u - 5)

            def finished(u):
                if u:
                    turn(u - 1)
            for c in range(w.chunks):
                products_n(nc, pe, w, split, h_t, X_COLS, ps, c, free, product, spent, finished, h_split)
            turn(U - 1)

        @block.gpsimd
        def _(pool):
            pool.wait_ge(meaned, 1)
            nc.gpsimd.tensor_tensor(rstd[:, 1, :], rstd[:, 0, :], core.c[:, C_MHALF:C_MHALF + 1].to_broadcast([P, TT * HA]),
                                    ALU.pow).then_inc(rooted, 1)
            split.split_lo(pool)

        @block.scalar
        def _(act):
            for b in range(2):
                split.split_hi(act, 0, b)
            for u in range(U):
                act.wait_ge(product, u + 1)
                if u >= 2:
                    act.wait_ge(mixed, u - 1)
                nc.scalar.activation(sil[:, u % 2, :], ps[u % 6][:, :], ACT.Silu).then_inc(gated, 1)
                group, i = divmod(u, TT)
                if i in (0, TT - 1) and group + 1 < U // TT:
                    split.split_hi(act, group + 1, i // (TT - 1))

        @block.vector
        def _(dve):
            nc.vector.tensor_scalar(rstd[:, 0, :], ss.rearrange("p i h -> p (i h)"), 1.0 / DV, EPS, ALU.mult, ALU.add).then_inc(meaned, 1)
            split_whole(nc, dve, whole, h_t, w.parts, h_hi, h_split)
            dve.wait_ge(rooted, 1)
            dve.wait_ge(gain_loaded, 16)

            def store(u):
                c, i = divmod(u, TT)
                dve.wait_ge(turned, u + 1)
                nc.vector.tensor_copy(o_t[:, 4 * c:4 * c + 4, i * P:(i + 1) * P],
                                      pt[u % 2][:, :].rearrange("p (k t) -> p k t", k=4)).then_inc(taken, 1)
            for u in range(U):
                c, i = divmod(u, TT)
                if u >= 2:
                    dve.wait_ge(turned, u - 1)
                for j in range(2):
                    h = 2 * c + j
                    nc.vector.scalar_tensor_tensor(on[:, u % 2, j * DV:(j + 1) * DV], o[:, h, i, :],
                                                   rstd[:, 1, i * HA + h:i * HA + h + 1], gb[:, :],
                                                   ALU.mult, ALU.mult).then_inc(step, 1)
                dve.wait_ge(step, 2 * u + 2)
                dve.wait_ge(gated, u + 1)
                nc.vector.tensor_tensor(on[:, u % 2, :], on[:, u % 2, :], sil[:, u % 2, :], ALU.mult).then_inc(mixed, 1)
                if u:
                    store(u - 1)
            store(U - 1)


def stage_shared_k(nc, core, kv, k_t):
    sem = lambda n: nc.alloc_semaphore(f"sk_{n}")
    squared, step, meaned, rooted, normed, turned, taken, gained = map(
        sem, ("squared", "step", "meaned", "rooted", "normed", "turned", "taken", "gained"))
    KW = KVB * HD
    with ExitStack() as ctx:
        sq = sb(nc, ctx, "sk_sq", [P, TT, KW])
        r = sb(nc, ctx, "sk_r", [P, 3, TT * KVB])
        kn = sb(nc, ctx, "sk_kn", [P, TT, KVB, 2, HD])
        g = sb(nc, ctx, "sk_g", [P, 1])
        ps = banks(nc, ctx, "sk_ps", 4)
        block = ctx.enter_context(nc.Block())

        @block.scalar
        def _(act):
            nc.scalar.activation(sq[:, :, :], kv[:, :, 0:KW], ACT.Square).then_inc(squared, 1)

        @block.gpsimd
        def _(pool):
            pool.wait_ge(meaned, 1)
            nc.gpsimd.tensor_tensor(r[:, 2, :], r[:, 1, :], core.c[:, C_MHALF:C_MHALF + 1].to_broadcast([P, TT * KVB]),
                                    ALU.pow).then_inc(rooted, 1)

        @block.tensor
        def _(pe):
            pe.wait_ge(normed, TT)
            for h in range(KVB):
                for i in range(TT):
                    last = nc.tensor.transpose(ps[h][:, i * P:(i + 1) * P], kn[:, i, h, :, :].rearrange("p a d -> p (a d)"),
                                               core.c[:, C_IDENT:C_IDENT + P])
                last.then_inc(turned, 1)

        @block.vector
        def _(dve):
            nc.vector.tensor_tensor(g[:, :], core.v[:, V_QGK:V_QGK + 1], core.v[:, V_QGK + 1:V_QGK + 2], ALU.mult).then_inc(gained, 1)
            dve.wait_ge(squared, 1)
            nc.vector.tensor_reduce(r[:, 0, :], sq[:, :, :].rearrange("p i (h d) -> p (i h) d", d=HD), AX.X, ALU.add).then_inc(step, 1)
            dve.wait_ge(step, 1)
            nc.vector.tensor_scalar(r[:, 1, :], r[:, 0, :], 1.0 / HD, EPS, ALU.mult, ALU.add).then_inc(meaned, 1)
            dve.wait_ge(rooted, 1)
            for i in range(TT):
                nc.vector.tensor_tensor(kn[:, i, :, :, :], kv[:, i, 0:KW].rearrange("p (h d) -> p h d", d=HD).unsqueeze(2).to_broadcast([P, KVB, 2, HD]),
                                        r[:, 2, i * KVB:(i + 1) * KVB].unsqueeze(2).unsqueeze(3).to_broadcast([P, KVB, 2, HD]),
                                        ALU.mult).then_inc(normed, 1)
            dve.wait_ge(gained, 1)
            for h in range(KVB):
                dve.wait_ge(turned, h + 1)
                nc.vector.tensor_scalar(k_t[:, h, :], ps[h][:, :], g[:, 0:1], None, ALU.mult).then_inc(taken, 1)


def stage_head_scale(nc, core, tag, q_t, tiles, cols, out, scale2):
    sem = lambda n: nc.alloc_semaphore(f"{tag}_{n}")
    squared, summed, rooted, inverted, scaled = map(sem, ("squared", "summed", "rooted", "inverted", "scaled"))
    w = len(cols) * 2 * tiles
    with ExitStack() as ctx:
        sq = sb(nc, ctx, f"{tag}_sq", [P, 2, T])
        rt = sb(nc, ctx, f"{tag}_rt", [P, w])
        ps = banks(nc, ctx, f"{tag}_ps", 1)[0]
        block = ctx.enter_context(nc.Block())

        @block.scalar
        def _(act):
            for n in range(tiles):
                if n >= 2:
                    act.wait_ge(summed, n - 1)
                nc.scalar.activation(sq[:, n % 2, :], q_t[:, n, :], ACT.Square).then_inc(squared, 1)
            act.wait_ge(summed, tiles)
            nc.scalar.activation(rt[:, :], ps[:, 0:w], ACT.Sqrt, bias=core.eps[:, 1:2]).then_inc(rooted, 1)

        @block.tensor
        def _(pe):
            for n in range(tiles):
                pe.wait_ge(squared, n + 1)
                for i, c in enumerate(cols):
                    at = (i * tiles + n) * 2
                    last = nc.tensor.matmul(ps[:, at:at + 2], sq[:, n % 2, c:c + P], core.c[:, C_PAIR:C_PAIR + 2], start=True, stop=True)
                last.then_inc(summed, 1)

        @block.vector
        def _(dve):
            dve.wait_ge(rooted, 1)
            nc.vector.reciprocal(out.rearrange("p i h -> p (i h)"), rt[:, :]).then_inc(inverted, 1)
            if scale2 != 1:
                dve.wait_ge(inverted, 1)
                nc.vector.tensor_scalar(out.rearrange("p i h -> p (i h)"), out.rearrange("p i h -> p (i h)"), scale2, None, ALU.mult).then_inc(scaled, 1)


def stage_bias(nc, core, tables, rel_bias, scratch, bias):
    sem = lambda n: nc.alloc_semaphore(f"rb_{n}")
    loaded, product, masked, stored, back, flipped, copied = map(sem, ("loaded", "product", "masked", "stored", "back", "flipped", "copied"))
    with ExitStack() as ctx:
        rb = sb(nc, ctx, "rb_in", [32, HB])
        buckets = sb(nc, ctx, "rb_buckets", [32, R_WIDTH - R_KEPT])
        row = sb(nc, ctx, "rb_row", [HB, 384])
        shifted = sb(nc, ctx, "rb_shifted", [P, HB, 256])
        ps = banks(nc, ctx, "rb_ps", 1)[0]
        turn = banks(nc, ctx, "rb_turn", 4)
        block = ctx.enter_context(nc.Block())

        @block.sync
        def _(sp):
            sp.dma_start(rb[:, :], rel_bias).then_inc(loaded, 16)
            sp.dma_start(buckets[:, :], tables[:, R_KEPT:R_WIDTH]).then_inc(loaded, 16)
            sp.wait_ge(masked, 1)
            sp.dma_start(scratch, row[:, :]).then_inc(stored, 16)
            sp.wait_ge(stored, 16)
            with nc.allow_non_contiguous_dma("rows shifted by one"):
                for h in range(0, HB, 8):
                    src = bass.AP(scratch.tensor, h * 384, [[1, P], [384, 8], [1, 256]])
                    sp.dma_start(shifted[:, h:h + 8, :], src).then_inc(back, 16)

        @block.tensor
        def _(pe):
            pe.wait_ge(loaded, 32)
            nc.tensor.matmul(ps[0:HB, 0:384], rb[:, :], buckets[:, 0:384], start=True, stop=True).then_inc(product, 1)
            pe.wait_ge(back, 64)
            for i in range(HB // 2):
                if i >= 4:
                    pe.wait_ge(copied, i - 3)
                nc.tensor.matmul(turn[i % 4][:, :], core.c[:, C_FLIP:C_FLIP + P], shifted[:, 2 * i:2 * i + 2, :],
                                 start=True, stop=True).then_inc(flipped, 1)

        @block.vector
        def _(dve):
            dve.wait_ge(product, 1)
            nc.vector.tensor_tensor(row[:, :], ps[0:HB, 0:384], buckets[:, 384:768], ALU.add).then_inc(masked, 1)
            for i in range(HB // 2):
                dve.wait_ge(flipped, i + 1)
                nc.vector.tensor_copy(bias[:, 2 * i:2 * i + 2, :], turn[i % 4][:, :].rearrange("p (h s) -> p h s", h=2)).then_inc(copied, 1)


def stage_window_attention(nc, core, q_t, k_t, kv, rq, bias, sinks, z):
    sem = lambda n: nc.alloc_semaphore(f"wa_{n}")
    (loaded, scored, biased, step, shifted, expd, sunk, turned, act_taken, dve_taken, summed, mixed, weighted) = map(sem, (
        "loaded", "scored", "biased", "step", "shifted", "expd", "sunk", "turned", "scalar_taken", "vector_taken", "summed", "mixed", "weighted"))
    ident = core.c[:, C_IDENT:C_IDENT + P]
    G = HB // 4
    U = [(n, g) for n in range(TT) for g in range(G)]
    with ExitStack() as ctx:
        lg = sb(nc, ctx, "wa_lg", [P, 2, 4, 256])
        pt = sb(nc, ctx, "wa_pt", [P, 4, 2, P])
        sm = sb(nc, ctx, "wa_sm", [P, 2, 8, 4])
        snk = sb(nc, ctx, "wa_snk", [P, HB])
        tmp = sb(nc, ctx, "wa_tmp", [P, 256])
        sc = [banks(nc, ctx, f"wa_sc{e}", 2) for e in range(2)]
        tp = banks(nc, ctx, "wa_tp", 2)
        po = banks(nc, ctx, "wa_po", 2)
        block = ctx.enter_context(nc.Block())
        first = lambda n: P if n == 0 else 0
        col = lambda u, k, e=slice(0, 4): sm[:, u % 2, k, e]

        @block.sync
        def _(sp):
            sp.dma_start(snk[:, :], sinks.partition_broadcast(P)).then_inc(loaded, 16)

        @block.tensor
        def _(pe):
            def scores(u):
                n, g = U[u]
                s0 = first(n)
                if u >= 2:
                    pe.wait_ge(biased, u - 1)
                for e in range(4):
                    half = slice(64 * (e % 2), 64 * (e % 2) + 64)
                    last = nc.tensor.matmul(sc[e % 2][u % 2][:, e // 2 * 256 + s0:e // 2 * 256 + 256],
                                            q_t[half, 2 * g + e // 2, n * P:(n + 1) * P],
                                            k_t[half, g // 2, n * P + s0 - P:(n + 1) * P], start=True, stop=True)
                last.then_inc(scored, 1)
            scores(0)
            for u, (n, g) in enumerate(U):
                if u + 1 < len(U):
                    scores(u + 1)
                blocks = range(1 if n == 0 else 0, 2)
                for p in range(2):
                    pe.wait_ge(expd, 2 * u + p + 1)
                    if u:
                        pe.wait_ge((act_taken, dve_taken)[p], u)
                    for e in (2 * p, 2 * p + 1):
                        for b in blocks:
                            last = nc.tensor.transpose(tp[p][:, (e % 2 * 2 + b) * P:(e % 2 * 2 + b + 1) * P],
                                                       lg[:, u % 2, e, b * P:(b + 1) * P], ident)
                    last.then_inc(turned, 1)
                if u >= 2:
                    pe.wait_ge(weighted, u - 1)
                for e in range(4):
                    if e % 2 == 0:
                        pe.wait_ge((act_taken, dve_taken)[e // 2], u + 1)
                    for b in blocks:
                        last = nc.tensor.matmul(po[u % 2][:, e * HD:(e + 1) * HD], pt[:, e, b, :],
                                                kv[:, n - 1 + b, (KVB + g // 2) * HD:(KVB + g // 2 + 1) * HD],
                                                start=(b == blocks[0]), stop=(b == 1))
                last.then_inc(mixed, 1)

        @block.scalar
        def _(act):
            for u, (n, g) in enumerate(U):
                s0 = first(n)
                act.wait_ge(shifted, u + 1)
                for e in range(4):
                    last = nc.scalar.activation(lg[:, u % 2, e, s0:256], lg[:, u % 2, e, s0:256], ACT.Exp,
                                                bias=col(u, 2, slice(e, e + 1)), accum_out=col(u, 4, slice(e, e + 1)))
                    if e % 2:
                        last.then_inc(expd, 1)
                nc.scalar.activation(col(u, 5), col(u, 3), ACT.Exp).then_inc(sunk, 1)
                act.wait_ge(turned, 2 * u + 1)
                if u:
                    act.wait_ge(mixed, u)
                nc.scalar.activation(pt[:, 0:2, first(n) // P:2, :], tp[0][:, :].rearrange("p (e b t) -> p e b t", e=2, b=2)[:, :, first(n) // P:2, :],
                                     ACT.Copy).then_inc(act_taken, 1)

        @block.vector
        def _(dve):
            then = Chain(dve, step)

            def logits(u):
                n, g = U[u]
                s0 = first(n)
                dve.wait_ge(scored, u + 1)
                if u >= 2:
                    dve.wait_ge(turned, 2 * (u - 1))
                for e in range(4):
                    h = 4 * g + e
                    last = nc.vector.scalar_tensor_tensor(lg[:, u % 2, e, s0:256], sc[e % 2][u % 2][:, e // 2 * 256 + s0:e // 2 * 256 + 256],
                                                          rq[:, n, h:h + 1], bias[:, h, s0:256], ALU.mult, ALU.add)
                last.then_inc(biased, 1)
                dve.wait_ge(biased, u + 1)
                sk = snk[:, 4 * g:4 * g + 4]
                then(nc.vector.tensor_reduce(col(u, 0), lg[:, u % 2, :, s0:256], AX.X, ALU.max))
                then(nc.vector.tensor_tensor(col(u, 1), col(u, 0), sk, ALU.max))
                nc.vector.tensor_scalar(col(u, 2), col(u, 1), -1.0, None, ALU.mult)
                nc.vector.tensor_tensor(col(u, 3), sk, col(u, 1), ALU.subtract).then_inc(shifted, 1)
            dve.wait_ge(loaded, 16)
            logits(0)
            for u, (n, g) in enumerate(U):
                if u + 1 < len(U):
                    logits(u + 1)
                dve.wait_ge(turned, 2 * u + 2)
                if u:
                    dve.wait_ge(mixed, u)
                nc.vector.tensor_copy(pt[:, 2:4, first(n) // P:2, :], tp[1][:, :].rearrange("p (e b t) -> p e b t", e=2, b=2)[:, :, first(n) // P:2, :]).then_inc(dve_taken, 1)
                dve.wait_ge(sunk, u + 1)
                then(nc.vector.tensor_tensor(col(u, 6), col(u, 4), col(u, 5), ALU.add))
                then(nc.vector.reciprocal(col(u, 7), col(u, 6)))
                dve.wait_ge(mixed, u + 1)
                then(nc.vector.tensor_tensor(tmp[:, :].rearrange("p (e d) -> p e d", e=4), po[u % 2][:, 0:256].rearrange("p (e d) -> p e d", e=4),
                                             sm[:, u % 2, 7, :].unsqueeze(2).to_broadcast([P, 4, HD]), ALU.mult))
                zz = z[:, n, g * 256:(g + 1) * 256]
                nc.vector.tensor_tensor(zz, zz, tmp[:, :], ALU.mult).then_inc(weighted, 1)


def stage_turn(nc, core, tag, src, n, out):
    turned, taken = [nc.alloc_semaphore(f"{tag}_turned{i}") for i in range(2)], [nc.alloc_semaphore(f"{tag}_taken{i}") for i in range(2)]
    with ExitStack() as ctx:
        ps = banks(nc, ctx, f"{tag}_ps", 4)
        block = ctx.enter_context(nc.Block())

        @block.tensor
        def _(pe):
            for k in range(n):
                if k >= 4:
                    pe.wait_ge(taken[k % 2], k // 2 - 1)
                for i in range(TT):
                    last = nc.tensor.transpose(ps[k % 4][:, i * P:(i + 1) * P], src[:, i, k * P:(k + 1) * P], core.c[:, C_IDENT:C_IDENT + P])
                last.then_inc(turned[k % 2], 1)

        @block.scalar
        def _(act):
            for k in range(0, n, 2):
                act.wait_ge(turned[0], k // 2 + 1)
                nc.scalar.activation(out[:, k, :], ps[k % 4][:, :], ACT.Copy).then_inc(taken[0], 1)

        @block.vector
        def _(dve):
            for k in range(1, n, 2):
                dve.wait_ge(turned[1], k // 2 + 1)
                nc.vector.tensor_copy(out[:, k, :], ps[k % 4][:, :]).then_inc(taken[1], 1)


def delta_block(nc, core, a):
    with ExitStack() as ctx:
        qk = sb(nc, ctx, "qk_t", [P, 2 * HA, T])
        with ExitStack() as c2:
            hw = sb(nc, c2, "h_t", [P, KD, T])
            c3 = c2.enter_context(ExitStack())
            h = sb_parts(nc, c3, "h_t", [P, KD, T], side="right")
            v = sb(nc, c2, "v_t", [P, 2 * HA, T])
            rows = sb(nc, c2, "gate_rows", [8, 2, T])
            cols = sb(nc, c2, "gate_cols", [P, 4, TT, HA])
            ss = sb(nc, c2, "o_squares", [P, TT, HA])
            stage_norm(nc, core, "na", x_tiles(core), V_ANORM, h, whole=hw)
            stage_proj_conv(nc, core, "pa", h, core.ta[:, 0:2 * HA, :], qk, [(0, T)], T)
            stage_proj_conv(nc, core, "pv", h, core.ta[:, 2 * HA:, :], v, [(0, T)], T)
            stage_unit_rows(nc, core, "ua", qk)
            stage_delta_gates(nc, core, h, a["a_w_in"], rows, cols)
            c3.close()
            stage_delta_chunks(nc, core, qk, v, rows, cols, ss)
            o = v[:, :, :].rearrange("p (h j) (a d) -> p h (j a) d", j=2, a=2)
            stage_delta_out(nc, core, hw, o, ss[:, :, :], a["a_o_gain"], qk)
        stage_proj_n(nc, core, "oa", None, X_COLS, "vector", add_to_x(nc, core), whole=qk)


def window_block(nc, core, a, scratch):
    silu_to = lambda dst: (lambda c, i, product: nc.scalar.activation(dst[:, i, c * 512:(c + 1) * 512], product, ACT.Silu))
    with ExitStack() as ctx:
        q_t = sb(nc, ctx, "q_t", [P, HB * HD // P, T])
        with ExitStack() as c2:
            z = sb(nc, c2, "z", [P, TT, HB * HD])
            kv = sb(nc, c2, "kv", [P, TT, 2 * KVB * HD])
            k_t = sb(nc, c2, "k_t", [P, KVB, T])
            rq = sb(nc, c2, "rq", [P, TT, HB])
            with ExitStack() as c3:
                h = sb_parts(nc, c3, "hb_t", [P, KD, T])
                stage_norm(nc, core, "nk", x_tiles(core), V_KVNORM, h)
                stage_proj_n(nc, core, "pk", h, X_COLS, "scalar", lambda c, i, product: nc.scalar.activation(kv[:, i, :], product, ACT.Copy))
                stage_shared_k(nc, core, kv, k_t)
                stage_norm(nc, core, "nb", x_tiles(core), V_BNORM, h)
                stage_proj_t(nc, core, "pq", h, q_t, [(0, T)])
                stage_proj_n(nc, core, "pz", h, X_COLS, "scalar", silu_to(z))
            stage_head_scale(nc, core, "hq", q_t, HB * HD // P, [i * P for i in range(TT)], rq[:, :, :], 1)
            with ExitStack() as c3:
                bias = sb(nc, c3, "bias", [P, HB, 256])
                stage_bias(nc, core, a["c32"], a["rel_bias"], scratch, bias)
                stage_window_attention(nc, core, q_t, k_t, kv, rq, bias, a["b_sinks"], z)
            stage_turn(nc, core, "tb", z, HB * HD // P, q_t)
        stage_proj_n(nc, core, "ob", None, X_COLS, "vector", add_to_x(nc, core), whole=q_t)


S_TILES = [(META, 0, 0)] + [(P, META + P * i, P * i) for i in range(TT)]
HALF2 = T2 // 2
MQ, MV, MO, MI, MF, FQ, FV, FF = 0, 1024, 1536, 2048, 2052, 2056, 3080, 3592


def stage_mix_gates(nc, core, h_t, w, mrow, acol, emcol, negc):
    sem = lambda n: nc.alloc_semaphore(f"mg_{n}")
    zeroed, loaded, product, vstep, astep, turned, cast, cast_taken, split = map(
        sem, ("zeroed", "loaded", "product", "vector_step", "scalar_step", "turned", "cast", "cast_taken", "weights_split"))
    G = GATE_COLS
    with ExitStack() as ctx:
        wg = sb(nc, ctx, "mg_w", [P, KD, G])
        wp = sb_parts(nc, ctx, "mg_wp", [P, KD, G])
        t = [sb(nc, ctx, f"mg_t{i}", [G, T2]) for i in range(4)]
        b = sb(nc, ctx, "mg_b", [HM, T2])
        am = sb(nc, ctx, "mg_am", [HM, 2, T2])
        nc8 = sb(nc, ctx, "mg_nc", [HF, T2])
        ps = banks(nc, ctx, "mg_ps", 2)
        pt = banks(nc, ctx, "mg_pt", 1)[0]
        pc = banks(nc, ctx, "mg_pc", 4)
        block = ctx.enter_context(nc.Block())
        wv = w_view(w, KD)

        @block.sync
        def _(sp):
            sp.wait_ge(zeroed, 1)
            for dst, src, n in ((0, MI, HM), (32, MF, HM), (64, FF, HF)):
                with nc.allow_non_contiguous_dma("a few gate columns"):
                    sp.dma_start(wg[:, :, dst:dst + n], wv[:, :, src:src + n]).then_inc(loaded, 16)

        @block.tensor
        def _(pe):
            pe.wait_ge(split, 2)
            for half in range(2):
                for k in range(KD):
                    cols = slice(half * HALF2, (half + 1) * HALF2)
                    last = matmul_parts(nc, ps[half][0:G, 0:HALF2], (wp[0][:, k, :], wp[1][:, k, :]),
                                        (h_t[0][:, k, cols], h_t[1][:, k, cols]), k == 0, k == KD - 1)
            last.then_inc(product, 1)
            pe.wait_ge(vstep, 10)
            pe.wait_ge(astep, 3)
            for j, (rows, c, _t) in enumerate(S_TILES):
                nc.tensor.transpose(pt[0:rows, j * 4:j * 4 + 4], am[:, 0, c:c + rows], core.c[0:HM, C_IDENT:C_IDENT + HM])
            for i in range(TT):
                c = META + i * P
                last = nc.tensor.transpose(pt[:, 32 + i * 4:36 + i * 4], am[:, 1, c:c + P], core.c[0:HM, C_IDENT:C_IDENT + HM])
            last.then_inc(turned, 1)
            for u in range(2 * HF):
                h, half = divmod(u, 2)
                if u >= 4:
                    pe.wait_ge(cast_taken, u - 3)
                nc.tensor.matmul(pc[u % 4][:, 0:HALF2], core.r[0:HF, R_SEL + h * P:R_SEL + (h + 1) * P],
                                 nc8[:, half * HALF2:(half + 1) * HALF2], start=True, stop=True).then_inc(cast, 1)

        @block.scalar
        def _(act):
            act.wait_ge(vstep, 3)
            nc.scalar.activation(t[1][:, :], t[1][:, :], ACT.Exp, scale=-1.0).then_inc(astep, 1)
            act.wait_ge(astep, 1)
            nc.scalar.activation(t[1][:, :], t[1][:, :], ACT.Ln, bias=1.0).then_inc(astep, 1)
            act.wait_ge(vstep, 10)
            nc.scalar.activation(am[:, 1, :], am[:, 1, :], ACT.Exp, scale=-1.0).then_inc(astep, 1)
            for u in range(2 * HF):
                h, half = divmod(u, 2)
                act.wait_ge(cast, u + 1)
                nc.scalar.activation(negc[:, h, half * HALF2:(half + 1) * HALF2], pc[u % 4][:, 0:HALF2], ACT.Copy).then_inc(cast_taken, 1)

        @block.vector
        def _(dve):
            nc.vector.memset(wg[:, :, :], 0.0).then_inc(zeroed, 1)
            dve.wait_ge(loaded, 48)
            split_small(nc, dve, wg, wp, split)
            then = Chain(dve, vstep)
            dve.wait_ge(product, 1)
            for half in range(2):
                then(nc.vector.tensor_scalar(t[0][:, half * HALF2:(half + 1) * HALF2], ps[half][0:G, 0:HALF2], core.v[0:G, V_BI:V_BI + 1], None, ALU.add))
            then(nc.vector.scalar_tensor_tensor(t[1][:, :], t[0][:, :], -1.0, t[0][:, :], ALU.mult, ALU.max))
            dve.wait_ge(astep, 2)
            then(nc.vector.scalar_tensor_tensor(t[2][:, :], t[0][:, :], 0.0, t[1][:, :], ALU.min, ALU.subtract))
            then(nc.vector.tensor_tensor_scan(t[3][:, :], core.one[0:G, :], t[2][:, :], 0.0, ALU.mult, ALU.add))
            then(nc.vector.tensor_copy(b[:, :], t[3][32:32 + HM, :]))
            then(nc.vector.tensor_scalar(nc8[:, :], t[3][64:64 + HF, :], -1.0, None, ALU.mult))
            then(nc.vector.tensor_tensor(am[:, 0, :], t[0][0:HM, :], b[:, :], ALU.subtract))
            then(nc.vector.tensor_tensor_scan(mrow[:, :], am[:, 0, :], am[:, 0, :], 0.0, ALU.max, ALU.max))
            then(nc.vector.tensor_tensor(am[:, 1, :], b[:, :], mrow[:, :], ALU.add))
            dve.wait_ge(turned, 1)
            nc.vector.tensor_copy(acol[:, 1:, :], pt[:, 4:20].rearrange("p (j h) -> p j h", h=4))
            nc.vector.tensor_copy(acol[0:META, 0, :], pt[0:META, 0:4])
            nc.vector.tensor_copy(emcol[:, :, :], pt[:, 32:48].rearrange("p (j h) -> p j h", h=4))


def stage_mlstm(nc, core, qk, v, mrow, acol, nd):
    sem = lambda n: nc.alloc_semaphore(f"ml_{n}")
    cast, shifted, expd, masked, scored, weighted, mixed, taken = map(
        sem, ("cast", "shifted", "expd", "masked", "scored", "weighted", "mixed", "taken"))
    offs, o = [], 0
    for j, (rows, c, t0) in enumerate(S_TILES):
        offs.append(o)
        o += T - t0
    N = len(S_TILES)
    with ExitStack() as ctx:
        ew = sb(nc, ctx, "ml_ew", [P, 2, o])
        pm = banks(nc, ctx, "ml_pm", 2)
        psc = banks(nc, ctx, "ml_ps", 4)
        po = banks(nc, ctx, "ml_po", 2)
        block = ctx.enter_context(nc.Block())
        e = lambda h, j, a=0, n=None: ew[0:S_TILES[j][0], h % 2, offs[j] + a:offs[j] + (T - S_TILES[j][2] if n is None else a + n)]

        @block.tensor
        def _(pe):
            for h in range(HM):
                if h >= 2:
                    pe.wait_ge(shifted, N * (h - 1))
                nc.tensor.matmul(pm[h % 2][:, :], core.r[0:HM, R_SEL + h * P:R_SEL + (h + 1) * P], mrow[:, META:], start=True, stop=True).then_inc(cast, 1)
                for j, (rows, c, t0) in enumerate(S_TILES):
                    u = h * N + j
                    if u >= 4:
                        pe.wait_ge(weighted, u - 3)
                    nc.tensor.matmul(psc[u % 4][0:rows, 0:T - t0], qk[:, HM + h, c:c + rows], qk[:, h, META + t0:T2], start=True, stop=True).then_inc(scored, 1)
                for i in range(TT):
                    u = h * TT + i
                    if u >= 2:
                        pe.wait_ge(taken, u - 1)
                    pe.wait_ge(weighted, h * N + i + 2)
                    for j in range(i + 2):
                        rows, c, t0 = S_TILES[j]
                        last = nc.tensor.matmul(po[u % 2][:, 0:DM + 1], e(h, j, i * P - t0, P), v[0:rows, j, h, :], start=(j == 0), stop=(j == i + 1))
                    last.then_inc(mixed, 1)

        @block.vector
        def _(dve):
            for h in range(HM):
                dve.wait_ge(cast, h + 1)
                if h >= 2:
                    dve.wait_ge(mixed, TT * (h - 1))
                for j, (rows, c, t0) in enumerate(S_TILES):
                    nc.vector.tensor_scalar(e(h, j), pm[h % 2][0:rows, t0:T], acol[0:rows, j, h:h + 1], 0.0, ALU.subtract, ALU.max).then_inc(shifted, 1)
                for j, (rows, c, t0) in enumerate(S_TILES):
                    u = h * N + j
                    dve.wait_ge(scored, u + 1)
                    dve.wait_ge(expd, u + 1)
                    if j:
                        dve.wait_ge(masked, h * TT + j)
                    nc.vector.scalar_tensor_tensor(e(h, j), psc[u % 4][0:rows, 0:T - t0], DM ** -0.5, e(h, j), ALU.mult, ALU.mult).then_inc(weighted, 1)

        @block.scalar
        def _(act):
            for h in range(HM):
                for j in range(N):
                    act.wait_ge(shifted, h * N + j + 1)
                    nc.scalar.activation(e(h, j), e(h, j), ACT.Exp, scale=-1.0).then_inc(expd, 1)
                for i in range(TT):
                    u = h * TT + i
                    act.wait_ge(mixed, u + 1)
                    nc.scalar.activation(nd[:, i, h, :], po[u % 2][:, 0:DM + 1], ACT.Copy).then_inc(taken, 1)

        @block.gpsimd
        def _(pool):
            for h in range(HM):
                for j in range(1, N):
                    pool.wait_ge(expd, h * N + j + 1)
                    nc.gpsimd.tensor_tensor(e(h, j, 0, P), e(h, j, 0, P), core.c[:, C_LE:C_LE + P], ALU.mult).then_inc(masked, 1)


def stage_mlstm_out(nc, core, nd, emcol, so, gain, y):
    sem = lambda n: nc.alloc_semaphore(f"mo_{n}")
    loaded, step, divided, squared, meaned, rooted = map(sem, ("loaded", "step", "divided", "squared", "meaned", "rooted"))
    with ExitStack() as ctx:
        gb = sb(nc, ctx, "mo_gain", [P, HM * DM])
        r = sb(nc, ctx, "mo_r", [P, 6, TT * HM])
        sq = sb(nc, ctx, "mo_sq", [P, TT, HM * DM])
        block = ctx.enter_context(nc.Block())
        th = lambda k: r[:, k, :].rearrange("p (i h) -> p i h", h=HM)
        wide = lambda k: th(k).unsqueeze(3).to_broadcast([P, TT, HM, DM])
        yh = y[:, :, 0:HM * DM].rearrange("p i (h d) -> p i h d", h=HM)
        ym = y[:, :, 0:HM * DM]

        @block.sync
        def _(sp):
            sp.dma_start(gb[:, :], gain.partition_broadcast(P)).then_inc(loaded, 16)

        @block.scalar
        def _(act):
            act.wait_ge(divided, 1)
            nc.scalar.activation(sq[:, :, :], ym, ACT.Square).then_inc(squared, 1)

        @block.gpsimd
        def _(pool):
            pool.wait_ge(meaned, 1)
            nc.gpsimd.tensor_tensor(r[:, 5, :], r[:, 4, :], core.c[:, C_MHALF:C_MHALF + 1].to_broadcast([P, TT * HM]), ALU.pow).then_inc(rooted, 1)

        @block.vector
        def _(dve):
            then = Chain(dve, step)
            den = nd[:, :, :, DM]
            then(nc.vector.scalar_tensor_tensor(th(0), den, -1.0, den, ALU.mult, ALU.max))
            then(nc.vector.tensor_tensor(th(1), th(0), emcol, ALU.max))
            then(nc.vector.reciprocal(r[:, 2, :], r[:, 1, :]))
            nc.vector.tensor_tensor(yh, nd[:, :, :, 0:DM], wide(2), ALU.mult).then_inc(divided, 1)
            dve.wait_ge(squared, 1)
            then(nc.vector.tensor_reduce(r[:, 3, :], sq[:, :, :].rearrange("p i (h d) -> p (i h) d", h=HM), AX.X, ALU.add))
            nc.vector.tensor_scalar(r[:, 4, :], r[:, 3, :], 1.0 / DM, EPS, ALU.mult, ALU.add).then_inc(meaned, 1)
            dve.wait_ge(rooted, 1)
            then(nc.vector.tensor_tensor(yh, yh, wide(5), ALU.mult))
            dve.wait_ge(loaded, 16)
            then(nc.vector.tensor_tensor(ym, ym, gb[:, :].unsqueeze(1).to_broadcast([P, TT, HM * DM]), ALU.mult))
            then(nc.vector.tensor_tensor(ym, ym, so[:, :, :], ALU.mult))


def stage_key_scale(nc, core, k_t):
    sem = lambda n: nc.alloc_semaphore(f"ks_{n}")
    gained, squared, summed, rooted, inverted, scaled = map(sem, ("gained", "squared", "summed", "rooted", "inverted", "scaled"))
    with ExitStack() as ctx:
        g = sb(nc, ctx, "ks_g", [P, 1])
        sq = sb(nc, ctx, "ks_sq", [P, 4, HALF2])
        rt = sb(nc, ctx, "ks_rt", [P, 4, HALF2])
        ps = banks(nc, ctx, "ks_ps", 4)
        block = ctx.enter_context(nc.Block())
        part = lambda u: k_t[:, u // 2, u % 2 * HALF2:(u % 2 + 1) * HALF2]
        N = 8

        @block.scalar
        def _(act):
            for b in range(0, N, 4):
                for u in range(b, b + 4):
                    if u >= 4:
                        act.wait_ge(summed, u - 3)
                    nc.scalar.activation(sq[:, u % 4, :], part(u), ACT.Square).then_inc(squared, 1)
                for u in range(b, b + 4):
                    act.wait_ge(summed, u + 1)
                    if u >= 4:
                        act.wait_ge(scaled, u - 3)
                    nc.scalar.activation(rt[:, u % 4, :], ps[u % 4][:, 0:HALF2], ACT.Sqrt, bias=core.eps[:, 0:1], scale=1.0 / DF).then_inc(rooted, 1)

        @block.tensor
        def _(pe):
            for u in range(N):
                pe.wait_ge(squared, u + 1)
                if u >= 4:
                    pe.wait_ge(rooted, u - 3)
                nc.tensor.matmul(ps[u % 4][:, 0:HALF2], core.c[:, C_HALVES:C_HALVES + P], sq[:, u % 4, :], start=True, stop=True).then_inc(summed, 1)

        @block.vector
        def _(dve):
            nc.vector.tensor_tensor(g[:, :], core.v[:, V_FQK:V_FQK + 1], core.v[:, V_FQK + 1:V_FQK + 2], ALU.mult).then_inc(gained, 1)
            dve.wait_ge(gained, 1)
            for u in range(N):
                dve.wait_ge(rooted, u + 1)
                nc.vector.reciprocal(rt[:, u % 4, :], rt[:, u % 4, :]).then_inc(inverted, 1)
                dve.wait_ge(inverted, u + 1)
                nc.vector.scalar_tensor_tensor(part(u), part(u), g[:, 0:1], rt[:, u % 4, :], ALU.mult, ALU.mult).then_inc(scaled, 1)


def stage_forgetting_attention(nc, core, qk, v, rq, negc, y):
    sem = lambda n: nc.alloc_semaphore(f"fa_{n}")
    (scored, biased, step, shifted, expd, turned_a, turned_b, act_taken, dve_taken, mixed, weighted) = map(sem, (
        "scored", "biased", "step", "shifted", "expd", "turned_a", "turned_b", "scalar_taken", "vector_taken", "mixed", "weighted"))
    ident = core.c[:, C_IDENT:C_IDENT + P]
    U = [(h, i) for h in range(HF) for i in range(TT)]
    nb = lambda u: sum(1 for w in range(u + 1) if U[w][1] >= 2)
    with ExitStack() as ctx:
        lg = sb(nc, ctx, "fa_lg", [P, 2, T2])
        pt = sb(nc, ctx, "fa_pt", [P, 5, P])
        sm = sb(nc, ctx, "fa_sm", [P, 2, 4])
        sc = [banks(nc, ctx, f"fa_sc{e}", 2) for e in range(2)]
        tp = banks(nc, ctx, "fa_tp", 2)
        po = banks(nc, ctx, "fa_po", 2)
        block = ctx.enter_context(nc.Block())
        width = lambda i: META + P * (i + 1)
        col = lambda u, k: sm[:, u % 2, k:k + 1]

        @block.tensor
        def _(pe):
            def scores(u):
                h, i = U[u]
                half, hw = slice(64 * (h % 2), 64 * (h % 2) + 64), width(i) // 2
                if u >= 2:
                    pe.wait_ge(biased, u - 1)
                for p in range(2):
                    last = nc.tensor.matmul(sc[p][u % 2][:, 0:hw], qk[half, h // 2, META + i * P:META + (i + 1) * P],
                                            qk[half, 4 + h // 2, p * hw:(p + 1) * hw], start=True, stop=True)
                last.then_inc(scored, 1)
            scores(0)
            for u, (h, i) in enumerate(U):
                if u + 1 < len(U):
                    scores(u + 1)
                pe.wait_ge(expd, u + 1)
                if u:
                    pe.wait_ge(act_taken, u)
                for j in range(min(3, i + 2)):
                    rows, c, _t = S_TILES[j]
                    last = nc.tensor.transpose(tp[0][0:rows, j * P:(j + 1) * P], lg[:, u % 2, c:c + rows], ident)
                last.then_inc(turned_a, 1)
                if i >= 2:
                    if nb(u) > 1:
                        pe.wait_ge(dve_taken, nb(u) - 1)
                    for j in range(3, i + 2):
                        rows, c, _t = S_TILES[j]
                        last = nc.tensor.transpose(tp[1][:, (j - 3) * P:(j - 2) * P], lg[:, u % 2, c:c + rows], ident)
                    last.then_inc(turned_b, 1)
                if u >= 2:
                    pe.wait_ge(weighted, u - 1)
                pe.wait_ge(act_taken, u + 1)
                if i >= 2:
                    pe.wait_ge(dve_taken, nb(u))
                for j in range(i + 2):
                    rows, c, _t = S_TILES[j]
                    last = nc.tensor.matmul(po[u % 2][:, 0:DF], pt[0:rows, j, :], v[0:rows, j, h * DF:(h + 1) * DF], start=(j == 0), stop=(j == i + 1))
                last.then_inc(mixed, 1)

        @block.scalar
        def _(act):
            for u, (h, i) in enumerate(U):
                act.wait_ge(shifted, u + 1)
                nc.scalar.activation(lg[:, u % 2, 0:width(i)], lg[:, u % 2, 0:width(i)], ACT.Exp, bias=col(u, 1), accum_out=col(u, 2)).then_inc(expd, 1)
                act.wait_ge(turned_a, u + 1)
                if u:
                    act.wait_ge(mixed, u)
                nc.scalar.activation(pt[0:META, 0, :], tp[0][0:META, 0:P], ACT.Copy)
                n = min(2, i + 1)
                nc.scalar.activation(pt[:, 1:1 + n, :], tp[0][:, P:P + n * P].rearrange("p (j t) -> p j t", t=P), ACT.Copy).then_inc(act_taken, 1)

        @block.vector
        def _(dve):
            then = Chain(dve, step)

            def logits(u):
                h, i = U[u]
                hw, w = width(i) // 2, width(i)
                dve.wait_ge(scored, u + 1)
                if u >= 2:
                    dve.wait_ge(mixed, u - 1)
                for p in range(2):
                    c = slice(p * hw, (p + 1) * hw)
                    last = nc.vector.scalar_tensor_tensor(lg[:, u % 2, c], sc[p][u % 2][:, 0:hw], rq[:, i, h:h + 1], negc[:, h, c], ALU.mult, ALU.add)
                last.then_inc(biased, 1)
                dve.wait_ge(biased, u + 1)
                then(nc.vector.tensor_tensor(lg[:, u % 2, w - P:w], lg[:, u % 2, w - P:w], core.c[:, C_NEGDIAG:C_NEGDIAG + P], ALU.add))
                then(nc.vector.tensor_reduce(col(u, 0), lg[:, u % 2, 0:w], AX.X, ALU.max))
                nc.vector.tensor_scalar(col(u, 1), col(u, 0), -1.0, None, ALU.mult).then_inc(shifted, 1)
            logits(0)
            for u, (h, i) in enumerate(U):
                if u + 1 < len(U):
                    logits(u + 1)
                if i >= 2:
                    dve.wait_ge(turned_b, nb(u))
                    dve.wait_ge(mixed, u)
                    nc.vector.tensor_copy(pt[:, 3:i + 2, :], tp[1][:, 0:(i - 1) * P].rearrange("p (j t) -> p j t", t=P)).then_inc(dve_taken, 1)
                dve.wait_ge(expd, u + 1)
                then(nc.vector.reciprocal(col(u, 3), col(u, 2)))
                dve.wait_ge(mixed, u + 1)
                nc.vector.tensor_scalar(y[:, i, HM * DM + h * DF:HM * DM + (h + 1) * DF], po[u % 2][:, 0:DF], col(u, 3), None, ALU.mult).then_inc(weighted, 1)


def mixers(nc, core, a):
    meta_loaded = nc.alloc_semaphore("meta_loaded")
    with ExitStack() as outer:
        xm, core.one = sb(nc, outer, "meta_sb", [META, D]), sb(nc, outer, "one_sb", [P, T2])
        tiles = [(xm[:, :], META, 0)] + [(core.x[:, i, :], P, META + i * P) for i in range(TT)]
        y = sb(nc, outer, "y", [P, TT, D])
        with ExitStack() as ctx:
            mqk = sb(nc, ctx, "mqk_t", [P, 2 * HM, T2])
            fqk = sb(nc, ctx, "fqk_t", [P, 8, T2])
            vm = sb(nc, ctx, "vm", [P, 5, HM, DM + 1])
            vf = sb(nc, ctx, "vf", [P, 5, HF * DF])
            so = sb(nc, ctx, "so", [P, TT, HM * DM])
            mrow = sb(nc, ctx, "m_row", [HM, T2])
            acol = sb(nc, ctx, "a_col", [P, 5, HM])
            emcol = sb(nc, ctx, "em_col", [P, TT, HM])
            rq = sb(nc, ctx, "rq2", [P, TT, HF])
            c2 = ctx.enter_context(ExitStack())
            with ExitStack() as c3:
                h = sb_parts(nc, c3, "h2_t", [P, KD, T2], side="right")
                with nc.Block() as block:
                    @block.sync
                    def _(sp):
                        sp.dma_start(xm[:, :], a["meta"]).then_inc(meta_loaded, 16)
                        sp.wait_ge(meta_loaded, 16)

                    @block.vector
                    def _(dve):
                        nc.vector.memset(vm[:, :, :, DM:DM + 1], 1.0)
                        nc.vector.memset(core.one[:, :], 1.0)
                stage_norm(nc, core, "n2", tiles, V_NORM2, h)
                stage_proj_conv(nc, core, "pm", h, core.tm, mqk, [(0, HALF2), (HALF2, HALF2)], T2)
                stage_proj_t(nc, core, "pf", h, fqk, [(0, HALF2), (HALF2, HALF2)])

                def values(c, j, product):
                    rows = S_TILES[j][0]
                    if c == 0:
                        return nc.scalar.activation(vm[0:rows, j, :, 0:DM], product.rearrange("p (h d) -> p h d", h=HM), ACT.Copy)
                    return nc.scalar.activation(vf[0:rows, j, :], product, ACT.Copy)
                stage_proj_n(nc, core, "pw", h, [(rows, c) for rows, c, _ in S_TILES], "scalar", values)
                stage_proj_n(nc, core, "po", h, [(P, META + i * P) for i in range(TT)], "scalar",
                             lambda c, i, product: nc.scalar.activation(so[:, i, :], product, ACT.Sigmoid))
                negc = sb(nc, c2, "negc", [P, HF, T2])
                stage_mix_gates(nc, core, h, a["w_in_2"], mrow, acol, emcol, negc)
            with ExitStack() as c3:
                nd = sb(nc, c3, "nd", [P, TT, HM, DM + 1])
                stage_mlstm(nc, core, mqk, vm, mrow, acol, nd)
                stage_mlstm_out(nc, core, nd, emcol[:, :, :], so, a["m_out_norm_2"], y)
            stage_head_scale(nc, core, "hf", fqk[:, 0:4, META:], 4, [i * P for i in range(TT)], rq[:, :, :], 1)
            stage_key_scale(nc, core, fqk[:, 4:8, :])
            stage_forgetting_attention(nc, core, fqk, vf, rq, negc, y)
        y_t = sb(nc, outer, "y_t", [P, KD, T])
        stage_turn(nc, core, "t2", y, KD, y_t)
        stage_proj_n(nc, core, "o2", None, X_COLS, "vector", add_to_x(nc, core), whole=y_t)


def weights_plan(a):
    wi, w2 = a["a_w_in"], a["w_in_2"]
    wide = lambda n0, n: [n0 + 512 * g for g in range(n)]
    return [
        Weights(wi, KD, 0, 2 * HA * P // 256), Weights(wi, KD, 2 * HA * P, 2 * HA * P // 256),
        Weights(wi, KD, groups=wide(QKV_TILES * P, 4)), Weights(a["a_w_out"], HA * DV // P, groups=wide(0, 2)),
        Weights(a["w_kv"], KD, groups=[0]), Weights(a["b_w_in"], KD, 0, HB * HD // 256),
        Weights(a["b_w_in"], KD, groups=wide(HB * HD, 4)), Weights(a["b_w_out"], HB * HD // P, groups=wide(0, 2)),
        Weights(w2, KD, MQ, 4), Weights(w2, KD, FQ, 4), Weights(w2, KD, groups=[MV, FV]), Weights(w2, KD, groups=[MO]),
        Weights(a["w_out_2"], KD, groups=wide(0, 2)), Weights(a["peer_query"], KD, 0, 8),
    ]


class Query:
    STEPS = 2 * PH

    def __init__(self, nc, core, ctx, h, scores):
        self.nc, self.ring, self.w, self.h, self.scores = nc, core.ring, core.ring.take(), h, scores
        self.base = self.ring.filled
        self.keys_loaded, self.product, self.copied, self.scored, self.kept = (
            nc.alloc_semaphore(f"qu_{n}") for n in ("keys_loaded", "product", "copied", "scored", "kept"))
        self.keys = sb(nc, ctx, "qu_keys", [P, 2 * PH, NK])
        self.q = sb(nc, ctx, "qu_q", [P, 2, 3 * P])
        self.qp, self.sp = banks(nc, ctx, "qu_qp", 2), banks(nc, ctx, "qu_sp", 2)

    def tiles(self, n):
        return range(1) if n < PH else range(1, TT)

    def loads(self, sp, keys):
        sp.dma_start(self.keys[:, :, :], keys).then_inc(self.keys_loaded, 16)
        for n in range(2, self.STEPS):
            sp.wait_ge(self.product, 2 * n - 2)
            self.ring.order(sp, self.w, n % PH, n % 2)

    def queries(self, pe, n):
        nc, tiles = self.nc, self.tiles(n)
        width = len(tiles) * P
        w = self.w.shaped(self.ring.raw[n % 2])
        pe.wait_ge(self.ring.loaded[n % 2], 16 * (self.base + n // 2) + 16)
        for j in range(2):
            if n:
                pe.wait_ge(self.copied, 2 * n - 1 + j)
            for k in range(KD):
                last = nc.tensor.matmul(self.qp[j][:, 0:width], w[:, k, j * P:(j + 1) * P], self.h[:, k, tiles[0] * P:tiles[0] * P + width],
                                        start=(k == 0), stop=(k == KD - 1))
            last.then_inc(self.product, 1)

    def dots(self, pe, n):
        nc = self.nc
        if n == 0:
            pe.wait_ge(self.keys_loaded, 16)
        pe.wait_ge(self.copied, 2 * n + 2)
        for m, tile in enumerate(self.tiles(n)):
            if n or m == 2:
                pe.wait_ge(self.kept, self.kepts(n, m))
            for j in range(2):
                last = nc.tensor.matmul(self.sp[m % 2][:, j * P + m // 2 * 2 * P:(j + 1) * P + m // 2 * 2 * P], self.q[:, j, m * P:(m + 1) * P],
                                        self.keys[:, 2 * (n % PH) + j, :], start=True, stop=True)
            last.then_inc(self.scored, 1)

    def count(self, n):
        return n if n < PH else PH + 3 * (n - PH)

    def kepts(self, n, m):
        return self.count(n) + (1 if m == 2 else 0)

    def copy_queries(self, act, n):
        width = len(self.tiles(n)) * P
        for j in range(2):
            act.wait_ge(self.product, 2 * n + j + 1)
            if n:
                act.wait_ge(self.scored, self.count(n))
            self.nc.scalar.activation(self.q[:, j, 0:width], self.qp[j][:, 0:width], ACT.Copy).then_inc(self.copied, 1)

    def keep_scores(self, act, n):
        for m, tile in enumerate(self.tiles(n)):
            act.wait_ge(self.scored, self.count(n) + m + 1)
            at = 2 * (n % PH)
            self.nc.scalar.activation(self.scores[:, tile, at:at + 2, :],
                                      self.sp[m % 2][:, m // 2 * 2 * P:(m // 2 + 1) * 2 * P].rearrange("p (n k) -> p n k", n=2),
                                      ACT.Copy).then_inc(self.kept, 1)


class TopK:
    PIECES = 4
    HEADS = PH // PIECES

    def __init__(self, nc, core, ctx, scores, ids, gate):
        self.nc, self.core, self.scores, self.ids, self.gate = nc, core, scores, ids, gate
        self.step, self.shifted, self.expd, self.ids_ready = (nc.alloc_semaphore(f"tk_{n}") for n in ("step", "shifted", "expd", "ids_ready"))
        n = self.HEADS
        self.cd = sb(nc, ctx, "tk_cd", [P, n, 256])
        self.eq = sb(nc, ctx, "tk_eq", [P, n, 16, 16])
        self.vv = sb(nc, ctx, "tk_vv", [P, 2 * n, TOPK])
        self.ii = sb(nc, ctx, "tk_ii", [P, 2 * n, TOPK], U32)
        self.fi = sb(nc, ctx, "tk_fi", [P, 2 * n, TOPK])
        self.ts = sb(nc, ctx, "tk_ts", [P, n, TOPK])
        self.tp = sb(nc, ctx, "tk_tp", [P, n, TOPK], U32)
        self.hl = sb(nc, ctx, "tk_hl", [P, 2, n * TOPK], U32)
        self.hf = sb(nc, ctx, "tk_hf", [P, 2, n * TOPK])
        self.pick = sb(nc, ctx, "tk_pick", [P, 3, n * TOPK])
        self.ex = sb(nc, ctx, "tk_ex", [P, PH, TOPK])
        self.den = sb(nc, ctx, "tk_den", [P, 2, PH])
        self.then = None

    def top16(self, n, scores, values, index):
        nc, then = self.nc, self.then
        for r in range(n):
            last = nc.vector.max(values[:, r, 0:8], scores[:, r, :])
        then(last)
        for r in range(n):
            last = nc.vector.max_index(index[:, r, 0:8], values[:, r, 0:8], scores[:, r, :])
        then(last)
        for r in range(n):
            last = nc.vector.match_replace(scores[:, r, :], values[:, r, 0:8], scores[:, r, :], -3.0e38)
        then(last)
        for r in range(n):
            last = nc.vector.max(values[:, r, 8:16], scores[:, r, :])
        then(last)
        for r in range(n):
            last = nc.vector.max_index(index[:, r, 8:16], values[:, r, 8:16], scores[:, r, :])
        then(last)

    def lists(self, tile, p):
        n = self.HEADS
        self.top16(2 * n, self.scores[:, tile, 2 * n * p:2 * n * (p + 1), :], self.vv, self.ii)

    def choose(self, tile, p):
        nc, then, n = self.nc, self.then, self.HEADS
        pair = lambda ap, k: ap[:, :, :].rearrange("p (h two) k -> p h two k", two=2)[:, :, k, :]
        nc.vector.tensor_copy(self.fi[:, :, :], self.ii[:, :, :])
        then(nc.vector.tensor_tensor(self.cd[:, :, :].rearrange("p h (i j) -> p h i j", i=16),
                                     pair(self.vv, 0).unsqueeze(3).to_broadcast([P, n, 16, 16]),
                                     pair(self.vv, 1).unsqueeze(2).to_broadcast([P, n, 16, 16]), ALU.add))
        self.top16(n, self.cd, self.ts, self.tp)
        flat = self.tp[:, :, :].rearrange("p h k -> p (h k)")
        nc.vector.tensor_scalar(self.hl[:, 0, :], flat, 4, None, ALU.logical_shift_right)
        then(nc.vector.tensor_scalar(self.hl[:, 1, :], flat, 15, None, ALU.bitwise_and))
        then(nc.vector.tensor_copy(self.hf[:, :, :], self.hl[:, :, :]))
        for k in range(2):
            e3 = self.eq[:, :, :, :].rearrange("p h k i -> p (h k) i")
            then(nc.vector.tensor_tensor(e3, self.hf[:, k, :].unsqueeze(2).to_broadcast([P, n * TOPK, 16]),
                                         self.core.c[:, C_IOTA:C_IOTA + 16].unsqueeze(1).to_broadcast([P, n * TOPK, 16]), ALU.is_equal))
            then(nc.vector.tensor_tensor(self.eq[:, :, :, :], self.eq[:, :, :, :], pair(self.fi, k).unsqueeze(2).to_broadcast([P, n, 16, 16]), ALU.mult))
            then(nc.vector.tensor_reduce(self.pick[:, k, :], e3, AX.X, ALU.add))
        then(nc.vector.scalar_tensor_tensor(self.pick[:, 2, :], self.pick[:, 0, :], float(NK), self.pick[:, 1, :], ALU.mult, ALU.add))
        nc.vector.tensor_copy(self.ids[:, tile, n * TOPK * p:n * TOPK * (p + 1)], self.pick[:, 2, :]).then_inc(self.ids_ready, 1)
        nc.vector.tensor_tensor(self.ex[:, n * p:n * (p + 1), :], self.ts[:, :, :], self.ts[:, :, 0:1].to_broadcast([P, n, TOPK]),
                                ALU.subtract).then_inc(self.shifted, 1)

    def gates(self, dve, tile):
        nc, then = self.nc, self.then
        dve.wait_ge(self.expd, tile + 1)
        then(nc.vector.tensor_reduce(self.den[:, 0, :], self.ex[:, :, :], AX.X, ALU.add))
        then(nc.vector.reciprocal(self.den[:, 1, :], self.den[:, 0, :]))
        then(nc.vector.tensor_tensor(self.gate[:, tile, :].rearrange("p (h k) -> p h k", h=PH), self.ex[:, :, :],
                                     self.den[:, 1, :].unsqueeze(2).to_broadcast([P, PH, TOPK]), ALU.mult))

    def exp(self, act, tile):
        act.wait_ge(self.shifted, self.PIECES * (tile + 1))
        self.nc.scalar.activation(self.ex[:, :, :], self.ex[:, :, :], ACT.Exp).then_inc(self.expd, 1)


RING = 4
ROUNDS = SLOTS // (2 * RING)
QUARTER = ROUNDS // TopK.PIECES
PIECE_AT = [5, 8, 11, 13]
GATES_AT = ROUNDS - 1
EARLY = PH // 2
QUERY_AT = [2, 4, 6, 8]


def segments(tile):
    ends = sorted({*PIECE_AT, *(r + 1 for r in PIECE_AT), GATES_AT, ROUNDS, *(QUERY_AT if tile == 0 else ())})
    return list(zip([0, *ends], ends))


def stage_experts(nc, core, xn, h, gain, keys, scores, ids, gate, u_emb, v_emb, out):
    sem = lambda n: nc.alloc_semaphore(f"ex_{n}")
    two = lambda n: [sem(f"{n}{i}") for i in range(2)]
    staged, u_in, v_in, dotted, gelud, weighed, spread, mixed = map(
        two, ("staged", "u_loaded", "v_loaded", "dotted", "gelud", "weighed", "spread", "mixed"))
    gained, zeroed, opened, closed, copied, stored, gloaded, passed = map(sem, (
        "gained", "zeroed", "opened", "closed", "copied", "stored", "gain_loaded", "wait_passed"))
    ident = core.c[:, C_IDENT:C_IDENT + P]
    with ExitStack() as ctx:
        query = Query(nc, core, ctx, h, scores)
        topk = TopK(nc, core, ctx, scores, ids, gate)
        ur = [[sb(nc, ctx, f"ex_u{b}_{r}", [P, D]) for r in range(RING)] for b in range(2)]
        vr = [[sb(nc, ctx, f"ex_v{b}_{r}", [P, D]) for r in range(RING)] for b in range(2)]
        stg = [[sb(nc, ctx, f"ex_stage{b}_{s}", [P, RING], U32) for s in "uv"] for b in range(2)]
        dot, gel, wgt = ([sb(nc, ctx, f"ex_{n}{b}", [P, RING]) for b in range(2)] for n in ("dot", "gel", "wgt"))
        diag = [sb(nc, ctx, f"ex_diag{b}", [P, RING, P]) for b in range(2)]
        zero = sb(nc, ctx, "ex_zero", [P, P])
        gb = ur[1][RING - 1][:, :]
        ob = core.ring.raw[1][:, 0:D]
        acc = [[ctx.enter_context(nc.psum_tensor(f"ex_acc{b}{i}", [P, 512], F32)) for i in range(2)] for b in range(2)]
        block = ctx.enter_context(nc.Block())
        at = lambda tile, i: tile * ROUNDS + i

        @block.sync
        def _(sp):
            sp.dma_start(gb, gain.partition_broadcast(P)).then_inc(gloaded, 16)
            query.loads(sp, keys)
            for tile in range(TT):
                sp.wait_ge(copied, tile + 1)
                sp.dma_start(out[tile * P:(tile + 1) * P, :], ob).then_inc(stored, 16)
            sp.wait_ge(stored, 16 * TT)

        @block.gpsimd
        def _(pool):
            for tile in range(TT):
                for quarter in range(TopK.PIECES):
                    pool.wait_ge(topk.ids_ready, TopK.PIECES * tile + quarter + 1)
                    pool.sem_inc(passed, 1)
                    with pool.Fori(quarter * QUARTER, (quarter + 1) * QUARTER) as i:
                        for b in range(2):
                            for s, (free, rows, table, loaded) in enumerate(((dotted, ur, u_emb, u_in), (mixed, vr, v_emb, v_in))):
                                pool.wait_ge(free[b], at(tile, i) + 1)
                                pool.sem_inc(passed, 1)
                                nc.gpsimd.tensor_copy(stg[b][s][:, :], ids[:, tile, bass.ds(i * 2 * RING + b * RING, RING)]).then_inc(staged[b], 1)
                                pool.wait_ge(staged[b], at(tile, i) * 2 + s + 1)
                                pool.sem_inc(passed, 1)
                                for r in range(RING):
                                    nc.gpsimd.indirect_dma_start(out=rows[b][r][:, :], out_offset=None, in_=table,
                                                                 in_offset=bass.IndirectOffsetOnAxis(ap=stg[b][s][:, r:r + 1], axis=0)).then_inc(loaded[b], 16)

        @block.vector
        def _(dve):
            for b in range(2):
                dve.sem_inc(dotted[b], 1)
            nc.vector.memset(zero[:, :], 0.0).then_inc(zeroed, 1)
            dve.wait_ge(gloaded, 16)
            for tile in range(TT):
                last = nc.vector.tensor_tensor(xn[:, tile, :], xn[:, tile, :], gb, ALU.mult)
            last.then_inc(gained, 1)
            dve.wait_ge(gained, 1)
            topk.then = Chain(dve, topk.step)
            for p in range(TopK.PIECES):
                dve.wait_ge(query.kept, (p + 1) * TopK.HEADS)
                topk.lists(0, p)
                topk.choose(0, p)
            topk.gates(dve, 0)
            for tile in range(TT):
                for start, end in segments(tile):
                    with dve.Fori(start, end) as i:
                        for b in range(2):
                            dve.wait_ge(u_in[b], (at(tile, i) + 1) * 16 * RING)
                            for r in range(RING):
                                last = nc.vector.tensor_tensor_reduce(ur[b][r][:, :], ur[b][r][:, :], xn[:, tile, :], 1.0, 0.0,
                                                                      ALU.mult, ALU.add, dot[b][:, r:r + 1])
                            last.then_inc(dotted[b], 1)
                            dve.wait_ge(gelud[b], at(tile, i) + 1)
                            nc.vector.tensor_tensor(wgt[b][:, :], gel[b][:, :], gate[:, tile, bass.ds(i * 2 * RING + b * RING, RING)],
                                                    ALU.mult).then_inc(weighed[b], 1)
                    if tile + 1 < TT:
                        if end in PIECE_AT:
                            p = PIECE_AT.index(end)
                            if tile == 0:
                                dve.wait_ge(query.kept, query.count(PH + (p + 1) * TopK.HEADS))
                            topk.lists(tile + 1, p)
                        elif end - 1 in PIECE_AT:
                            topk.choose(tile + 1, PIECE_AT.index(end - 1))
                        if end == GATES_AT:
                            topk.gates(dve, tile + 1)

        @block.scalar
        def _(act):
            def rounds(tile, start, end):
                with act.Fori(start, end) as i:
                    for b in range(2):
                        act.wait_ge(dotted[b], at(tile, i) + 2)
                        nc.scalar.activation(gel[b][:, :], dot[b][:, :], ACT.Gelu).then_inc(gelud[b], 1)
                        act.wait_ge(weighed[b], at(tile, i) + 1)
                        act.wait_ge(mixed[b], at(tile, i) + 1)
                        for r in range(RING):
                            last = nc.scalar.activation(diag[b][:, r, :], ident, ACT.Copy, scale=wgt[b][:, r:r + 1])
                        last.then_inc(spread[b], 1)

            for n in range(PH):
                query.copy_queries(act, n)
                if n:
                    query.keep_scores(act, n - 1)
            query.keep_scores(act, PH - 1)
            for n in range(PH, PH + EARLY):
                query.copy_queries(act, n)
                query.keep_scores(act, n)
            topk.exp(act, 0)
            for tile in range(TT):
                for start, end in segments(tile):
                    rounds(tile, start, end)
                    if tile == 0 and end in QUERY_AT:
                        n = PH + EARLY + QUERY_AT.index(end)
                        if n > PH + EARLY:
                            query.keep_scores(act, n - 1)
                        query.copy_queries(act, n)
                        if n == 2 * PH - 1:
                            query.keep_scores(act, n)
                    if tile + 1 < TT and end == GATES_AT:
                        topk.exp(act, tile + 1)
                act.wait_ge(closed, tile + 1)
                if tile:
                    act.wait_ge(stored, 16 * tile)
                for half in range(2):
                    last = nc.scalar.activation(ob[:, half * 512:(half + 1) * 512], acc[tile % 2][half][:, :], ACT.Copy)
                last.then_inc(copied, 1)

        @block.tensor
        def _(pe):
            for b in range(2):
                pe.sem_inc(mixed[b], 1)
            for n in range(PH):
                query.queries(pe, n)
                if n:
                    query.dots(pe, n - 1)
            query.dots(pe, PH - 1)
            for n in range(PH, PH + EARLY):
                query.queries(pe, n)
                query.dots(pe, n)
            pe.wait_ge(zeroed, 1)
            for tile in range(TT):
                if tile >= 2:
                    pe.wait_ge(copied, tile - 1)
                for half in range(2):
                    nc.tensor.matmul(acc[tile % 2][half][:, :], ident, core.x[:, tile, half * 512:(half + 1) * 512], start=True, stop=False,
                                     skip_group_check=True)
                for start, end in segments(tile):
                    with pe.Fori(start, end) as i:
                        for b in range(2):
                            pe.wait_ge(v_in[b], (at(tile, i) + 1) * 16 * RING)
                            pe.wait_ge(spread[b], at(tile, i) + 1)
                            for r in range(RING):
                                for half in range(2):
                                    last = nc.tensor.matmul(acc[tile % 2][half][:, :], diag[b][:, r, :], vr[b][r][:, half * 512:(half + 1) * 512],
                                                            start=False, stop=False, skip_group_check=True)
                            last.then_inc(mixed[b], 1)
                    if tile == 0 and end in QUERY_AT:
                        n = PH + EARLY + QUERY_AT.index(end)
                        query.queries(pe, n)
                        if n > PH + EARLY:
                            query.dots(pe, n - 1)
                        if n == 2 * PH - 1:
                            query.dots(pe, n)
                for half in range(2):
                    last = nc.tensor.matmul(acc[tile % 2][half][:, :], zero[:, :], core.x[:, tile, half * 512:(half + 1) * 512],
                                            start=False, stop=True, skip_group_check=True)
                last.then_inc(closed, 1)


def peer(nc, core, a, out):
    with ExitStack() as ctx:
        xn = sb(nc, ctx, "xn", [P, TT, D])
        h = sb(nc, ctx, "h3_t", [P, KD, T])
        ids = sb(nc, ctx, "expert_ids", [P, TT, SLOTS], U32)
        gate = sb(nc, ctx, "expert_gates", [P, TT, SLOTS])
        scores = sb(nc, ctx, "scores", [P, TT, 2 * PH, NK])
        stage_norm(nc, core, "nf", x_tiles(core), V_NORMF, None, natural=lambda i: xn[:, i, :], whole=h)
        stage_experts(nc, core, xn, h, a["norm_ffn_2"], a["keys"], scores, ids, gate, a["peer_u"], a["peer_v"], out)


def build(nc, a, scratch, out):
    with ExitStack() as stack:
        core = open_core(nc, stack, a)
        stage_load(nc, core, a)
        for part in (lambda: delta_block(nc, core, a), lambda: window_block(nc, core, a, scratch), lambda: mixers(nc, core, a), lambda: peer(nc, core, a, out)):
            before = nc.snapshot_sems()
            part()
            nc.clear_and_free_semaphores(nc.allocated_since(before))
            nc.all_engine_barrier()


def _columns(v):
    return np.reshape(v, (KD, P)).T


def _layout(i):
    consts, rows = shape_constants()
    v = np.zeros((P, V_WIDTH), np.float32)
    for name, at in (("a_norm", V_ANORM), ("kv_norm", V_KVNORM), ("b_norm", V_BNORM), ("norm_mix_2", V_NORM2), ("norm_ffn_2", V_NORMF)):
        v[:, at:at + KD] = _columns(i[name])
    for name, at in (("b_q_gain", V_QGK), ("k_gain", V_QGK + 1), ("f_q_norm_2", V_FQK), ("f_k_norm_2", V_FQK + 1)):
        v[0:HD, at] = v[HD:P, at] = np.reshape(i[name], HD)
    v[32:32 + HA, V_ALOG] = i["a_A_log"][0]
    v[32:32 + HA, V_DT] = i["a_dt_bias"][0]
    v[0:HM, V_BI] = i["b_igate_2"][0]
    v[32:32 + HM, V_BI] = i["b_fgate_m_2"][0]
    v[64:64 + HF, V_BI] = i["b_fgate_f_2"][0]
    taps = lambda w: np.transpose(np.reshape(w, (4, -1, P)), (2, 1, 0))
    return {
        "c128": consts, "c32": rows, "v128": v, "x": i["x"][0], "meta": i["meta_tokens_2"],
        "a_w_in": i["a_w_in"][0], "a_conv": taps(i["a_conv"][0]), "a_o_gain": i["a_o_gain"][0], "a_w_out": i["a_w_out"][0],
        "w_kv": i["w_kv"], "rel_bias": i["rel_bias"], "b_w_in": i["b_w_in"][0], "b_sinks": i["b_sinks"][0], "b_w_out": i["b_w_out"][0],
        "w_in_2": i["w_in_2"][0], "conv_qk_2": taps(i["conv_qk_2"][0]), "m_out_norm_2": i["m_out_norm_2"][0], "w_out_2": i["w_out_2"][0],
        "norm_ffn_2": i["norm_ffn_2"][0], "peer_query": i["peer_query_2"][0],
        "keys": np.transpose(np.reshape(i["peer_sub_keys_2"][0], (2 * PH, NK, P)), (2, 0, 1)),
        "peer_u": i["peer_u_2"][0], "peer_v": i["peer_v_2"][0],
    }


def kernel(**inputs):
    import concourse.bacc as bacc
    from concourse.bass_utils import run_bass_kernel_spmd

    nc = bacc.Bacc("TRN2", target_bir_lowering=False, num_devices=1)
    arrays, a = {}, {}
    for name, value in _layout({k: np.asarray(v) for k, v in inputs.items()}).items():
        arrays[f"in_{name}"] = np.ascontiguousarray(value)
        a[name] = nc.dram_tensor(f"in_{name}", value.shape, F32, kind="ExternalInput").ap()
    scratch = nc.dram_tensor("bias_rows", (HB, 384), F32, kind="Internal").ap()
    out = nc.dram_tensor("out_0", (T, D), F32, kind="ExternalOutput").ap()
    build(nc, a, scratch, out)
    r = run_bass_kernel_spmd(nc, [arrays], core_ids=[0])
    return r.results[0]["out_0"].reshape(1, T, D)
```

```python
from contextlib import ExitStack, contextmanager, nullcontext

import numpy as np

import concourse.bass as bass
from concourse import mybir

F32 = mybir.dt.float32
U32 = mybir.dt.uint32
F32R = mybir.dt.float32r
ACT = mybir.ActivationFunctionType
ALU = mybir.AluOpType
AX = mybir.AxisListType

P = 128
D = 1024
KD = D // P
T = 512
TT = T // P
EPS = 1e-6
NEG = -1e30

HA, DK, DV = 8, 128, 256
QKV_TILES = (2 * HA * DK + HA * DV) // P
HB, KVB, HD = 32, 4, 64
META = 16
T2 = T + META
HM, DM = 4, 128
HF, DF = 8, 64
PH, NK, TOPK = 8, 128, 16
SLOTS = PH * TOPK

C_IDENT, C_ONES, C_HALVES, C_LE, C_LEVEL = 0, 128, 256, 384, 512
LEVELS = 7
C_NEGDIAG = C_LEVEL + LEVELS * P
C_PAIR = C_NEGDIAG + P
C_IOTA = C_PAIR + 2
C_MHALF = C_IOTA + 16
C_FLIP = C_MHALF + 1
C_COLUMN = C_FLIP + P
C_WIDTH = C_COLUMN + HA * HA
R_SEL, R_BUCKET, R_WINDOW = 0, 8 * P, 8 * P + 384
R_WIDTH = R_WINDOW + 384
R_KEPT = R_BUCKET
(V_ANORM, V_KVNORM, V_BNORM, V_NORM2, V_NORMF) = (0, 8, 16, 24, 32)
V_QGK = 40
V_FQK = 42
V_ALOG, V_DT, V_BI = 44, 45, 46
V_WIDTH = 47


def shape_constants():
    c = np.zeros((P, C_WIDTH), np.float32)
    s, t = np.arange(P)[:, None], np.arange(P)[None, :]
    c[:, C_IDENT:C_IDENT + P] = s == t
    c[:, C_ONES:C_ONES + P] = 1
    c[:, C_HALVES:C_HALVES + P] = s // 64 == t // 64
    c[:, C_LE:C_LE + P] = s <= t
    for n in range(LEVELS):
        b = 1 << n
        c[:, C_LEVEL + n * P:C_LEVEL + (n + 1) * P] = (s // (2 * b) == t // (2 * b)) & (s % (2 * b) < b) & (t % (2 * b) >= b)
    c[:, C_NEGDIAG:C_NEGDIAG + P] = np.where(t <= s, 0, NEG)
    c[:, C_PAIR:C_PAIR + 2] = s // 64 == np.arange(2)[None, :]
    c[:, C_IOTA:C_IOTA + 16] = np.arange(16)[None, :]
    c[:, C_MHALF] = -0.5
    c[:, C_FLIP:C_FLIP + P] = s + t == P - 1
    c[:, C_COLUMN:C_COLUMN + HA * HA] = np.eye(HA).reshape(1, HA * HA)
    r = np.zeros((32, R_WIDTH), np.float32)
    for h in range(8):
        r[h, R_SEL + h * P:R_SEL + (h + 1) * P] = 1
    dist = 255 - np.arange(384)
    n = np.maximum(dist, 0)
    large = 16 + (np.log(np.maximum(n, 1) / 16) / np.log(128 / 16) * 16).astype(np.int64)
    bucket = np.where(n < 16, n, np.minimum(large, 31))
    r[:, R_BUCKET:R_BUCKET + 384] = np.arange(32)[:, None] == bucket[None, :]
    r[:, R_WINDOW:R_WINDOW + 384] = np.where((dist >= 0) & (dist < 128), 0, NEG)
    return c, r


class Chain:

    def __init__(self, eng, sem, base=0):
        self.eng, self.sem, self.base, self.n = eng, sem, base, 0

    def __call__(self, ins):
        ins.then_inc(self.sem, 1)
        self.n += 1
        self.eng.wait_ge(self.sem, self.base + self.n)


class Marks:

    def __init__(self, eng, sem):
        self.eng, self.sem, self.n = eng, sem, 0

    def mark(self, ins):
        ins.then_inc(self.sem, 1)
        self.n += 1
        return self.n

    def after(self, step):
        self.eng.wait_ge(self.sem, step)


class Core:

    def __init__(self, nc, stack):
        self.nc, self.stack = nc, stack

    shared = None

    def keep(self, name, shape, dt=F32):
        return self.stack.enter_context(self.nc.sbuf_tensor(name, shape, dt))

    @contextmanager
    def together(self):
        with ExitStack() as ctx:
            self.shared = ctx, ctx.enter_context(self.nc.Block())
            yield
            self.shared = None

    def stage(self):
        return ExitStack() if self.shared is None else nullcontext(self.shared[0])

    def open_block(self, ctx):
        return ctx.enter_context(self.nc.Block()) if self.shared is None else self.shared[1]


def sb(nc, ctx, name, shape, dt=F32, side=None):
    return ctx.enter_context(nc.sbuf_tensor(name, shape, dt, side=side))


def sb_parts(nc, ctx, name, shape, side=None):
    return [sb(nc, ctx, f"{name}_{part}", shape, F32R, side) for part in ("hi", "lo")]


def matmul_parts(nc, out, lhs, rhs, start, stop):
    nc.tensor.matmul(out, lhs[0], rhs[0], start=start, stop=False)
    nc.tensor.matmul(out, lhs[0], rhs[1], start=False, stop=False)
    return nc.tensor.matmul(out, lhs[1], rhs[0], start=False, stop=stop)


def banks(nc, ctx, name, n):
    return [ctx.enter_context(nc.psum_tensor(f"{name}{i}", [P, 512], F32)) for i in range(n)]


def stage_load(nc, core, a):
    loaded = nc.alloc_semaphore("loaded")
    with nc.Block() as block:
        @block.sync
        def _(sp):
            sp.dma_start(core.c[:, :], a["c128"]).then_inc(loaded, 16)
            sp.dma_start(core.r[:, :], a["c32"][:, 0:R_KEPT]).then_inc(loaded, 16)
            sp.dma_start(core.v[:, :], a["v128"]).then_inc(loaded, 16)
            sp.dma_start(core.x[:, :, :], a["x"].rearrange("(i p) d -> p i d", p=P)).then_inc(loaded, 16)
            sp.dma_start(core.ta[:, :, :], a["a_conv"]).then_inc(loaded, 16)
            sp.dma_start(core.tm[:, :, :], a["conv_qk_2"]).then_inc(loaded, 16)
            core.ring.first(sp)
            sp.wait_ge(loaded, 96)

        @block.vector
        def _(dve):
            nc.vector.memset(core.eps[:, 0:1], EPS)
            nc.vector.memset(core.eps[:, 1:2], 64 * EPS)


def stage_norm(nc, core, tag, tiles, gain, h_t, natural=None, whole=None):
    sem = lambda n: nc.alloc_semaphore(f"{tag}_{n}")
    squared, meaned, rooted, scaled, turned, stored, hi_ready, split, own_squared = map(sem, (
        "squared", "meaned", "rooted", "scaled", "turned", "stored", "hi_ready", "split", "vector_squared"))
    ident = core.c[:, C_IDENT:C_IDENT + P]
    n = len(tiles)
    with core.stage() as ctx:
        junk = sb(nc, ctx, f"{tag}_junk", [P, D])
        ss = sb(nc, ctx, f"{tag}_ss", [P, 3, n])
        xn = sb(nc, ctx, f"{tag}_xn", [P, 2, D]) if natural is None else None
        ring = sb(nc, ctx, f"{tag}_full", [P, 2, 4 * P]) if whole is None else None
        own_junk = (ring[:, :, :] if whole is None else whole[:, 0:2, :]).rearrange("p a t -> p (a t)")
        ps = banks(nc, ctx, f"{tag}_ps", 4)
        block = core.open_block(ctx)

        def full(b):
            rows, col = tiles[b // 2][1:]
            if whole is not None:
                return whole[:, 4 * (b % 2):4 * (b % 2) + 4, col:col + rows]
            return ring[:, b % 2, 0:4 * rows].rearrange("p (k t) -> p k t", k=4)
        where = [natural(i) if natural else xn[0:tiles[i][1], i % 2, :] for i in range(n)]

        @block.scalar
        def _(act):
            for i in range(0, n, 2):
                x, rows, _c = tiles[i]
                if i:
                    act.wait_ge(squared, i // 2)
                nc.scalar.activation(junk[0:rows, :], x, ACT.Square, accum_out=ss[0:rows, 0, i:i + 1]).then_inc(squared, 1)
            def hi_part(b):
                if h_t is None:
                    return
                rows, col = tiles[b // 2][1:]
                act.wait_ge(stored, b + 1)
                nc.scalar.activation(h_t[0][:, 4 * (b % 2):4 * (b % 2) + 4, col:col + rows],
                                     full(b), ACT.Copy).then_inc(hi_ready, 1)

            for i, (x, rows, _c) in enumerate(tiles):
                act.wait_ge(rooted, i + 1)
                if natural is None and i >= 2:
                    act.wait_ge(turned, 2 * (i - 1))
                nc.scalar.activation(where[i], x, ACT.Copy, scale=ss[0:rows, 2, i:i + 1]).then_inc(scaled, 1)
                if i:
                    hi_part(2 * i - 2)
                    hi_part(2 * i - 1)
            hi_part(2 * n - 2)
            hi_part(2 * n - 1)

        @block.gpsimd
        def _(pool):
            for i, (x, rows, _c) in enumerate(tiles):
                pool.wait_ge(meaned, i + 1)
                nc.gpsimd.tensor_tensor(ss[0:rows, 2, i:i + 1], ss[0:rows, 1, i:i + 1],
                                        core.c[0:rows, C_MHALF:C_MHALF + 1], ALU.pow).then_inc(rooted, 1)

        @block.tensor
        def _(pe):
            for i, (x, rows, _c) in enumerate(tiles):
                pe.wait_ge(scaled, i + 1)
                for half in range(2):
                    b = 2 * i + half
                    if b >= 4:
                        pe.wait_ge(stored, b - 3)
                    for k in range(4):
                        d = (4 * half + k) * P
                        last = nc.tensor.transpose(ps[b % 4][:, k * rows:(k + 1) * rows], where[i][:, d:d + P], ident[0:rows, 0:rows])
                    last.then_inc(turned, 1)

        @block.vector
        def _(dve):
            for i, (x, rows, _c) in enumerate(tiles):
                if i % 2 == 0 and i + 1 < n:
                    odd, odd_rows, _ = tiles[i + 1]
                    if i:
                        dve.wait_ge(own_squared, i // 2)
                    nc.vector.tensor_tensor_reduce(own_junk[0:odd_rows, :], odd, odd, 1.0, 0.0, ALU.mult, ALU.add,
                                                   ss[0:odd_rows, 0, i + 1:i + 2]).then_inc(own_squared, 1)
                dve.wait_ge(own_squared if i % 2 else squared, i // 2 + 1)
                nc.vector.tensor_scalar(ss[0:rows, 1, i:i + 1], ss[0:rows, 0, i:i + 1], 1.0 / D, EPS, ALU.mult, ALU.add).then_inc(meaned, 1)
            def lo_part(b):
                if h_t is None:
                    return
                rows, col = tiles[b // 2][1:]
                where = (slice(None), slice(4 * (b % 2), 4 * (b % 2) + 4), slice(col, col + rows))
                dve.wait_ge(hi_ready, b + 1)
                nc.vector.tensor_tensor(h_t[1][where], full(b),
                                        h_t[0][where].bitcast(F32), ALU.subtract).then_inc(split, 1)

            for b in range(2 * n):
                rows = tiles[b // 2][1]
                k0 = 4 * (b % 2)
                dve.wait_ge(turned, b + 1)
                if b >= 2 and whole is None:
                    dve.wait_ge(split, b - 1)
                nc.vector.tensor_tensor(full(b),
                                        ps[b % 4][:, 0:4 * rows].rearrange("p (k t) -> p k t", k=4),
                                        core.v[:, gain + k0:gain + k0 + 4].unsqueeze(2).to_broadcast([P, 4, rows]),
                                        ALU.mult).then_inc(stored, 1)
                if b:
                    lo_part(b - 1)
            lo_part(2 * n - 1)


def x_tiles(core):
    return [(core.x[:, i, :], P, i * P) for i in range(TT)]


def w_view(w, kt):
    return w.rearrange("(k p) n -> p k n", p=P)


class Weights:

    def __init__(self, w, kt, n0=None, chunks=None, groups=None):
        self.view, self.n0, self.groups, self.parts = w_view(w, kt), n0, groups, kt // 4
        self.k, self.n = (KD, 256) if groups is None else (4, 512)
        self.chunks = chunks if groups is None else len(groups) * self.parts

    def source(self, c):
        if self.groups is None:
            return self.view[:, :, bass.ds(self.n0 + 256 * c, 256)]
        group, part = divmod(c, self.parts)
        return self.view[:, 4 * part:4 * part + 4, self.groups[group]:self.groups[group] + 512]

    def shaped(self, chunk):
        return chunk[:, :].rearrange("p (k n) -> p k n", k=self.k)


class Ring:

    def __init__(self, nc, core, plan):
        self.raw = [core.keep(f"weights_raw{b}", [P, 2048]) for b in range(2)]
        self.loaded = [nc.alloc_semaphore(f"weights_loaded{b}") for b in range(2)]
        self.plan, self.at, self.filled = plan, -1, 0

    def order(self, sp, w, c, b):
        sp.dma_start(w.shaped(self.raw[b]), w.source(c)).then_inc(self.loaded[b], 16)

    def first(self, sp):
        for b in range(2):
            self.order(sp, self.plan[0], b, b)

    def take(self):
        if self.at >= 0:
            self.filled += self.plan[self.at].chunks // 2
        self.at += 1
        return self.plan[self.at]


class Split:

    POOL = 512

    def __init__(self, nc, core, ctx, tag, shared_opening=False):
        self.nc, self.ring, self.w = nc, core.ring, core.ring.take()
        self.base = self.ring.filled
        self.after = self.ring.plan[self.ring.at + 1] if self.ring.at + 1 < len(self.ring.plan) else None
        self.hi, self.lo = ([sb(nc, ctx, f"{tag}_w_{part}{b}", [P, 2048], F32R) for b in range(2)] for part in ("hi", "lo"))
        self.hi_ready, self.ready = nc.alloc_semaphore(f"{tag}_w_hi"), nc.alloc_semaphore(f"{tag}_w_split")
        self.opened, self.opened_hi = (nc.alloc_semaphore(f"{tag}_w_opened"), nc.alloc_semaphore(f"{tag}_w_opened_hi")) if shared_opening else (None, None)

    def parts(self, b):
        return self.w.shaped(self.hi[b]), self.w.shaped(self.lo[b])

    def loads(self, sp):
        w = self.w
        if self.opened is not None:
            sp.wait_ge(self.opened, 2)
        if w.groups is None and w.chunks > 2:
            with sp.Fori(1, w.chunks // 2) as i:
                for b in range(2):
                    sp.wait_ge(self.ready, 2 * i + b - 1)
                    self.ring.order(sp, w, 2 * i + b, b)
        else:
            for c in range(2, w.chunks):
                sp.wait_ge(self.ready, c - 1)
                self.ring.order(sp, w, c, c % 2)
        if self.after is not None:
            for b in range(2):
                sp.wait_ge(self.ready, w.chunks - 1 + b)
                self.ring.order(sp, self.after, b, b)

    def split_hi(self, eng, i, b):
        eng.wait_ge(self.ring.loaded[b], 16 * (self.base + i) + 16)
        if eng is self.nc.scalar:
            self.nc.scalar.activation(self.hi[b][:, :], self.ring.raw[b][:, :], ACT.Copy).then_inc(self.hi_ready, 1)
        else:
            self.nc.vector.tensor_copy(self.hi[b][:, :], self.ring.raw[b][:, :]).then_inc(self.hi_ready, 1)

    def open_scalar(self, act):
        act.wait_ge(self.ring.loaded[0], 16 * self.base + 16)
        self.nc.scalar.activation(self.hi[0][:, 0:self.POOL], self.ring.raw[0][:, 0:self.POOL], ACT.Copy).then_inc(self.opened_hi, 1)

    def open_vector(self, dve):
        rest = slice(self.POOL, 2048)
        dve.wait_ge(self.ring.loaded[0], 16 * self.base + 16)
        self.nc.vector.tensor_copy(self.hi[0][:, rest], self.ring.raw[0][:, rest]).then_inc(self.opened, 1)
        dve.wait_ge(self.opened, 1)
        self.nc.vector.tensor_tensor(self.lo[0][:, rest], self.ring.raw[0][:, rest], self.hi[0][:, rest].bitcast(F32),
                                     ALU.subtract).then_inc(self.opened, 1)

    def split_lo(self, pool):
        def one(b, cols=slice(0, 2048)):
            self.nc.gpsimd.tensor_tensor(self.lo[b][:, cols], self.ring.raw[b][:, cols], self.hi[b][:, cols].bitcast(F32),
                                         ALU.subtract).then_inc(self.ready, 1)
        start = 0
        if self.opened is not None:
            pool.wait_ge(self.opened_hi, 1)
            one(0, slice(0, self.POOL))
            pool.wait_ge(self.hi_ready, 1)
            one(1)
            start = 1
        if self.w.chunks // 2 > start:
            with pool.Fori(start, self.w.chunks // 2) as i:
                for b in range(2):
                    pool.wait_ge(self.hi_ready, 2 * i + b + 1 - start)
                    one(b)

    def wait_opened(self, pe):
        if self.opened is not None:
            pe.wait_ge(self.opened, 2)


def products_t(nc, pe, split, h_t, spans, ps, done, free):
    ns = len(spans)
    split.wait_opened(pe)
    with pe.Fori(0, split.w.chunks // 2) as i:
        for b in range(2):
            pe.wait_ge(split.ready, 2 * i + b + 1)
            hi, lo = split.parts(b)
            for j in range(2):
                for si, (c0, cw) in enumerate(spans):
                    u = (b * 2 + j) * ns + si
                    pe.wait_ge(free, i * 4 * ns + u + 1)
                    for k in range(KD):
                        last = matmul_parts(nc, ps[u % 4][:, 0:cw], (hi[:, k, j * P:(j + 1) * P], lo[:, k, j * P:(j + 1) * P]),
                                            (h_t[0][:, k, c0:c0 + cw], h_t[1][:, k, c0:c0 + cw]), k == 0, k == KD - 1)
                    last.then_inc(done, 1)


def stage_proj_t(nc, core, tag, h_t, out, spans):
    done, free = (nc.alloc_semaphore(f"{tag}_{n}") for n in ("product", "bank_free"))
    ns = len(spans)
    with core.stage() as ctx:
        split = Split(nc, core, ctx, tag, shared_opening=True)
        pairs = split.w.chunks // 2
        ps = banks(nc, ctx, f"{tag}_ps", 4)
        block = core.open_block(ctx)

        @block.sync
        def _(sp):
            split.loads(sp)

        @block.gpsimd
        def _(pool):
            split.split_lo(pool)

        @block.tensor
        def _(pe):
            products_t(nc, pe, split, h_t, spans, ps, done, free)

        @block.vector
        def _(dve):
            split.open_vector(dve)
            split.split_hi(dve, 0, 1)
            if pairs > 1:
                with dve.Fori(1, pairs) as i:
                    for b in range(2):
                        dve.wait_ge(done, i * 4 * ns + (b - 1) * 2 * ns)
                        split.split_hi(dve, i, b)

        @block.scalar
        def _(act):
            act.sem_inc(free, 4)
            split.open_scalar(act)
            with act.Fori(0, pairs) as i:
                for j in range(4):
                    for si, (c0, cw) in enumerate(spans):
                        u = j * ns + si
                        act.wait_ge(done, i * 4 * ns + u + 1)
                        nc.scalar.activation(out[:, bass.ds(i * 4 + j, 1), c0:c0 + cw],
                                             ps[u % 4][:, 0:cw].unsqueeze(1), ACT.Copy).then_inc(free, 1)


def stage_proj_conv(nc, core, tag, h_t, taps, out, spans, width, shared_opening=True):
    done, free, conved, step, zeroed, activated = (
        nc.alloc_semaphore(f"{tag}_{n}") for n in ("product", "bank_free", "conved", "conv_step", "zeroed", "activated"))
    ns = len(spans)
    with core.stage() as ctx:
        split = Split(nc, core, ctx, tag, shared_opening)
        pairs = split.w.chunks // 2
        xp = sb(nc, ctx, f"{tag}_xp", [P, 2, 3 + width])
        y = sb(nc, ctx, f"{tag}_y", [P, 2, width])
        ps = banks(nc, ctx, f"{tag}_ps", 4)
        block = core.open_block(ctx)

        @block.sync
        def _(sp):
            split.loads(sp)

        @block.gpsimd
        def _(pool):
            split.split_lo(pool)

        @block.tensor
        def _(pe):
            products_t(nc, pe, split, h_t, spans, ps, done, free)

        @block.scalar
        def _(act):
            def tiles(i, last):
                for j in range(4):
                    for si, (c0, cw) in enumerate(spans):
                        u = j * ns + si
                        act.wait_ge(done, i * 4 * ns + u + 1)
                        if si == 0:
                            act.wait_ge(conved, i * 4 + j + 1)
                        nc.scalar.activation(xp[:, j % 2, 3 + c0:3 + c0 + cw], ps[u % 4][:, 0:cw], ACT.Copy).then_inc(free, 1)
                    if j % 2 and not last:
                        split.split_hi(act, i + 1, j // 2)
                    act.wait_ge(conved, i * 4 + j + 3)
                    nc.scalar.activation(out[:, bass.ds(i * 4 + j, 1), :], y[:, j % 2:j % 2 + 1, :], ACT.Silu).then_inc(activated, 1)

            act.sem_inc(free, 4)
            if shared_opening:
                split.open_scalar(act)
            else:
                split.split_hi(act, 0, 0)
            split.split_hi(act, 0, 1)
            act.wait_ge(zeroed, 1)
            if pairs > 1:
                with act.Fori(0, pairs - 1) as i:
                    tiles(i, False)
            tiles(pairs - 1, True)

        @block.vector
        def _(dve):
            dve.sem_inc(conved, 2)
            dve.sem_inc(activated, 2)
            if shared_opening:
                split.open_vector(dve)
            nc.vector.memset(xp[:, :, 0:3], 0.0).then_inc(zeroed, 1)
            with dve.Fori(0, pairs) as i:
                for j in range(4):
                    tap = lambda k: taps[:, bass.ds(i * 4 + j, 1), k]
                    row, to = xp[:, j % 2, :], y[:, j % 2, :]
                    dve.wait_ge(free, 4 + i * 4 * ns + (j + 1) * ns)
                    dve.wait_ge(activated, i * 4 + j + 1)
                    nc.vector.tensor_scalar(to, row[:, 3:3 + width], tap(3), None, ALU.mult).then_inc(step, 1)
                    for k in range(3):
                        dve.wait_ge(step, i * 12 + j * 3 + k + 1)
                        last = nc.vector.scalar_tensor_tensor(to, row[:, k:k + width], tap(k), to, ALU.mult, ALU.add)
                        if k < 2:
                            last.then_inc(step, 1)
                    last.then_inc(conved, 1)


class UnitRows:

    def __init__(self, nc, core, ctx, qk):
        self.nc, self.core, self.qk = nc, core, qk
        self.inverse = sb(nc, ctx, "ur_inverse", [HA, 2, T], side="right")
        self.squared, self.summed, self.rooted, self.inverted, self.cast, self.scaled = (
            nc.alloc_semaphore(f"ur_{n}") for n in ("squared", "summed", "rooted", "inverted", "cast", "scaled"))

    def sums(self, sq):
        nc, core = self.nc, self.core
        with core.stage() as ctx:
            ps = banks(nc, ctx, "ur_sums", 2)
            block = core.open_block(ctx)

            @block.scalar
            def _(act):
                for n in range(2 * HA):
                    if n >= 2:
                        act.wait_ge(self.summed, n - 1)
                    nc.scalar.activation(sq[:, n % 2, :], self.qk[:, n, :], ACT.Square).then_inc(self.squared, 1)
                for kind in range(2):
                    act.wait_ge(self.summed, HA * (kind + 1))
                    nc.scalar.activation(self.inverse[:, kind, :], ps[kind][0:HA, :], ACT.Sqrt, bias=core.eps[0:HA, 0:1]).then_inc(self.rooted, 1)

            @block.tensor
            def _(pe):
                for n in range(2 * HA):
                    kind, h = divmod(n, HA)
                    pe.wait_ge(self.squared, n + 1)
                    nc.tensor.matmul(ps[kind][0:HA, :], core.c[:, C_COLUMN + h * HA:C_COLUMN + (h + 1) * HA], sq[:, n % 2, :],
                                     start=(h == 0), stop=(h == HA - 1)).then_inc(self.summed, 1)

            @block.vector
            def _(dve):
                for kind in range(2):
                    dve.wait_ge(self.rooted, kind + 1)
                    nc.vector.reciprocal(self.inverse[:, kind, :], self.inverse[:, kind, :]).then_inc(self.inverted, 1)

    def scale(self):
        nc, core = self.nc, self.core
        with core.stage() as ctx:
            ps = banks(nc, ctx, "ur_cast", 4)
            block = core.open_block(ctx)

            @block.tensor
            def _(pe):
                pe.wait_ge(self.inverted, 2)
                for n in range(2 * HA):
                    kind, h = divmod(n, HA)
                    if n >= 4:
                        pe.wait_ge(self.scaled, n - 3)
                    nc.tensor.matmul(ps[n % 4][:, :], core.r[0:HA, R_SEL + h * P:R_SEL + (h + 1) * P], self.inverse[:, kind, :],
                                     start=True, stop=True).then_inc(self.cast, 1)

            @block.vector
            def _(dve):
                for n in range(2 * HA):
                    dve.wait_ge(self.cast, n + 1)
                    nc.vector.scalar_tensor_tensor(self.qk[:, n, :], self.qk[:, n, :], DK ** -0.5 if n < HA else 1.0, ps[n % 4][:, :],
                                                   ALU.mult, ALU.mult).then_inc(self.scaled, 1)


GATE_COLS = 72


def split_small(nc, dve, w, parts, split):
    nc.vector.tensor_copy(parts[0][:, :, :], w[:, :, :]).then_inc(split, 1)
    dve.wait_ge(split, 1)
    nc.vector.tensor_tensor(parts[1][:, :, :], w[:, :, :], parts[0][:, :, :].bitcast(F32), ALU.subtract).then_inc(split, 1)


def stage_delta_gates(nc, core, h_t, w, rows, cols):
    sem = lambda n: nc.alloc_semaphore(f"dg_{n}")
    loaded, zeroed, product, vdone, adone, turned, split = map(sem, (
        "loaded", "zeroed", "product", "vector_step", "scalar_step", "turned", "weights_split"))
    with core.stage() as ctx:
        wg = sb(nc, ctx, "dg_w", [P, KD, GATE_COLS])
        wp = sb_parts(nc, ctx, "dg_wp", [P, KD, GATE_COLS])
        t = sb(nc, ctx, "dg_t", [P, 4, T])
        more = sb(nc, ctx, "dg_more", [8, 2, T])
        ea = sb(nc, ctx, "dg_ea", [P, 1])
        ps = banks(nc, ctx, "dg_ps", 2)
        block = core.open_block(ctx)
        wv = w_view(w, KD)
        ab = QKV_TILES * P + HA * DV
        A = slice(32, 40)

        @block.sync
        def _(sp):
            sp.wait_ge(zeroed, 1)
            sp.dma_start(wg[:, :, 0:8], wv[:, :, ab:ab + 8]).then_inc(loaded, 16)
            sp.dma_start(wg[:, :, 32:40], wv[:, :, ab + 8:ab + 16]).then_inc(loaded, 16)

        @block.tensor
        def _(pe):
            pe.wait_ge(split, 2)
            for k in range(KD):
                last = matmul_parts(nc, ps[0][0:GATE_COLS, :], (wp[0][:, k, :], wp[1][:, k, :]), (h_t[0][:, k, :], h_t[1][:, k, :]),
                                    k == 0, k == KD - 1)
            last.then_inc(product, 1)
            pe.wait_ge(vdone, 11)
            pe.wait_ge(adone, 6)
            for kind in range(4):
                src = rows[0:8, kind, :] if kind < 2 else more[:, kind - 2, :]
                for i in range(TT):
                    last = nc.tensor.transpose(ps[1][:, (kind * TT + i) * 8:(kind * TT + i) * 8 + 8],
                                               src[:, i * P:(i + 1) * P], core.c[0:8, C_IDENT:C_IDENT + 8])
            last.then_inc(turned, 1)

        @block.scalar
        def _(act):
            nc.scalar.activation(ea[A, :], core.v[A, V_ALOG:V_ALOG + 1], ACT.Exp).then_inc(adone, 1)
            act.wait_ge(vdone, 2)
            nc.scalar.activation(t[A, 1, :], t[A, 1, :], ACT.Exp, scale=-1.0).then_inc(adone, 1)
            act.wait_ge(adone, 2)
            nc.scalar.activation(t[A, 1, :], t[A, 1, :], ACT.Ln, bias=1.0).then_inc(adone, 1)
            act.wait_ge(vdone, 9)
            nc.scalar.activation(more[:, 0, :], rows[0:8, 0, :], ACT.Exp).then_inc(adone, 1)
            act.wait_ge(vdone, 10)
            nc.scalar.activation(more[:, 1, :], more[:, 1, :], ACT.Exp).then_inc(adone, 1)
            act.wait_ge(product, 1)
            nc.scalar.activation(rows[0:8, 1, :], ps[0][0:8, :], ACT.Sigmoid).then_inc(adone, 1)

        @block.vector
        def _(dve):
            nc.vector.memset(wg[:, :, :], 0.0).then_inc(zeroed, 1)
            dve.wait_ge(loaded, 32)
            split_small(nc, dve, wg, wp, split)
            then = Chain(dve, vdone)
            dve.wait_ge(product, 1)
            then(nc.vector.tensor_scalar(t[A, 0, :], ps[0][A, :], core.v[A, V_DT:V_DT + 1], None, ALU.add))
            then(nc.vector.scalar_tensor_tensor(t[A, 1, :], t[A, 0, :], -1.0, t[A, 0, :], ALU.mult, ALU.max))
            dve.wait_ge(adone, 3)
            then(nc.vector.scalar_tensor_tensor(t[A, 2, :], t[A, 0, :], 0.0, t[A, 1, :], ALU.max, ALU.add))
            then(nc.vector.tensor_scalar(t[A, 0, :], t[A, 2, :], ea[A, 0:1], -1.0, ALU.mult, ALU.mult))
            for i in range(TT):
                c = slice(i * P, (i + 1) * P)
                then(nc.vector.tensor_tensor_scan(t[A, 3, c], core.c[A, C_ONES:C_ONES + P], t[A, 0, c], 0.0, ALU.mult, ALU.add))
            then(nc.vector.tensor_copy(rows[0:8, 0, :], t[A, 3, :]))
            g = rows[0:8, 0, :].rearrange("p (i c) -> p i c", i=TT)
            then(nc.vector.tensor_tensor(more[:, 1, :].rearrange("p (i c) -> p i c", i=TT),
                                         g[:, :, P - 1:P].to_broadcast([8, TT, P]), g, ALU.subtract))
            dve.wait_ge(adone, 6)
            then(nc.vector.tensor_tensor(more[:, 0, :], more[:, 0, :], rows[0:8, 1, :], ALU.mult))
            dve.wait_ge(turned, 1)
            nc.vector.tensor_copy(cols[:, :, :, :], ps[1][:, 0:4 * TT * 8].rearrange("p (a i h) -> p a i h", a=4, i=TT))


def stage_delta_chunks(nc, core, qk_in, v, rows, cols, ss):
    sem = lambda n: nc.alloc_semaphore(f"dc_{n}")
    (rowcast, exp_g, decayed, gramed, masked, weighted, qk_ready, qdec_ready, level_ready, x_ready, x_copied, mx_ready, m_ready,
     turned, turn_copied, kdec_ready, t_scaled, w_ready, w_copied, vnew_ready, vnew_copied, out_ready, out_read, s_ready,
     step, adj_ready) = map(sem, (
        "rowcast", "exp_g", "decayed", "gramed", "masked", "weighted", "qk_ready", "qdec_ready", "level_ready", "x_ready", "x_copied",
        "mx_ready", "m_ready", "turned", "turn_copied", "kdec_ready", "t_scaled", "w_ready", "w_copied", "vnew_ready", "vnew_copied",
        "out_ready", "out_read", "s_ready", "step", "adjusted"))
    ident = core.c[:, C_IDENT:C_IDENT + P]
    q_t = lambda h: qk_in[:, h, :]
    k_t = lambda h: qk_in[:, HA + h, :]
    v_t = lambda h, j: v[:, 2 * h + j, :]
    o_h = lambda h: v[:, 2 * h:2 * h + 2, :].rearrange("p j (a d) -> p (j a) d", a=2)
    w4 = lambda ap: ap.rearrange("p (i c) -> p i c", i=TT)
    PAIRS = [(2 * p, 2 * p + 1) for p in range(HA // 2)]
    with core.stage() as ctx:
        two = lambda name, n=T: [sb(nc, ctx, f"dc_{name}{j}", [P, n]) for j in range(2)]
        dec, at, em, m, mt, xs = two("dec"), two("at"), two("em"), two("m"), two("mt"), two("xs")
        lv = two("lv", 2 * T)
        tb, tbg, kn, kd, wt, qd, qk, eg = (two(n) for n in ("tb", "tbg", "kn", "kd", "wt", "qd", "qk", "eg"))
        vn, vnew, st, junk = two("vn", TT * DV), two("vnew", DV), two("st", DV), two("junk", DV)
        ba, bb, bc, bd = (banks(nc, ctx, f"dc_p{n}", 2) for n in "abcd")
        block = core.open_block(ctx)

        @block.tensor
        def _(pe):
            def turn(h, n):
                j = h % 2
                if n == 0:
                    pe.wait_ge(qk_ready, h + 1)
                else:
                    pe.wait_ge(turn_copied, h // 2 * 6 + 2 * (n - 1) + j + 1)
                src = k_t(h) if n == 0 else v_t(h, n - 1)
                for i in range(TT):
                    last = nc.tensor.transpose(bd[j][:, i * P:(i + 1) * P], src[:, i * P:(i + 1) * P], ident)
                last.then_inc(turned, 1)

            for pair in PAIRS:
                for h in pair:
                    j = h % 2
                    if h >= 2:
                        pe.wait_ge(s_ready, 6 * (h // 2))
                        pe.wait_ge(vnew_copied, 8 * (h // 2))
                        pe.wait_ge(out_read, 8 * (h // 2))
                        pe.wait_ge(turn_copied, 6 * (h // 2))
                    sel = core.r[0:8, R_SEL + h * P:R_SEL + (h + 1) * P]
                    nc.tensor.matmul(ba[j][:, :], sel, rows[0:8, 0, :], start=True, stop=True)
                    nc.tensor.matmul(bb[j][:, :], sel, rows[0:8, 1, :], start=True, stop=True).then_inc(rowcast, 1)
                    for bank, rhs in ((bc, k_t(h)), (bd, q_t(h))):
                        for i in range(TT):
                            c = slice(i * P, (i + 1) * P)
                            last = nc.tensor.matmul(bank[j][:, c], k_t(h)[:, c], rhs[:, c], start=True, stop=True)
                    last.then_inc(gramed, 1)
                for n in range(LEVELS):
                    for h in pair:
                        j = h % 2
                        pe.wait_ge(level_ready, h // 2 * 2 * LEVELS + 2 * n + j + 1)
                        pe.wait_ge(m_ready, h // 2 * 2 * (LEVELS + 1) + 2 * n + j + 1)
                        if n == 0:
                            pe.wait_ge(exp_g, 2 * h + 2)
                            pe.wait_ge(decayed, h + 1)
                        for i in range(TT):
                            c = slice(i * P, (i + 1) * P)
                            last = nc.tensor.matmul(ba[j][:, c], lv[j][:, n % 2 * T + i * P:n % 2 * T + (i + 1) * P], m[j][:, c],
                                                    start=True, stop=True)
                        last.then_inc(x_ready, 1)
                    for h in pair if n else ():
                        j = h % 2
                        if n in (1, 3, 5):
                            turn(h, n // 2)
                        pe.wait_ge(x_copied, h // 2 * 2 * (LEVELS - 1) + 2 * (n - 1) + j + 1)
                        for i in range(TT):
                            c = slice(i * P, (i + 1) * P)
                            if n < LEVELS - 1:
                                nc.tensor.matmul(bb[j][:, c], mt[j][:, c], xs[j][:, c], start=True, stop=True)
                            last = nc.tensor.matmul(bc[j][:, c], xs[j][:, c], mt[j][:, c], start=True, stop=True)
                        last.then_inc(mx_ready, 1)
                for h in pair:
                    j = h % 2
                    pe.wait_ge(t_scaled, h + 1)
                    pe.wait_ge(turn_copied, h // 2 * 6 + 4 + j + 1)
                    for i in range(TT):
                        c = slice(i * P, (i + 1) * P)
                        last = nc.tensor.matmul(ba[j][:, c], kn[j][:, c], tbg[j][:, c], start=True, stop=True)
                    last.then_inc(w_ready, 1)
                for i in range(TT):
                    c = slice(i * P, (i + 1) * P)
                    for h in pair:
                        j = h % 2
                        if i:
                            pe.wait_ge(s_ready, h // 2 * 6 + (i - 1) * 2 + j + 1)
                        last = nc.tensor.matmul(bb[j][:, 0:DV], tb[j][:, c], vn[j][:, i * DV:(i + 1) * DV], start=True, stop=i == 0)
                        if i:
                            last = nc.tensor.matmul(bb[j][:, 0:DV], wt[j][:, c], st[j][:, :], start=False, stop=True)
                        last.then_inc(vnew_ready, 1)
                    for h in pair:
                        j = h % 2
                        pe.wait_ge(vnew_copied, h // 2 * 8 + 2 * i + j + 1)
                        if i:
                            pe.wait_ge(out_read, h // 2 * 8 + 2 * (i - 1) + j + 1)
                            nc.tensor.matmul(bc[j][:, 0:DV], qd[j][:, c], st[j][:, :], start=True, stop=False)
                        else:
                            pe.wait_ge(w_copied, h + 1)
                            pe.wait_ge(qdec_ready, h + 1)
                            pe.wait_ge(kdec_ready, h + 1)
                        last = nc.tensor.matmul(bc[j][:, 0:DV], qk[j][:, c], vnew[j][:, :], start=i == 0, stop=True)
                        if i < TT - 1:
                            last = nc.tensor.matmul(ba[j][:, 0:DV], kd[j][:, c], vnew[j][:, :], start=True, stop=True)
                        last.then_inc(out_ready, 1)

        @block.scalar
        def _(act):
            for pair in PAIRS:
                for h in pair:
                    j = h % 2
                    act.wait_ge(decayed, h + 1)
                    if h >= 2:
                        act.wait_ge(s_ready, 6 * (h // 2))
                    nc.scalar.activation(eg[j][:, :], ba[j][:, :], ACT.Exp).then_inc(exp_g, 1)
                    nc.scalar.activation(dec[j][:, :], dec[j][:, :], ACT.Exp).then_inc(exp_g, 1)
                for n in range(1, LEVELS):
                    for h in pair:
                        j = h % 2
                        act.wait_ge(x_ready, h // 2 * 2 * LEVELS + 2 * n + j + 1)
                        nc.scalar.activation(xs[j][:, :], ba[j][:, :], ACT.Copy).then_inc(x_copied, 1)
                    for h in pair:
                        j = h % 2
                        if n in (1, 3, 5):
                            act.wait_ge(turned, h // 2 * 6 + (n // 2) * 2 + j + 1)
                            dst = kn[j][:, :] if n == 1 else w4v(vn[j], DV)[:, :, (n // 2 - 1) * P:(n // 2) * P]
                            nc.scalar.activation(dst, bd[j][:, :] if n == 1 else w4(bd[j][:, :]), ACT.Copy).then_inc(turn_copied, 1)
                for h in pair:
                    j = h % 2
                    act.wait_ge(w_ready, h + 1)
                    nc.scalar.activation(wt[j][:, :], ba[j][:, :], ACT.Copy, scale=-1.0).then_inc(w_copied, 1)
                for i in range(TT):
                    for h in pair:
                        j = h % 2
                        act.wait_ge(vnew_ready, h // 2 * 8 + 2 * i + j + 1)
                        nc.scalar.activation(vnew[j][:, :], bb[j][:, 0:DV], ACT.Copy).then_inc(vnew_copied, 1)
                    for h in pair:
                        j = h % 2
                        act.wait_ge(out_ready, h // 2 * 8 + 2 * i + j + 1)
                        nc.scalar.activation(o_h(h)[:, i, :], bc[j][:, 0:DV], ACT.Copy)
                        nc.scalar.activation(junk[j][:, :], bc[j][:, 0:DV], ACT.Square, accum_out=ss[:, i, h:h + 1]).then_inc(out_read, 1)

        @block.gpsimd
        def _(pool):
            for pair in PAIRS:
                for h in pair:
                    j = h % 2
                    pool.wait_ge(exp_g, 2 * h + 2)
                    nc.gpsimd.tensor_tensor(w4(em[j][:, :]), w4(dec[j][:, :]),
                                            core.c[:, C_LE:C_LE + P].unsqueeze(1).to_broadcast([P, TT, P]), ALU.mult).then_inc(masked, 1)
                for n in range(LEVELS):
                    for h in pair:
                        j = h % 2
                        if n == 0:
                            pool.wait_ge(weighted, h + 1)
                        if n >= 2:
                            pool.wait_ge(x_ready, h // 2 * 2 * LEVELS + 2 * (n - 2) + j + 1)
                        elif h >= 2:
                            pool.wait_ge(x_ready, h // 2 * 2 * LEVELS)
                        if n == 2:
                            pool.wait_ge(m_ready, h // 2 * 2 * (LEVELS + 1) + 2 + j + 1)
                        lo = C_LEVEL + n * P
                        nc.gpsimd.tensor_tensor(w4(lv[j][:, n % 2 * T:n % 2 * T + T]), w4(at[j][:, :]),
                                                core.c[:, lo:lo + P].unsqueeze(1).to_broadcast([P, TT, P]), ALU.mult).then_inc(level_ready, 1)
                for h in pair:
                    j = h % 2
                    pool.wait_ge(turn_copied, h // 2 * 6 + j + 1)
                    if h >= 2:
                        pool.wait_ge(out_ready, 8 * (h // 2))
                    nc.gpsimd.tensor_tensor(w4(kd[j][:, :]), w4(kn[j][:, :]), cols[:, 3, :, h:h + 1].to_broadcast([P, TT, P]),
                                            ALU.mult).then_inc(kdec_ready, 1)

        @block.vector
        def _(dve):
            eye = ident.unsqueeze(1).to_broadcast([P, TT, P])
            for pair in PAIRS:
                for h in pair:
                    j = h % 2
                    dve.wait_ge(rowcast, h + 1)
                    if h >= 2:
                        dve.wait_ge(masked, h - 1)
                    for i in range(TT):
                        c = slice(i * P, (i + 1) * P)
                        last = nc.vector.tensor_scalar(dec[j][:, c], ba[j][:, c], cols[:, 0, i, h:h + 1], 0.0, ALU.subtract, ALU.min)
                    last.then_inc(decayed, 1)
                    nc.vector.tensor_copy(w4(m[j][:, :]), eye)
                    nc.vector.tensor_copy(w4(mt[j][:, :]), eye).then_inc(m_ready, 1)
                for h in pair:
                    j = h % 2
                    dve.wait_ge(gramed, h + 1)
                    dve.wait_ge(exp_g, 2 * h + 2)
                    nc.vector.tensor_tensor(at[j][:, :], bc[j][:, :], dec[j][:, :], ALU.mult).then_inc(step, 1)
                    dve.wait_ge(step, h + 1)
                    nc.vector.tensor_tensor(at[j][:, :], bb[j][:, :], at[j][:, :], ALU.mult).then_inc(weighted, 1)
                    dve.wait_ge(masked, h + 1)
                    nc.vector.tensor_tensor(qk[j][:, :], bd[j][:, :], em[j][:, :], ALU.mult).then_inc(qk_ready, 1)
                    nc.vector.tensor_tensor(qd[j][:, :], q_t(h), eg[j][:, :], ALU.mult).then_inc(qdec_ready, 1)
                for h in pair:
                    j = h % 2
                    dve.wait_ge(x_ready, h // 2 * 2 * LEVELS + j + 1)
                    nc.vector.tensor_tensor(m[j][:, :], m[j][:, :], ba[j][:, :], ALU.subtract)
                    nc.vector.tensor_tensor(mt[j][:, :], mt[j][:, :], lv[j][:, 0:T], ALU.subtract).then_inc(m_ready, 1)
                for n in range(1, LEVELS):
                    for h in pair:
                        j = h % 2
                        dve.wait_ge(mx_ready, h // 2 * 2 * (LEVELS - 1) + 2 * (n - 1) + j + 1)
                        if n < LEVELS - 1:
                            nc.vector.tensor_tensor(m[j][:, :], m[j][:, :], bb[j][:, :], ALU.subtract)
                        nc.vector.tensor_tensor(mt[j][:, :], mt[j][:, :], bc[j][:, :], ALU.subtract).then_inc(m_ready, 1)
                for h in pair:
                    j = h % 2
                    dve.wait_ge(m_ready, h // 2 * 2 * (LEVELS + 1) + 2 * LEVELS + j + 1)
                    nc.vector.tensor_tensor(w4(tb[j][:, :]), w4(mt[j][:, :]), cols[:, 1, :, h:h + 1].to_broadcast([P, TT, P]), ALU.mult)
                    nc.vector.tensor_tensor(w4(tbg[j][:, :]), w4(mt[j][:, :]), cols[:, 2, :, h:h + 1].to_broadcast([P, TT, P]),
                                            ALU.mult).then_inc(t_scaled, 1)
                for i in range(TT - 1):
                    for h in pair:
                        j = h % 2
                        dve.wait_ge(out_ready, h // 2 * 8 + 2 * i + j + 1)
                        if i:
                            dve.wait_ge(s_ready, h // 2 * 6 + (i - 1) * 2 + j + 1)
                            last = nc.vector.scalar_tensor_tensor(st[j][:, :], st[j][:, :], eg[j][:, i * P + P - 1:i * P + P],
                                                                  ba[j][:, 0:DV], ALU.mult, ALU.add)
                        else:
                            last = nc.vector.tensor_copy(st[j][:, :], ba[j][:, 0:DV])
                        last.then_inc(s_ready, 1)


def w4v(buf, n):
    return buf[:, :].rearrange("p (i d) -> p i d", d=n)


def open_core(nc, stack, a):
    core = Core(nc, stack)
    core.c = core.keep("c128_sb", [P, C_WIDTH])
    core.r = core.keep("c32_sb", [32, R_KEPT])
    core.v = core.keep("v128_sb", [P, V_WIDTH])
    core.x = core.keep("x_sb", [P, TT, D])
    core.eps = core.keep("eps_sb", [P, 2])
    core.ta = core.keep("taps_a_sb", [P, QKV_TILES, 4])
    core.tm = core.keep("taps_m_sb", [P, 2 * HM, 4])
    core.ring = Ring(nc, core, weights_plan(a))
    return core


def products_n(nc, pe, w, split, h_t, tiles, ps, c, free, done, spent, finished=None, h_ready=None):
    group, part = divmod(c, w.parts)
    nt = len(tiles)
    pe.wait_ge(split.ready, c + 1)
    if h_ready is not None and group == 0:
        pe.wait_ge(h_ready, part + 1)
    hi, lo = split.parts(c % 2)
    for i, (rows, col) in enumerate(tiles):
        u = group * nt + i
        if part == 0:
            free(u)
        for k in range(4):
            kk = 4 * part + k
            last = matmul_parts(nc, ps[u % len(ps)][:, :], (h_t[0][:, kk, col:col + P], h_t[1][:, kk, col:col + P]),
                                (hi[:, k, :], lo[:, k, :]), kk == 0, kk == 4 * w.parts - 1)
        if part == w.parts - 1:
            last.then_inc(done, 1)
            if finished is not None:
                finished(u)
    if part < w.parts - 1:
        last.then_inc(spent, 1)


def wait_spent(eng, w, c, nt, done, spent):
    group, part = divmod(c, w.parts)
    if part == w.parts - 1:
        eng.wait_ge(done, (group + 1) * nt)
    else:
        eng.wait_ge(spent, group * (w.parts - 1) + part + 1)


def split_whole(nc, dve, whole, parts, n, hi_ready, split):
    for i in range(n):
        k = slice(4 * i, 4 * i + 4)
        nc.vector.tensor_copy(parts[0][:, k, :], whole[:, k, :]).then_inc(hi_ready, 1)
        dve.wait_ge(hi_ready, i + 1)
        nc.vector.tensor_tensor(parts[1][:, k, :], whole[:, k, :], parts[0][:, k, :].bitcast(F32), ALU.subtract).then_inc(split, 1)


def stage_proj_n(nc, core, tag, h_t, tiles, engine, emit, whole=None):
    product, taken, spent, h_hi, h_split = (nc.alloc_semaphore(f"{tag}_{n}") for n in ("product", "taken", "spent", "h_hi", "h_split"))
    nt = len(tiles)
    with core.stage() as ctx:
        split = Split(nc, core, ctx, tag, shared_opening=whole is None)
        w = split.w
        if whole is not None:
            h_t = sb_parts(nc, ctx, f"{tag}_h", [P, 4 * w.parts, T])
        ps = banks(nc, ctx, f"{tag}_ps", 8)
        block = core.open_block(ctx)

        @block.sync
        def _(sp):
            split.loads(sp)

        @block.gpsimd
        def _(pool):
            split.split_lo(pool)

        @block.tensor
        def _(pe):
            def free(u):
                if u >= 8:
                    pe.wait_ge(taken, u - 7)
            split.wait_opened(pe)
            for c in range(w.chunks):
                products_n(nc, pe, w, split, h_t, tiles, ps, c, free, product, spent, h_ready=None if whole is None else h_split)

        def take(eng):
            for g in range(w.chunks // w.parts):
                for i, (rows, col) in enumerate(tiles):
                    u = g * nt + i
                    eng.wait_ge(product, u + 1)
                    emit(g, i, ps[u % 8][0:rows, :]).then_inc(taken, 1)

        def split_hi(eng):
            for c in range(0 if whole is not None else 1, w.chunks):
                if c >= 2:
                    wait_spent(eng, w, c - 2, nt, product, spent)
                split.split_hi(eng, c // 2, c % 2)

        @block.scalar
        def _(act):
            if whole is None:
                split.open_scalar(act)
            if engine == "scalar":
                take(act)
            else:
                split_hi(act)

        @block.vector
        def _(dve):
            if whole is not None:
                split_whole(nc, dve, whole, h_t, w.parts, h_hi, h_split)
            else:
                split.open_vector(dve)
            if engine == "scalar":
                split_hi(dve)
            else:
                take(dve)


X_COLS = [(P, i * P) for i in range(TT)]


def add_to_x(nc, core, width=512):
    def emit(c, i, product):
        x = core.x[:, i, c * width:(c + 1) * width]
        return nc.vector.tensor_tensor(x, x, product, ALU.add)
    return emit


def stage_delta_out(nc, core, whole, o, ss, gain, o_t):
    sem = lambda n: nc.alloc_semaphore(f"do_{n}")
    gain_loaded, spent, h_hi, h_split = map(sem, ("gain_loaded", "spent", "h_hi", "h_split"))
    meaned, rooted, product, gated, normed, mixed, step, turned, taken = map(
        sem, ("meaned", "rooted", "product", "gated", "normed", "mixed", "step", "turned", "taken"))
    with core.stage() as ctx:
        split = Split(nc, core, ctx, "do")
        h_t = sb_parts(nc, ctx, "do_h", [P, KD, T])
        rstd = sb(nc, ctx, "do_rstd", [P, 2, TT * HA])
        sil = sb(nc, ctx, "do_sil", [P, 2, 512])
        on = sb(nc, ctx, "do_on", [P, 2, 512])
        gb = sb(nc, ctx, "do_gain", [P, DV])
        ps, pt = banks(nc, ctx, "do_ps", 6), banks(nc, ctx, "do_pt", 2)
        block = core.open_block(ctx)
        w = split.w
        U = 4 * TT

        @block.sync
        def _(sp):
            sp.dma_start(gb[:, :], gain.partition_broadcast(P)).then_inc(gain_loaded, 16)
            split.loads(sp)

        @block.tensor
        def _(pe):
            def turn(u):
                pe.wait_ge(mixed, u + 1)
                if u >= 2:
                    pe.wait_ge(taken, u - 1)
                for k in range(4):
                    last = nc.tensor.transpose(pt[u % 2][:, k * P:(k + 1) * P], on[:, u % 2, k * P:(k + 1) * P],
                                               core.c[:, C_IDENT:C_IDENT + P])
                last.then_inc(turned, 1)
            def free(u):
                if u >= 6:
                    pe.wait_ge(gated, u - 5)

            def finished(u):
                if u:
                    turn(u - 1)
            for c in range(w.chunks):
                products_n(nc, pe, w, split, h_t, X_COLS, ps, c, free, product, spent, finished, h_split)
            turn(U - 1)

        @block.gpsimd
        def _(pool):
            pool.wait_ge(meaned, 1)
            nc.gpsimd.tensor_tensor(rstd[:, 1, :], rstd[:, 0, :], core.c[:, C_MHALF:C_MHALF + 1].to_broadcast([P, TT * HA]),
                                    ALU.pow).then_inc(rooted, 1)
            split.split_lo(pool)

        @block.scalar
        def _(act):
            for b in range(2):
                split.split_hi(act, 0, b)
            for u in range(U):
                act.wait_ge(product, u + 1)
                if u >= 2:
                    act.wait_ge(mixed, u - 1)
                nc.scalar.activation(sil[:, u % 2, :], ps[u % 6][:, :], ACT.Silu).then_inc(gated, 1)
                group, i = divmod(u, TT)
                if i in (0, TT - 1) and group + 1 < U // TT:
                    split.split_hi(act, group + 1, i // (TT - 1))

        @block.vector
        def _(dve):
            nc.vector.tensor_scalar(rstd[:, 0, :], ss.rearrange("p i h -> p (i h)"), 1.0 / DV, EPS, ALU.mult, ALU.add).then_inc(meaned, 1)
            split_whole(nc, dve, whole, h_t, w.parts, h_hi, h_split)
            dve.wait_ge(rooted, 1)
            dve.wait_ge(gain_loaded, 16)

            def store(u):
                c, i = divmod(u, TT)
                dve.wait_ge(turned, u + 1)
                nc.vector.tensor_copy(o_t[:, 4 * c:4 * c + 4, i * P:(i + 1) * P],
                                      pt[u % 2][:, :].rearrange("p (k t) -> p k t", k=4)).then_inc(taken, 1)
            for u in range(U):
                c, i = divmod(u, TT)
                if u >= 2:
                    dve.wait_ge(turned, u - 1)
                for j in range(2):
                    h = 2 * c + j
                    nc.vector.scalar_tensor_tensor(on[:, u % 2, j * DV:(j + 1) * DV], o[:, h, i, :],
                                                   rstd[:, 1, i * HA + h:i * HA + h + 1], gb[:, :],
                                                   ALU.mult, ALU.mult).then_inc(step, 1)
                dve.wait_ge(step, 2 * u + 2)
                dve.wait_ge(gated, u + 1)
                nc.vector.tensor_tensor(on[:, u % 2, :], on[:, u % 2, :], sil[:, u % 2, :], ALU.mult).then_inc(mixed, 1)
                if u:
                    store(u - 1)
            store(U - 1)


def stage_shared_k(nc, core, kv, k_t):
    sem = lambda n: nc.alloc_semaphore(f"sk_{n}")
    squared, step, meaned, rooted, normed, turned, taken, gained = map(
        sem, ("squared", "step", "meaned", "rooted", "normed", "turned", "taken", "gained"))
    KW = KVB * HD
    with core.stage() as ctx:
        sq = sb(nc, ctx, "sk_sq", [P, TT, KW])
        r = sb(nc, ctx, "sk_r", [P, 3, TT * KVB])
        kn = sb(nc, ctx, "sk_kn", [P, TT, KVB, 2, HD])
        g = sb(nc, ctx, "sk_g", [P, 1])
        ps = banks(nc, ctx, "sk_ps", 4)
        block = core.open_block(ctx)

        @block.scalar
        def _(act):
            nc.scalar.activation(sq[:, :, :], kv[:, :, 0:KW], ACT.Square).then_inc(squared, 1)

        @block.gpsimd
        def _(pool):
            pool.wait_ge(meaned, 1)
            nc.gpsimd.tensor_tensor(r[:, 2, :], r[:, 1, :], core.c[:, C_MHALF:C_MHALF + 1].to_broadcast([P, TT * KVB]),
                                    ALU.pow).then_inc(rooted, 1)

        @block.tensor
        def _(pe):
            pe.wait_ge(normed, TT)
            for h in range(KVB):
                for i in range(TT):
                    last = nc.tensor.transpose(ps[h][:, i * P:(i + 1) * P], kn[:, i, h, :, :].rearrange("p a d -> p (a d)"),
                                               core.c[:, C_IDENT:C_IDENT + P])
                last.then_inc(turned, 1)

        @block.vector
        def _(dve):
            nc.vector.tensor_tensor(g[:, :], core.v[:, V_QGK:V_QGK + 1], core.v[:, V_QGK + 1:V_QGK + 2], ALU.mult).then_inc(gained, 1)
            dve.wait_ge(squared, 1)
            nc.vector.tensor_reduce(r[:, 0, :], sq[:, :, :].rearrange("p i (h d) -> p (i h) d", d=HD), AX.X, ALU.add).then_inc(step, 1)
            dve.wait_ge(step, 1)
            nc.vector.tensor_scalar(r[:, 1, :], r[:, 0, :], 1.0 / HD, EPS, ALU.mult, ALU.add).then_inc(meaned, 1)
            dve.wait_ge(rooted, 1)
            for i in range(TT):
                nc.vector.tensor_tensor(kn[:, i, :, :, :], kv[:, i, 0:KW].rearrange("p (h d) -> p h d", d=HD).unsqueeze(2).to_broadcast([P, KVB, 2, HD]),
                                        r[:, 2, i * KVB:(i + 1) * KVB].unsqueeze(2).unsqueeze(3).to_broadcast([P, KVB, 2, HD]),
                                        ALU.mult).then_inc(normed, 1)
            dve.wait_ge(gained, 1)
            for h in range(KVB):
                dve.wait_ge(turned, h + 1)
                nc.vector.tensor_scalar(k_t[:, h, :], ps[h][:, :], g[:, 0:1], None, ALU.mult).then_inc(taken, 1)


def stage_head_scale(nc, core, tag, q_t, tiles, cols, out, scale2):
    sem = lambda n: nc.alloc_semaphore(f"{tag}_{n}")
    squared, summed, rooted, inverted, scaled = map(sem, ("squared", "summed", "rooted", "inverted", "scaled"))
    w = len(cols) * 2 * tiles
    with core.stage() as ctx:
        sq = sb(nc, ctx, f"{tag}_sq", [P, 2, T])
        rt = sb(nc, ctx, f"{tag}_rt", [P, w])
        ps = banks(nc, ctx, f"{tag}_ps", 1)[0]
        block = core.open_block(ctx)

        @block.scalar
        def _(act):
            for n in range(tiles):
                if n >= 2:
                    act.wait_ge(summed, n - 1)
                nc.scalar.activation(sq[:, n % 2, :], q_t[:, n, :], ACT.Square).then_inc(squared, 1)
            act.wait_ge(summed, tiles)
            nc.scalar.activation(rt[:, :], ps[:, 0:w], ACT.Sqrt, bias=core.eps[:, 1:2]).then_inc(rooted, 1)

        @block.tensor
        def _(pe):
            for n in range(tiles):
                pe.wait_ge(squared, n + 1)
                for i, c in enumerate(cols):
                    at = (i * tiles + n) * 2
                    last = nc.tensor.matmul(ps[:, at:at + 2], sq[:, n % 2, c:c + P], core.c[:, C_PAIR:C_PAIR + 2], start=True, stop=True)
                last.then_inc(summed, 1)

        @block.vector
        def _(dve):
            dve.wait_ge(rooted, 1)
            nc.vector.reciprocal(out.rearrange("p i h -> p (i h)"), rt[:, :]).then_inc(inverted, 1)
            if scale2 != 1:
                dve.wait_ge(inverted, 1)
                nc.vector.tensor_scalar(out.rearrange("p i h -> p (i h)"), out.rearrange("p i h -> p (i h)"), scale2, None, ALU.mult).then_inc(scaled, 1)


class Bias:

    def __init__(self, nc, core):
        self.nc, self.core = nc, core
        self.loaded, self.product, self.masked, self.stored, self.back, self.flipped, self.copied = (
            nc.alloc_semaphore(f"rb_{n}") for n in ("loaded", "product", "masked", "stored", "back", "flipped", "copied"))

    def rows(self, tables, rel_bias, scratch, room):
        nc, core = self.nc, self.core
        with core.stage() as ctx:
            rb, buckets, row = room[0:32, 0, 0:HB], room[0:32, 1, 0:R_WIDTH - R_KEPT], room[0:HB, 2, 0:384]
            ps = banks(nc, ctx, "rb_ps", 1)[0]
            block = core.open_block(ctx)

            @block.sync
            def _(sp):
                sp.dma_start(rb[:, :], rel_bias).then_inc(self.loaded, 16)
                sp.dma_start(buckets[:, :], tables[:, R_KEPT:R_WIDTH]).then_inc(self.loaded, 16)
                sp.wait_ge(self.masked, 1)
                sp.dma_start(scratch, row[:, :]).then_inc(self.stored, 16)

            @block.tensor
            def _(pe):
                pe.wait_ge(self.loaded, 32)
                nc.tensor.matmul(ps[0:HB, 0:384], rb[:, :], buckets[:, 0:384], start=True, stop=True).then_inc(self.product, 1)

            @block.vector
            def _(dve):
                dve.wait_ge(self.product, 1)
                nc.vector.tensor_tensor(row[:, :], ps[0:HB, 0:384], buckets[:, 384:768], ALU.add).then_inc(self.masked, 1)

    def flip(self, scratch, shifted, bias):
        nc, core = self.nc, self.core
        with core.stage() as ctx:
            turn = banks(nc, ctx, "rb_turn", 4)
            block = core.open_block(ctx)

            @block.sync
            def _(sp):
                sp.wait_ge(self.stored, 16)
                with nc.allow_non_contiguous_dma("rows shifted by one"):
                    for n, h in enumerate(range(0, HB, 8)):
                        src = bass.AP(scratch.tensor, h * 384, [[1, P], [384, 8], [1, 256]])
                        if n:
                            sp.wait_ge(self.back, 16 * n)
                        sp.dma_start(shifted[:, h:h + 8, :], src).then_inc(self.back, 16)

            @block.tensor
            def _(pe):
                for i in range(HB // 2):
                    if i % 4 == 0:
                        pe.wait_ge(self.back, 4 * i + 16)
                    if i >= 4:
                        pe.wait_ge(self.copied, i - 3)
                    nc.tensor.matmul(turn[i % 4][:, :], core.c[:, C_FLIP:C_FLIP + P], shifted[:, 2 * i:2 * i + 2, :],
                                     start=True, stop=True).then_inc(self.flipped, 1)

            @block.vector
            def _(dve):
                for i in range(HB // 2):
                    dve.wait_ge(self.flipped, i + 1)
                    nc.vector.tensor_copy(bias[:, 2 * i:2 * i + 2, :], turn[i % 4][:, :].rearrange("p (h s) -> p h s", h=2)).then_inc(self.copied, 1)


def stage_window_attention(nc, core, q_t, k_t, kv, rq, bias, sinks, z):
    sem = lambda n: nc.alloc_semaphore(f"wa_{n}")
    (loaded, scored, biased, step, shifted, expd, sunk, turned, act_taken, dve_taken, mixed, weighted, gated) = map(sem, (
        "loaded", "scored", "biased", "step", "shifted", "expd", "sunk", "turned", "scalar_taken", "vector_taken", "mixed", "weighted", "gated"))
    ident = core.c[:, C_IDENT:C_IDENT + P]
    G = HB // 4
    U = [(n, g) for n in range(TT) for g in range(G)]
    with core.stage() as ctx:
        lg = sb(nc, ctx, "wa_lg", [P, 2, 4, 256])
        pt = sb(nc, ctx, "wa_pt", [P, 2, 4, 2, P])
        sm = sb(nc, ctx, "wa_sm", [P, 3, 8, 4])
        snk = sb(nc, ctx, "wa_snk", [P, HB])
        tmp = sb(nc, ctx, "wa_tmp", [P, 2, 256])
        sc = [banks(nc, ctx, f"wa_sc{e}", 2) for e in range(2)]
        tp = banks(nc, ctx, "wa_tp", 2)
        po = banks(nc, ctx, "wa_po", 2)
        block = core.open_block(ctx)
        first = lambda n: P if n == 0 else 0
        col = lambda u, k, e=slice(0, 4): sm[:, u % 3, k, e]

        @block.sync
        def _(sp):
            sp.dma_start(snk[:, :], sinks.partition_broadcast(P)).then_inc(loaded, 16)

        @block.tensor
        def _(pe):
            def scores(u):
                n, g = U[u]
                s0 = first(n)
                if u >= 2:
                    pe.wait_ge(biased, u - 1)
                for e in range(4):
                    half = slice(64 * (e % 2), 64 * (e % 2) + 64)
                    last = nc.tensor.matmul(sc[e % 2][u % 2][:, e // 2 * 256 + s0:e // 2 * 256 + 256],
                                            q_t[half, 2 * g + e // 2, n * P:(n + 1) * P],
                                            k_t[half, g // 2, n * P + s0 - P:(n + 1) * P], start=True, stop=True)
                last.then_inc(scored, 1)
            blocks = lambda u: range(1 if U[u][0] == 0 else 0, 2)

            def turn(u):
                for p in range(2):
                    pe.wait_ge(expd, 2 * u + p + 1)
                    if u:
                        pe.wait_ge((act_taken, dve_taken)[p], u)
                    for e in (2 * p, 2 * p + 1):
                        for b in blocks(u):
                            last = nc.tensor.transpose(tp[p][:, (e % 2 * 2 + b) * P:(e % 2 * 2 + b + 1) * P],
                                                       lg[:, u % 2, e, b * P:(b + 1) * P], ident)
                    last.then_inc(turned, 1)

            def mix(u):
                n, g = U[u]
                if u >= 2:
                    pe.wait_ge(weighted, u - 1)
                for e in range(4):
                    if e % 2 == 0:
                        pe.wait_ge((act_taken, dve_taken)[e // 2], u + 1)
                    for b in blocks(u):
                        last = nc.tensor.matmul(po[u % 2][:, e * HD:(e + 1) * HD], pt[:, u % 2, e, b, :],
                                                kv[:, n - 1 + b, (KVB + g // 2) * HD:(KVB + g // 2 + 1) * HD],
                                                start=(b == blocks(u)[0]), stop=(b == 1))
                last.then_inc(mixed, 1)
            for u in range(3):
                scores(u)
            turn(0)
            for u in range(len(U)):
                if u + 3 < len(U):
                    scores(u + 3)
                if u + 1 < len(U):
                    turn(u + 1)
                mix(u)

        @block.scalar
        def _(act):
            def exp(u):
                s0 = first(U[u][0])
                act.wait_ge(shifted, u + 1)
                for e in range(4):
                    last = nc.scalar.activation(lg[:, u % 2, e, s0:256], lg[:, u % 2, e, s0:256], ACT.Exp,
                                                bias=col(u, 2, slice(e, e + 1)), accum_out=col(u, 4, slice(e, e + 1)))
                    if e % 2:
                        last.then_inc(expd, 1)
                nc.scalar.activation(col(u, 5), col(u, 3), ACT.Exp).then_inc(sunk, 1)

            def take(u):
                b0 = first(U[u][0]) // P
                act.wait_ge(turned, 2 * u + 1)
                if u >= 2:
                    act.wait_ge(mixed, u - 1)
                nc.scalar.activation(pt[:, u % 2, 0:2, b0:2, :], tp[0][:, :].rearrange("p (e b t) -> p e b t", e=2, b=2)[:, :, b0:2, :],
                                     ACT.Copy).then_inc(act_taken, 1)
            exp(0)
            exp(1)
            take(0)
            for u in range(len(U)):
                if u + 2 < len(U):
                    exp(u + 2)
                if u + 1 < len(U):
                    take(u + 1)

        @block.vector
        def _(dve):
            own = Marks(dve, step)

            def logits(u):
                n, g = U[u]
                s0 = first(n)
                dve.wait_ge(scored, u + 1)
                if u >= 2:
                    dve.wait_ge(turned, 2 * (u - 1))
                for e in range(4):
                    h = 4 * g + e
                    last = nc.vector.scalar_tensor_tensor(lg[:, u % 2, e, s0:256], sc[e % 2][u % 2][:, e // 2 * 256 + s0:e // 2 * 256 + 256],
                                                          rq[:, n, h:h + 1], bias[:, h, s0:256], ALU.mult, ALU.add)
                last.then_inc(biased, 1)

            def top(u):
                dve.wait_ge(biased, u + 1)
                return own.mark(nc.vector.tensor_reduce(col(u, 0), lg[:, u % 2, :, first(U[u][0]):256], AX.X, ALU.max))

            def with_sink(u, maximum):
                g = U[u][1]
                own.after(maximum)
                return own.mark(nc.vector.tensor_tensor(col(u, 1), col(u, 0), snk[:, 4 * g:4 * g + 4], ALU.max))

            def shifts(u, maximum):
                g = U[u][1]
                own.after(maximum)
                nc.vector.tensor_scalar(col(u, 2), col(u, 1), -1.0, None, ALU.mult)
                nc.vector.tensor_tensor(col(u, 3), snk[:, 4 * g:4 * g + 4], col(u, 1), ALU.subtract).then_inc(shifted, 1)

            def take(u):
                b0 = first(U[u][0]) // P
                dve.wait_ge(turned, 2 * u + 2)
                if u >= 2:
                    dve.wait_ge(mixed, u - 1)
                nc.vector.tensor_copy(pt[:, u % 2, 2:4, b0:2, :], tp[1][:, :].rearrange("p (e b t) -> p e b t", e=2, b=2)[:, :, b0:2, :]).then_inc(dve_taken, 1)
            dve.wait_ge(loaded, 16)
            for u in range(2):
                logits(u)
                shifts(u, with_sink(u, top(u)))
            take(0)
            for u in range(len(U)):
                if u + 2 < len(U):
                    logits(u + 2)
                    shifts(u + 2, with_sink(u + 2, top(u + 2)))
                dve.wait_ge(sunk, u + 1)
                total = own.mark(nc.vector.tensor_tensor(col(u, 6), col(u, 4), col(u, 5), ALU.add))
                if u + 1 < len(U):
                    take(u + 1)
                own.after(total)
                inverse = own.mark(nc.vector.reciprocal(col(u, 7), col(u, 6)))
                dve.wait_ge(mixed, u + 1)
                own.after(inverse)
                if u >= 2:
                    dve.wait_ge(gated, u - 1)
                nc.vector.tensor_tensor(tmp[:, u % 2, :].rearrange("p (e d) -> p e d", e=4), po[u % 2][:, 0:256].rearrange("p (e d) -> p e d", e=4),
                                        sm[:, u % 3, 7, :].unsqueeze(2).to_broadcast([P, 4, HD]), ALU.mult).then_inc(weighted, 1)

        @block.gpsimd
        def _(pool):
            for u, (n, g) in enumerate(U):
                pool.wait_ge(weighted, u + 1)
                zz = z[:, n, g * 256:(g + 1) * 256]
                nc.gpsimd.tensor_tensor(zz, zz, tmp[:, u % 2, :], ALU.mult).then_inc(gated, 1)


def stage_turn(nc, core, tag, src, n, out):
    turned, taken = [nc.alloc_semaphore(f"{tag}_turned{i}") for i in range(2)], [nc.alloc_semaphore(f"{tag}_taken{i}") for i in range(2)]
    with core.stage() as ctx:
        ps = banks(nc, ctx, f"{tag}_ps", 4)
        block = core.open_block(ctx)

        @block.tensor
        def _(pe):
            for k in range(n):
                if k >= 4:
                    pe.wait_ge(taken[k % 2], k // 2 - 1)
                for i in range(TT):
                    last = nc.tensor.transpose(ps[k % 4][:, i * P:(i + 1) * P], src[:, i, k * P:(k + 1) * P], core.c[:, C_IDENT:C_IDENT + P])
                last.then_inc(turned[k % 2], 1)

        @block.scalar
        def _(act):
            for k in range(0, n, 2):
                act.wait_ge(turned[0], k // 2 + 1)
                nc.scalar.activation(out[:, k, :], ps[k % 4][:, :], ACT.Copy).then_inc(taken[0], 1)

        @block.vector
        def _(dve):
            for k in range(1, n, 2):
                dve.wait_ge(turned[1], k // 2 + 1)
                nc.vector.tensor_copy(out[:, k, :], ps[k % 4][:, :]).then_inc(taken[1], 1)


def delta_block(nc, core, a):
    with ExitStack() as ctx:
        qk = sb(nc, ctx, "qk_t", [P, 2 * HA, T])
        with ExitStack() as c2:
            hw = sb(nc, c2, "h_t", [P, KD, T])
            c3 = c2.enter_context(ExitStack())
            h = sb_parts(nc, c3, "h_t", [P, KD, T], side="right")
            v = sb(nc, c2, "v_t", [P, 2 * HA, T])
            rows = sb(nc, c2, "gate_rows", [8, 2, T])
            cols = sb(nc, c2, "gate_cols", [P, 4, TT, HA])
            ss = sb(nc, c2, "o_squares", [P, TT, HA])
            stage_norm(nc, core, "na", x_tiles(core), V_ANORM, h, whole=hw)
            stage_proj_conv(nc, core, "pa", h, core.ta[:, 0:2 * HA, :], qk, [(0, T)], T)
            unit = UnitRows(nc, core, c3, qk)
            with core.together():
                unit.sums(v[:, 2 * HA - 2:2 * HA, :])
                stage_proj_conv(nc, core, "pv", h, core.ta[:, 2 * HA:, :], v, [(0, T)], T, shared_opening=False)
            with core.together():
                unit.scale()
                stage_delta_gates(nc, core, h, a["a_w_in"], rows, cols)
            c3.close()
            stage_delta_chunks(nc, core, qk, v, rows, cols, ss)
            o = v[:, :, :].rearrange("p (h j) (a d) -> p h (j a) d", j=2, a=2)
            stage_delta_out(nc, core, hw, o, ss[:, :, :], a["a_o_gain"], qk)
        stage_proj_n(nc, core, "oa", None, X_COLS, "vector", add_to_x(nc, core), whole=qk)


def window_block(nc, core, a, scratch):
    silu_to = lambda dst: (lambda c, i, product: nc.scalar.activation(dst[:, i, c * 512:(c + 1) * 512], product, ACT.Silu))
    with ExitStack() as ctx:
        q_t = sb(nc, ctx, "q_t", [P, HB * HD // P, T])
        with ExitStack() as c2:
            z = sb(nc, c2, "z", [P, TT, HB * HD])
            kv = sb(nc, c2, "kv", [P, TT, 2 * KVB * HD])
            k_t = sb(nc, c2, "k_t", [P, KVB, T])
            rq = sb(nc, c2, "rq", [P, TT, HB])
            table = Bias(nc, core)
            with ExitStack() as c3:
                h = sb_parts(nc, c3, "hb_t", [P, KD, T])
                with core.together():
                    stage_norm(nc, core, "nk", x_tiles(core), V_KVNORM, h)
                    table.rows(a["c32"], a["rel_bias"], scratch, z)
                stage_proj_n(nc, core, "pk", h, X_COLS, "scalar", lambda c, i, product: nc.scalar.activation(kv[:, i, :], product, ACT.Copy))
                with core.together():
                    stage_norm(nc, core, "nb", x_tiles(core), V_BNORM, h)
                    stage_shared_k(nc, core, kv, k_t)
                stage_proj_t(nc, core, "pq", h, q_t, [(0, T)])
                stage_proj_n(nc, core, "pz", h, X_COLS, "scalar", silu_to(z))
            with ExitStack() as c3:
                bias = sb(nc, c3, "bias", [P, HB, 256])
                with core.together():
                    stage_head_scale(nc, core, "hq", q_t, HB * HD // P, [i * P for i in range(TT)], rq[:, :, :], 1)
                    table.flip(scratch, sb(nc, core.shared[0], "rb_shifted", [P, HB, 256]), bias)
                stage_window_attention(nc, core, q_t, k_t, kv, rq, bias, a["b_sinks"], z)
            stage_turn(nc, core, "tb", z, HB * HD // P, q_t)
        stage_proj_n(nc, core, "ob", None, X_COLS, "vector", add_to_x(nc, core), whole=q_t)


S_TILES = [(META, 0, 0)] + [(P, META + P * i, P * i) for i in range(TT)]
HALF2 = T2 // 2
MQ, MV, MO, MI, MF, FQ, FV, FF = 0, 1024, 1536, 2048, 2052, 2056, 3080, 3592


def stage_mix_gates(nc, core, h_t, w, mrow, acol, emcol, negc):
    sem = lambda n: nc.alloc_semaphore(f"mg_{n}")
    zeroed, loaded, product, vstep, astep, turned, cast, cast_taken, split = map(
        sem, ("zeroed", "loaded", "product", "vector_step", "scalar_step", "turned", "cast", "cast_taken", "weights_split"))
    G = GATE_COLS
    with core.stage() as ctx:
        wg = sb(nc, ctx, "mg_w", [P, KD, G])
        wp = sb_parts(nc, ctx, "mg_wp", [P, KD, G])
        t = [sb(nc, ctx, f"mg_t{i}", [G, T2]) for i in range(4)]
        b = sb(nc, ctx, "mg_b", [HM, T2])
        am = sb(nc, ctx, "mg_am", [HM, 2, T2])
        nc8 = sb(nc, ctx, "mg_nc", [HF, T2])
        ps = banks(nc, ctx, "mg_ps", 2)
        pt = banks(nc, ctx, "mg_pt", 1)[0]
        pc = banks(nc, ctx, "mg_pc", 4)
        block = core.open_block(ctx)
        wv = w_view(w, KD)

        @block.sync
        def _(sp):
            sp.wait_ge(zeroed, 1)
            for dst, src, n in ((0, MI, HM), (32, MF, HM), (64, FF, HF)):
                with nc.allow_non_contiguous_dma("a few gate columns"):
                    sp.dma_start(wg[:, :, dst:dst + n], wv[:, :, src:src + n]).then_inc(loaded, 16)

        @block.tensor
        def _(pe):
            pe.wait_ge(split, 2)
            for half in range(2):
                for k in range(KD):
                    cols = slice(half * HALF2, (half + 1) * HALF2)
                    last = matmul_parts(nc, ps[half][0:G, 0:HALF2], (wp[0][:, k, :], wp[1][:, k, :]),
                                        (h_t[0][:, k, cols], h_t[1][:, k, cols]), k == 0, k == KD - 1)
            last.then_inc(product, 1)
            pe.wait_ge(vstep, 10)
            pe.wait_ge(astep, 3)
            for j, (rows, c, _t) in enumerate(S_TILES):
                nc.tensor.transpose(pt[0:rows, j * 4:j * 4 + 4], am[:, 0, c:c + rows], core.c[0:HM, C_IDENT:C_IDENT + HM])
            for i in range(TT):
                c = META + i * P
                last = nc.tensor.transpose(pt[:, 32 + i * 4:36 + i * 4], am[:, 1, c:c + P], core.c[0:HM, C_IDENT:C_IDENT + HM])
            last.then_inc(turned, 1)
            for u in range(2 * HF):
                h, half = divmod(u, 2)
                if u >= 4:
                    pe.wait_ge(cast_taken, u - 3)
                nc.tensor.matmul(pc[u % 4][:, 0:HALF2], core.r[0:HF, R_SEL + h * P:R_SEL + (h + 1) * P],
                                 nc8[:, half * HALF2:(half + 1) * HALF2], start=True, stop=True).then_inc(cast, 1)

        @block.scalar
        def _(act):
            act.wait_ge(vstep, 3)
            nc.scalar.activation(t[1][:, :], t[1][:, :], ACT.Exp, scale=-1.0).then_inc(astep, 1)
            act.wait_ge(astep, 1)
            nc.scalar.activation(t[1][:, :], t[1][:, :], ACT.Ln, bias=1.0).then_inc(astep, 1)
            act.wait_ge(vstep, 10)
            nc.scalar.activation(am[:, 1, :], am[:, 1, :], ACT.Exp, scale=-1.0).then_inc(astep, 1)
            for u in range(2 * HF):
                h, half = divmod(u, 2)
                act.wait_ge(cast, u + 1)
                nc.scalar.activation(negc[:, h, half * HALF2:(half + 1) * HALF2], pc[u % 4][:, 0:HALF2], ACT.Copy).then_inc(cast_taken, 1)

        @block.vector
        def _(dve):
            nc.vector.memset(wg[:, :, :], 0.0).then_inc(zeroed, 1)
            dve.wait_ge(loaded, 48)
            split_small(nc, dve, wg, wp, split)
            then = Chain(dve, vstep)
            dve.wait_ge(product, 1)
            for half in range(2):
                then(nc.vector.tensor_scalar(t[0][:, half * HALF2:(half + 1) * HALF2], ps[half][0:G, 0:HALF2], core.v[0:G, V_BI:V_BI + 1], None, ALU.add))
            then(nc.vector.scalar_tensor_tensor(t[1][:, :], t[0][:, :], -1.0, t[0][:, :], ALU.mult, ALU.max))
            dve.wait_ge(astep, 2)
            then(nc.vector.scalar_tensor_tensor(t[2][:, :], t[0][:, :], 0.0, t[1][:, :], ALU.min, ALU.subtract))
            then(nc.vector.tensor_tensor_scan(t[3][:, :], core.one[0:G, :], t[2][:, :], 0.0, ALU.mult, ALU.add))
            then(nc.vector.tensor_copy(b[:, :], t[3][32:32 + HM, :]))
            then(nc.vector.tensor_scalar(nc8[:, :], t[3][64:64 + HF, :], -1.0, None, ALU.mult))
            then(nc.vector.tensor_tensor(am[:, 0, :], t[0][0:HM, :], b[:, :], ALU.subtract))
            then(nc.vector.tensor_tensor_scan(mrow[:, :], am[:, 0, :], am[:, 0, :], 0.0, ALU.max, ALU.max))
            then(nc.vector.tensor_tensor(am[:, 1, :], b[:, :], mrow[:, :], ALU.add))
            dve.wait_ge(turned, 1)
            nc.vector.tensor_copy(acol[:, 1:, :], pt[:, 4:20].rearrange("p (j h) -> p j h", h=4))
            nc.vector.tensor_copy(acol[0:META, 0, :], pt[0:META, 0:4])
            nc.vector.tensor_copy(emcol[:, :, :], pt[:, 32:48].rearrange("p (j h) -> p j h", h=4))


def stage_mlstm(nc, core, qk, v, mrow, acol, nd):
    sem = lambda n: nc.alloc_semaphore(f"ml_{n}")
    cast, shifted, expd, masked, scored, weighted, mixed, taken = map(
        sem, ("cast", "shifted", "expd", "masked", "scored", "weighted", "mixed", "taken"))
    offs, o = [], 0
    for j, (rows, c, t0) in enumerate(S_TILES):
        offs.append(o)
        o += T - t0
    N = len(S_TILES)
    with core.stage() as ctx:
        ew = sb(nc, ctx, "ml_ew", [P, 2, o])
        pm = banks(nc, ctx, "ml_pm", 2)
        psc = banks(nc, ctx, "ml_ps", 4)
        po = banks(nc, ctx, "ml_po", 2)
        block = core.open_block(ctx)
        e = lambda h, j, a=0, n=None: ew[0:S_TILES[j][0], h % 2, offs[j] + a:offs[j] + (T - S_TILES[j][2] if n is None else a + n)]

        @block.tensor
        def _(pe):
            for h in range(HM):
                if h >= 2:
                    pe.wait_ge(shifted, N * (h - 1))
                nc.tensor.matmul(pm[h % 2][:, :], core.r[0:HM, R_SEL + h * P:R_SEL + (h + 1) * P], mrow[:, META:], start=True, stop=True).then_inc(cast, 1)
                for j, (rows, c, t0) in enumerate(S_TILES):
                    u = h * N + j
                    if u >= 4:
                        pe.wait_ge(weighted, u - 3)
                    nc.tensor.matmul(psc[u % 4][0:rows, 0:T - t0], qk[:, HM + h, c:c + rows], qk[:, h, META + t0:T2], start=True, stop=True).then_inc(scored, 1)
                for i in range(TT):
                    u = h * TT + i
                    if u >= 2:
                        pe.wait_ge(taken, u - 1)
                    pe.wait_ge(weighted, h * N + i + 2)
                    for j in range(i + 2):
                        rows, c, t0 = S_TILES[j]
                        last = nc.tensor.matmul(po[u % 2][:, 0:DM + 1], e(h, j, i * P - t0, P), v[0:rows, j, h, :], start=(j == 0), stop=(j == i + 1))
                    last.then_inc(mixed, 1)

        @block.vector
        def _(dve):
            for h in range(HM):
                dve.wait_ge(cast, h + 1)
                if h >= 2:
                    dve.wait_ge(mixed, TT * (h - 1))
                for j, (rows, c, t0) in enumerate(S_TILES):
                    nc.vector.tensor_scalar(e(h, j), pm[h % 2][0:rows, t0:T], acol[0:rows, j, h:h + 1], 0.0, ALU.subtract, ALU.max).then_inc(shifted, 1)
                for j, (rows, c, t0) in enumerate(S_TILES):
                    u = h * N + j
                    dve.wait_ge(scored, u + 1)
                    dve.wait_ge(expd, u + 1)
                    if j:
                        dve.wait_ge(masked, h * TT + j)
                    nc.vector.scalar_tensor_tensor(e(h, j), psc[u % 4][0:rows, 0:T - t0], DM ** -0.5, e(h, j), ALU.mult, ALU.mult).then_inc(weighted, 1)

        @block.scalar
        def _(act):
            for h in range(HM):
                for j in range(N):
                    act.wait_ge(shifted, h * N + j + 1)
                    nc.scalar.activation(e(h, j), e(h, j), ACT.Exp, scale=-1.0).then_inc(expd, 1)
                for i in range(TT):
                    u = h * TT + i
                    act.wait_ge(mixed, u + 1)
                    nc.scalar.activation(nd[:, i, h, :], po[u % 2][:, 0:DM + 1], ACT.Copy).then_inc(taken, 1)

        @block.gpsimd
        def _(pool):
            for h in range(HM):
                for j in range(1, N):
                    pool.wait_ge(expd, h * N + j + 1)
                    nc.gpsimd.tensor_tensor(e(h, j, 0, P), e(h, j, 0, P), core.c[:, C_LE:C_LE + P], ALU.mult).then_inc(masked, 1)


def stage_mlstm_out(nc, core, nd, emcol, so, gain, y):
    sem = lambda n: nc.alloc_semaphore(f"mo_{n}")
    loaded, step, divided, squared, meaned, rooted = map(sem, ("loaded", "step", "divided", "squared", "meaned", "rooted"))
    with core.stage() as ctx:
        gb = sb(nc, ctx, "mo_gain", [P, HM * DM])
        r = sb(nc, ctx, "mo_r", [P, 6, TT * HM])
        sq = sb(nc, ctx, "mo_sq", [P, TT, HM * DM])
        block = core.open_block(ctx)
        th = lambda k: r[:, k, :].rearrange("p (i h) -> p i h", h=HM)
        wide = lambda k: th(k).unsqueeze(3).to_broadcast([P, TT, HM, DM])
        yh = y[:, :, 0:HM * DM].rearrange("p i (h d) -> p i h d", h=HM)
        ym = y[:, :, 0:HM * DM]

        @block.sync
        def _(sp):
            sp.dma_start(gb[:, :], gain.partition_broadcast(P)).then_inc(loaded, 16)

        @block.scalar
        def _(act):
            act.wait_ge(divided, 1)
            nc.scalar.activation(sq[:, :, :], ym, ACT.Square).then_inc(squared, 1)

        @block.gpsimd
        def _(pool):
            pool.wait_ge(meaned, 1)
            nc.gpsimd.tensor_tensor(r[:, 5, :], r[:, 4, :], core.c[:, C_MHALF:C_MHALF + 1].to_broadcast([P, TT * HM]), ALU.pow).then_inc(rooted, 1)

        @block.vector
        def _(dve):
            then = Chain(dve, step)
            den = nd[:, :, :, DM]
            then(nc.vector.scalar_tensor_tensor(th(0), den, -1.0, den, ALU.mult, ALU.max))
            then(nc.vector.tensor_tensor(th(1), th(0), emcol, ALU.max))
            then(nc.vector.reciprocal(r[:, 2, :], r[:, 1, :]))
            nc.vector.tensor_tensor(yh, nd[:, :, :, 0:DM], wide(2), ALU.mult).then_inc(divided, 1)
            dve.wait_ge(squared, 1)
            then(nc.vector.tensor_reduce(r[:, 3, :], sq[:, :, :].rearrange("p i (h d) -> p (i h) d", h=HM), AX.X, ALU.add))
            nc.vector.tensor_scalar(r[:, 4, :], r[:, 3, :], 1.0 / DM, EPS, ALU.mult, ALU.add).then_inc(meaned, 1)
            dve.wait_ge(rooted, 1)
            then(nc.vector.tensor_tensor(yh, yh, wide(5), ALU.mult))
            dve.wait_ge(loaded, 16)
            then(nc.vector.tensor_tensor(ym, ym, gb[:, :].unsqueeze(1).to_broadcast([P, TT, HM * DM]), ALU.mult))
            then(nc.vector.tensor_tensor(ym, ym, so[:, :, :], ALU.mult))


def stage_key_scale(nc, core, k_t):
    sem = lambda n: nc.alloc_semaphore(f"ks_{n}")
    gained, squared, summed, rooted, inverted, scaled = map(sem, ("gained", "squared", "summed", "rooted", "inverted", "scaled"))
    with core.stage() as ctx:
        g = sb(nc, ctx, "ks_g", [P, 1])
        sq = sb(nc, ctx, "ks_sq", [P, 4, HALF2])
        rt = sb(nc, ctx, "ks_rt", [P, 4, HALF2])
        ps = banks(nc, ctx, "ks_ps", 4)
        block = core.open_block(ctx)
        part = lambda u: k_t[:, u // 2, u % 2 * HALF2:(u % 2 + 1) * HALF2]
        N = 8

        @block.scalar
        def _(act):
            for b in range(0, N, 4):
                for u in range(b, b + 4):
                    if u >= 4:
                        act.wait_ge(summed, u - 3)
                    nc.scalar.activation(sq[:, u % 4, :], part(u), ACT.Square).then_inc(squared, 1)
                for u in range(b, b + 4):
                    act.wait_ge(summed, u + 1)
                    if u >= 4:
                        act.wait_ge(scaled, u - 3)
                    nc.scalar.activation(rt[:, u % 4, :], ps[u % 4][:, 0:HALF2], ACT.Sqrt, bias=core.eps[:, 0:1], scale=1.0 / DF).then_inc(rooted, 1)

        @block.tensor
        def _(pe):
            for u in range(N):
                pe.wait_ge(squared, u + 1)
                if u >= 4:
                    pe.wait_ge(rooted, u - 3)
                nc.tensor.matmul(ps[u % 4][:, 0:HALF2], core.c[:, C_HALVES:C_HALVES + P], sq[:, u % 4, :], start=True, stop=True).then_inc(summed, 1)

        @block.vector
        def _(dve):
            nc.vector.tensor_tensor(g[:, :], core.v[:, V_FQK:V_FQK + 1], core.v[:, V_FQK + 1:V_FQK + 2], ALU.mult).then_inc(gained, 1)
            dve.wait_ge(gained, 1)
            for u in range(N):
                dve.wait_ge(rooted, u + 1)
                nc.vector.reciprocal(rt[:, u % 4, :], rt[:, u % 4, :]).then_inc(inverted, 1)
                dve.wait_ge(inverted, u + 1)
                nc.vector.scalar_tensor_tensor(part(u), part(u), g[:, 0:1], rt[:, u % 4, :], ALU.mult, ALU.mult).then_inc(scaled, 1)


def stage_forgetting_attention(nc, core, qk, v, rq, negc, y):
    sem = lambda n: nc.alloc_semaphore(f"fa_{n}")
    (scored, biased, step, shifted, expd, turned_a, turned_b, act_taken, dve_taken, mixed, weighted) = map(sem, (
        "scored", "biased", "step", "shifted", "expd", "turned_a", "turned_b", "scalar_taken", "vector_taken", "mixed", "weighted"))
    ident = core.c[:, C_IDENT:C_IDENT + P]
    U = [(h, i) for h in range(HF) for i in range(TT)]
    nb = lambda u: sum(1 for w in range(u + 1) if U[w][1] >= 2)
    with core.stage() as ctx:
        lg = sb(nc, ctx, "fa_lg", [P, 2, T2])
        pt = sb(nc, ctx, "fa_pt", [P, 2, 5, P])
        sm = sb(nc, ctx, "fa_sm", [P, 3, 4])
        sc = [banks(nc, ctx, f"fa_sc{e}", 2) for e in range(2)]
        tp = banks(nc, ctx, "fa_tp", 2)
        po = banks(nc, ctx, "fa_po", 2)
        block = core.open_block(ctx)
        width = lambda i: META + P * (i + 1)
        col = lambda u, k: sm[:, u % 3, k:k + 1]

        @block.tensor
        def _(pe):
            def scores(u):
                h, i = U[u]
                half, hw = slice(64 * (h % 2), 64 * (h % 2) + 64), width(i) // 2
                if u >= 2:
                    pe.wait_ge(biased, u - 1)
                for p in range(2):
                    last = nc.tensor.matmul(sc[p][u % 2][:, 0:hw], qk[half, h // 2, META + i * P:META + (i + 1) * P],
                                            qk[half, 4 + h // 2, p * hw:(p + 1) * hw], start=True, stop=True)
                last.then_inc(scored, 1)
            def turn(u):
                h, i = U[u]
                pe.wait_ge(expd, u + 1)
                if u:
                    pe.wait_ge(act_taken, u)
                for j in range(min(3, i + 2)):
                    rows, c, _t = S_TILES[j]
                    last = nc.tensor.transpose(tp[0][0:rows, j * P:(j + 1) * P], lg[:, u % 2, c:c + rows], ident)
                last.then_inc(turned_a, 1)
                if i >= 2:
                    if nb(u) > 1:
                        pe.wait_ge(dve_taken, nb(u) - 1)
                    for j in range(3, i + 2):
                        rows, c, _t = S_TILES[j]
                        last = nc.tensor.transpose(tp[1][:, (j - 3) * P:(j - 2) * P], lg[:, u % 2, c:c + rows], ident)
                    last.then_inc(turned_b, 1)

            def mix(u):
                h, i = U[u]
                if u >= 2:
                    pe.wait_ge(weighted, u - 1)
                pe.wait_ge(act_taken, u + 1)
                if i >= 2:
                    pe.wait_ge(dve_taken, nb(u))
                for j in range(i + 2):
                    rows, c, _t = S_TILES[j]
                    last = nc.tensor.matmul(po[u % 2][:, 0:DF], pt[0:rows, u % 2, j, :], v[0:rows, j, h * DF:(h + 1) * DF], start=(j == 0), stop=(j == i + 1))
                last.then_inc(mixed, 1)
            for u in range(3):
                scores(u)
            turn(0)
            for u in range(len(U)):
                if u + 3 < len(U):
                    scores(u + 3)
                if u + 1 < len(U):
                    turn(u + 1)
                mix(u)

        @block.scalar
        def _(act):
            def exp(u):
                i = U[u][1]
                act.wait_ge(shifted, u + 1)
                nc.scalar.activation(lg[:, u % 2, 0:width(i)], lg[:, u % 2, 0:width(i)], ACT.Exp, bias=col(u, 1), accum_out=col(u, 2)).then_inc(expd, 1)

            def take(u):
                act.wait_ge(turned_a, u + 1)
                if u >= 2:
                    act.wait_ge(mixed, u - 1)
                n = min(2, U[u][1] + 1)
                nc.scalar.activation(pt[0:META, u % 2, 0, :], tp[0][0:META, 0:P], ACT.Copy)
                nc.scalar.activation(pt[:, u % 2, 1:1 + n, :], tp[0][:, P:P + n * P].rearrange("p (j t) -> p j t", t=P), ACT.Copy).then_inc(act_taken, 1)
            exp(0)
            exp(1)
            take(0)
            for u in range(len(U)):
                if u + 2 < len(U):
                    exp(u + 2)
                if u + 1 < len(U):
                    take(u + 1)

        @block.vector
        def _(dve):
            own = Marks(dve, step)

            def logits(u):
                h, i = U[u]
                hw = width(i) // 2
                dve.wait_ge(scored, u + 1)
                if u >= 2:
                    dve.wait_ge(turned_a, u - 1)
                    if nb(u - 2):
                        dve.wait_ge(turned_b, nb(u - 2))
                for p in range(2):
                    c = slice(p * hw, (p + 1) * hw)
                    last = nc.vector.scalar_tensor_tensor(lg[:, u % 2, c], sc[p][u % 2][:, 0:hw], rq[:, i, h:h + 1], negc[:, h, c], ALU.mult, ALU.add)
                last.then_inc(biased, 1)

            def causal(u):
                w = width(U[u][1])
                dve.wait_ge(biased, u + 1)
                return own.mark(nc.vector.tensor_tensor(lg[:, u % 2, w - P:w], lg[:, u % 2, w - P:w], core.c[:, C_NEGDIAG:C_NEGDIAG + P], ALU.add))

            def top(u, masked):
                own.after(masked)
                return own.mark(nc.vector.tensor_reduce(col(u, 0), lg[:, u % 2, 0:width(U[u][1])], AX.X, ALU.max))

            def shift(u, maximum):
                own.after(maximum)
                nc.vector.tensor_scalar(col(u, 1), col(u, 0), -1.0, None, ALU.mult).then_inc(shifted, 1)

            def take(u):
                i = U[u][1]
                if i >= 2:
                    dve.wait_ge(turned_b, nb(u))
                    dve.wait_ge(mixed, u - 1)
                    nc.vector.tensor_copy(pt[:, u % 2, 3:i + 2, :], tp[1][:, 0:(i - 1) * P].rearrange("p (j t) -> p j t", t=P)).then_inc(dve_taken, 1)
            for u in range(2):
                logits(u)
                shift(u, top(u, causal(u)))
            take(0)
            for u, (h, i) in enumerate(U):
                if u + 2 < len(U):
                    logits(u + 2)
                    shift(u + 2, top(u + 2, causal(u + 2)))
                dve.wait_ge(expd, u + 1)
                inverse = own.mark(nc.vector.reciprocal(col(u, 3), col(u, 2)))
                if u + 1 < len(U):
                    take(u + 1)
                own.after(inverse)
                dve.wait_ge(mixed, u + 1)
                nc.vector.tensor_scalar(y[:, i, HM * DM + h * DF:HM * DM + (h + 1) * DF], po[u % 2][:, 0:DF], col(u, 3), None, ALU.mult).then_inc(weighted, 1)


def mixers(nc, core, a):
    meta_loaded = nc.alloc_semaphore("meta_loaded")
    with ExitStack() as outer:
        xm, core.one = sb(nc, outer, "meta_sb", [META, D]), sb(nc, outer, "one_sb", [P, T2])
        tiles = [(xm[:, :], META, 0)] + [(core.x[:, i, :], P, META + i * P) for i in range(TT)]
        y = sb(nc, outer, "y", [P, TT, D])
        with ExitStack() as ctx:
            mqk = sb(nc, ctx, "mqk_t", [P, 2 * HM, T2])
            fqk = sb(nc, ctx, "fqk_t", [P, 8, T2])
            vm = sb(nc, ctx, "vm", [P, 5, HM, DM + 1])
            vf = sb(nc, ctx, "vf", [P, 5, HF * DF])
            so = sb(nc, ctx, "so", [P, TT, HM * DM])
            mrow = sb(nc, ctx, "m_row", [HM, T2])
            acol = sb(nc, ctx, "a_col", [P, 5, HM])
            emcol = sb(nc, ctx, "em_col", [P, TT, HM])
            rq = sb(nc, ctx, "rq2", [P, TT, HF])
            c2 = ctx.enter_context(ExitStack())
            with ExitStack() as c3:
                h = sb_parts(nc, c3, "h2_t", [P, KD, T2], side="right")
                with nc.Block() as block:
                    @block.sync
                    def _(sp):
                        sp.dma_start(xm[:, :], a["meta"]).then_inc(meta_loaded, 16)
                        sp.wait_ge(meta_loaded, 16)

                    @block.vector
                    def _(dve):
                        nc.vector.memset(vm[:, :, :, DM:DM + 1], 1.0)
                        nc.vector.memset(core.one[:, :], 1.0)
                stage_norm(nc, core, "n2", tiles, V_NORM2, h)
                stage_proj_conv(nc, core, "pm", h, core.tm, mqk, [(0, HALF2), (HALF2, HALF2)], T2)
                stage_proj_t(nc, core, "pf", h, fqk, [(0, HALF2), (HALF2, HALF2)])

                def values(c, j, product):
                    rows = S_TILES[j][0]
                    if c == 0:
                        return nc.scalar.activation(vm[0:rows, j, :, 0:DM], product.rearrange("p (h d) -> p h d", h=HM), ACT.Copy)
                    return nc.scalar.activation(vf[0:rows, j, :], product, ACT.Copy)
                stage_proj_n(nc, core, "pw", h, [(rows, c) for rows, c, _ in S_TILES], "scalar", values)
                stage_proj_n(nc, core, "po", h, [(P, META + i * P) for i in range(TT)], "scalar",
                             lambda c, i, product: nc.scalar.activation(so[:, i, :], product, ACT.Sigmoid))
                negc = sb(nc, c2, "negc", [P, HF, T2])
                stage_mix_gates(nc, core, h, a["w_in_2"], mrow, acol, emcol, negc)
            with ExitStack() as c3:
                nd = sb(nc, c3, "nd", [P, TT, HM, DM + 1])
                stage_mlstm(nc, core, mqk, vm, mrow, acol, nd)
                with core.together():
                    stage_head_scale(nc, core, "hf", fqk[:, 0:4, META:], 4, [i * P for i in range(TT)], rq[:, :, :], 1)
                    stage_key_scale(nc, core, fqk[:, 4:8, :])
                    stage_mlstm_out(nc, core, nd, emcol[:, :, :], so, a["m_out_norm_2"], y)
            stage_forgetting_attention(nc, core, fqk, vf, rq, negc, y)
        y_t = sb(nc, outer, "y_t", [P, KD, T])
        stage_turn(nc, core, "t2", y, KD, y_t)
        stage_proj_n(nc, core, "o2", None, X_COLS, "vector", add_to_x(nc, core), whole=y_t)


def weights_plan(a):
    wi, w2 = a["a_w_in"], a["w_in_2"]
    wide = lambda n0, n: [n0 + 512 * g for g in range(n)]
    return [
        Weights(wi, KD, 0, 2 * HA * P // 256), Weights(wi, KD, 2 * HA * P, 2 * HA * P // 256),
        Weights(wi, KD, groups=wide(QKV_TILES * P, 4)), Weights(a["a_w_out"], HA * DV // P, groups=wide(0, 2)),
        Weights(a["w_kv"], KD, groups=[0]), Weights(a["b_w_in"], KD, 0, HB * HD // 256),
        Weights(a["b_w_in"], KD, groups=wide(HB * HD, 4)), Weights(a["b_w_out"], HB * HD // P, groups=wide(0, 2)),
        Weights(w2, KD, MQ, 4), Weights(w2, KD, FQ, 4), Weights(w2, KD, groups=[MV, FV]), Weights(w2, KD, groups=[MO]),
        Weights(a["w_out_2"], KD, groups=wide(0, 2)), Weights(a["peer_query"], KD, 0, 8),
    ]


class Query:
    STEPS = 2 * PH

    def __init__(self, nc, core, ctx, h, scores):
        self.nc, self.ring, self.w, self.h, self.scores = nc, core.ring, core.ring.take(), h, scores
        self.base = self.ring.filled
        self.keys_loaded, self.product, self.copied, self.scored, self.kept = (
            nc.alloc_semaphore(f"qu_{n}") for n in ("keys_loaded", "product", "copied", "scored", "kept"))
        self.keys = sb(nc, ctx, "qu_keys", [P, 2 * PH, NK])
        self.q = sb(nc, ctx, "qu_q", [P, 2, 3 * P])
        self.qp, self.sp = banks(nc, ctx, "qu_qp", 2), banks(nc, ctx, "qu_sp", 2)

    def tiles(self, n):
        return range(1) if n < PH else range(1, TT)

    def loads(self, sp, keys):
        sp.dma_start(self.keys[:, :, :], keys).then_inc(self.keys_loaded, 16)
        for n in range(2, self.STEPS):
            sp.wait_ge(self.product, 2 * n - 2)
            self.ring.order(sp, self.w, n % PH, n % 2)

    def queries(self, pe, n):
        nc, tiles = self.nc, self.tiles(n)
        width = len(tiles) * P
        w = self.w.shaped(self.ring.raw[n % 2])
        pe.wait_ge(self.ring.loaded[n % 2], 16 * (self.base + n // 2) + 16)
        for j in range(2):
            if n:
                pe.wait_ge(self.copied, 2 * n - 1 + j)
            for k in range(KD):
                last = nc.tensor.matmul(self.qp[j][:, 0:width], w[:, k, j * P:(j + 1) * P], self.h[:, k, tiles[0] * P:tiles[0] * P + width],
                                        start=(k == 0), stop=(k == KD - 1))
            last.then_inc(self.product, 1)

    def dots(self, pe, n):
        nc = self.nc
        if n == 0:
            pe.wait_ge(self.keys_loaded, 16)
        pe.wait_ge(self.copied, 2 * n + 2)
        for m, tile in enumerate(self.tiles(n)):
            if n or m == 2:
                pe.wait_ge(self.kept, self.kepts(n, m))
            for j in range(2):
                last = nc.tensor.matmul(self.sp[m % 2][:, j * P + m // 2 * 2 * P:(j + 1) * P + m // 2 * 2 * P], self.q[:, j, m * P:(m + 1) * P],
                                        self.keys[:, 2 * (n % PH) + j, :], start=True, stop=True)
            last.then_inc(self.scored, 1)

    def count(self, n):
        return n if n < PH else PH + 3 * (n - PH)

    def kepts(self, n, m):
        return self.count(n) + (1 if m == 2 else 0)

    def copy_queries(self, act, n):
        width = len(self.tiles(n)) * P
        for j in range(2):
            act.wait_ge(self.product, 2 * n + j + 1)
            if n:
                act.wait_ge(self.scored, self.count(n))
            self.nc.scalar.activation(self.q[:, j, 0:width], self.qp[j][:, 0:width], ACT.Copy).then_inc(self.copied, 1)

    def keep_scores(self, act, n):
        for m, tile in enumerate(self.tiles(n)):
            act.wait_ge(self.scored, self.count(n) + m + 1)
            at = 2 * (n % PH)
            self.nc.scalar.activation(self.scores[:, tile, at:at + 2, :],
                                      self.sp[m % 2][:, m // 2 * 2 * P:(m // 2 + 1) * 2 * P].rearrange("p (n k) -> p n k", n=2),
                                      ACT.Copy).then_inc(self.kept, 1)


class TopK:
    PIECES = 4
    HEADS = PH // PIECES

    def __init__(self, nc, core, ctx, scores, ids, gate):
        self.nc, self.core, self.scores, self.ids, self.gate = nc, core, scores, ids, gate
        self.step, self.shifted, self.expd, self.ids_ready = (nc.alloc_semaphore(f"tk_{n}") for n in ("step", "shifted", "expd", "ids_ready"))
        n = self.HEADS
        self.cd = sb(nc, ctx, "tk_cd", [P, n, 256])
        self.eq = sb(nc, ctx, "tk_eq", [P, n, 16, 16])
        self.vv = sb(nc, ctx, "tk_vv", [P, 2 * n, TOPK])
        self.ii = sb(nc, ctx, "tk_ii", [P, 2 * n, TOPK], U32)
        self.fi = sb(nc, ctx, "tk_fi", [P, 2 * n, TOPK])
        self.ts = sb(nc, ctx, "tk_ts", [P, n, TOPK])
        self.tp = sb(nc, ctx, "tk_tp", [P, n, TOPK], U32)
        self.hl = sb(nc, ctx, "tk_hl", [P, 2, n * TOPK], U32)
        self.hf = sb(nc, ctx, "tk_hf", [P, 2, n * TOPK])
        self.pick = sb(nc, ctx, "tk_pick", [P, 3, n * TOPK])
        self.ex = sb(nc, ctx, "tk_ex", [P, PH, TOPK])
        self.den = sb(nc, ctx, "tk_den", [P, 2, PH])
        self.then = None

    def top16(self, n, scores, values, index):
        nc, then = self.nc, self.then
        for r in range(n):
            last = nc.vector.max(values[:, r, 0:8], scores[:, r, :])
        then(last)
        for r in range(n):
            last = nc.vector.max_index(index[:, r, 0:8], values[:, r, 0:8], scores[:, r, :])
        then(last)
        for r in range(n):
            last = nc.vector.match_replace(scores[:, r, :], values[:, r, 0:8], scores[:, r, :], -3.0e38)
        then(last)
        for r in range(n):
            last = nc.vector.max(values[:, r, 8:16], scores[:, r, :])
        then(last)
        for r in range(n):
            last = nc.vector.max_index(index[:, r, 8:16], values[:, r, 8:16], scores[:, r, :])
        then(last)

    def lists(self, tile, p):
        n = self.HEADS
        self.top16(2 * n, self.scores[:, tile, 2 * n * p:2 * n * (p + 1), :], self.vv, self.ii)

    def choose(self, tile, p):
        nc, then, n = self.nc, self.then, self.HEADS
        pair = lambda ap, k: ap[:, :, :].rearrange("p (h two) k -> p h two k", two=2)[:, :, k, :]
        nc.vector.tensor_copy(self.fi[:, :, :], self.ii[:, :, :])
        then(nc.vector.tensor_tensor(self.cd[:, :, :].rearrange("p h (i j) -> p h i j", i=16),
                                     pair(self.vv, 0).unsqueeze(3).to_broadcast([P, n, 16, 16]),
                                     pair(self.vv, 1).unsqueeze(2).to_broadcast([P, n, 16, 16]), ALU.add))
        self.top16(n, self.cd, self.ts, self.tp)
        flat = self.tp[:, :, :].rearrange("p h k -> p (h k)")
        nc.vector.tensor_scalar(self.hl[:, 0, :], flat, 4, None, ALU.logical_shift_right)
        then(nc.vector.tensor_scalar(self.hl[:, 1, :], flat, 15, None, ALU.bitwise_and))
        then(nc.vector.tensor_copy(self.hf[:, :, :], self.hl[:, :, :]))
        for k in range(2):
            e3 = self.eq[:, :, :, :].rearrange("p h k i -> p (h k) i")
            then(nc.vector.tensor_tensor(e3, self.hf[:, k, :].unsqueeze(2).to_broadcast([P, n * TOPK, 16]),
                                         self.core.c[:, C_IOTA:C_IOTA + 16].unsqueeze(1).to_broadcast([P, n * TOPK, 16]), ALU.is_equal))
            then(nc.vector.tensor_tensor(self.eq[:, :, :, :], self.eq[:, :, :, :], pair(self.fi, k).unsqueeze(2).to_broadcast([P, n, 16, 16]), ALU.mult))
            then(nc.vector.tensor_reduce(self.pick[:, k, :], e3, AX.X, ALU.add))
        then(nc.vector.scalar_tensor_tensor(self.pick[:, 2, :], self.pick[:, 0, :], float(NK), self.pick[:, 1, :], ALU.mult, ALU.add))
        nc.vector.tensor_copy(self.ids[:, tile, n * TOPK * p:n * TOPK * (p + 1)], self.pick[:, 2, :]).then_inc(self.ids_ready, 1)
        nc.vector.tensor_tensor(self.ex[:, n * p:n * (p + 1), :], self.ts[:, :, :], self.ts[:, :, 0:1].to_broadcast([P, n, TOPK]),
                                ALU.subtract).then_inc(self.shifted, 1)

    def gates(self, dve, tile):
        nc, then = self.nc, self.then
        dve.wait_ge(self.expd, tile + 1)
        then(nc.vector.tensor_reduce(self.den[:, 0, :], self.ex[:, :, :], AX.X, ALU.add))
        then(nc.vector.reciprocal(self.den[:, 1, :], self.den[:, 0, :]))
        then(nc.vector.tensor_tensor(self.gate[:, tile, :].rearrange("p (h k) -> p h k", h=PH), self.ex[:, :, :],
                                     self.den[:, 1, :].unsqueeze(2).to_broadcast([P, PH, TOPK]), ALU.mult))

    def exp(self, act, tile):
        act.wait_ge(self.shifted, self.PIECES * (tile + 1))
        self.nc.scalar.activation(self.ex[:, :, :], self.ex[:, :, :], ACT.Exp).then_inc(self.expd, 1)


RING = 4
ROUNDS = SLOTS // (2 * RING)
QUARTER = ROUNDS // TopK.PIECES
PIECE_AT = [5, 8, 11, 13]
GATES_AT = ROUNDS - 1
EARLY = PH // 2
QUERY_AT = [2, 4, 6, 8]


def segments(tile):
    ends = sorted({*PIECE_AT, *(r + 1 for r in PIECE_AT), GATES_AT, ROUNDS, *(QUERY_AT if tile == 0 else ())})
    return list(zip([0, *ends], ends))


def stage_experts(nc, core, xn, h, gain, keys, scores, ids, gate, u_emb, v_emb, out):
    sem = lambda n: nc.alloc_semaphore(f"ex_{n}")
    two = lambda n: [sem(f"{n}{i}") for i in range(2)]
    staged, u_in, v_in, dotted, gelud, weighed, spread, mixed = map(
        two, ("staged", "u_loaded", "v_loaded", "dotted", "gelud", "weighed", "spread", "mixed"))
    gained, zeroed, closed, copied, stored, gloaded, passed = map(sem, (
        "gained", "zeroed", "closed", "copied", "stored", "gain_loaded", "wait_passed"))
    ident = core.c[:, C_IDENT:C_IDENT + P]
    with core.stage() as ctx:
        query = Query(nc, core, ctx, h, scores)
        topk = TopK(nc, core, ctx, scores, ids, gate)
        ur = [[sb(nc, ctx, f"ex_u{b}_{r}", [P, D]) for r in range(RING)] for b in range(2)]
        vr = [[sb(nc, ctx, f"ex_v{b}_{r}", [P, D]) for r in range(RING)] for b in range(2)]
        stg = [[sb(nc, ctx, f"ex_stage{b}_{s}", [P, RING], U32) for s in "uv"] for b in range(2)]
        dot, gel, wgt = ([sb(nc, ctx, f"ex_{n}{b}", [P, RING]) for b in range(2)] for n in ("dot", "gel", "wgt"))
        diag = [sb(nc, ctx, f"ex_diag{b}", [P, RING, P]) for b in range(2)]
        zero = sb(nc, ctx, "ex_zero", [P, P])
        gb = ur[1][RING - 1][:, :]
        ob = core.ring.raw[1][:, 0:D]
        acc = [[ctx.enter_context(nc.psum_tensor(f"ex_acc{b}{i}", [P, 512], F32)) for i in range(2)] for b in range(2)]
        block = core.open_block(ctx)
        at = lambda tile, i: tile * ROUNDS + i

        @block.sync
        def _(sp):
            sp.dma_start(gb, gain.partition_broadcast(P)).then_inc(gloaded, 16)
            query.loads(sp, keys)
            for tile in range(TT):
                sp.wait_ge(copied, tile + 1)
                sp.dma_start(out[tile * P:(tile + 1) * P, :], ob).then_inc(stored, 16)
            sp.wait_ge(stored, 16 * TT)

        @block.gpsimd
        def _(pool):
            for tile in range(TT):
                for quarter in range(TopK.PIECES):
                    pool.wait_ge(topk.ids_ready, TopK.PIECES * tile + quarter + 1)
                    pool.sem_inc(passed, 1)
                    with pool.Fori(quarter * QUARTER, (quarter + 1) * QUARTER) as i:
                        for b in range(2):
                            for s, (free, rows, table, loaded) in enumerate(((dotted, ur, u_emb, u_in), (mixed, vr, v_emb, v_in))):
                                pool.wait_ge(free[b], at(tile, i) + 1)
                                pool.sem_inc(passed, 1)
                                nc.gpsimd.tensor_copy(stg[b][s][:, :], ids[:, tile, bass.ds(i * 2 * RING + b * RING, RING)]).then_inc(staged[b], 1)
                                pool.wait_ge(staged[b], at(tile, i) * 2 + s + 1)
                                pool.sem_inc(passed, 1)
                                for r in range(RING):
                                    nc.gpsimd.indirect_dma_start(out=rows[b][r][:, :], out_offset=None, in_=table,
                                                                 in_offset=bass.IndirectOffsetOnAxis(ap=stg[b][s][:, r:r + 1], axis=0)).then_inc(loaded[b], 16)

        @block.vector
        def _(dve):
            for b in range(2):
                dve.sem_inc(dotted[b], 1)
            nc.vector.memset(zero[:, :], 0.0).then_inc(zeroed, 1)
            dve.wait_ge(gloaded, 16)
            for tile in range(TT):
                last = nc.vector.tensor_tensor(xn[:, tile, :], xn[:, tile, :], gb, ALU.mult)
            last.then_inc(gained, 1)
            dve.wait_ge(gained, 1)
            topk.then = Chain(dve, topk.step)
            for p in range(TopK.PIECES):
                dve.wait_ge(query.kept, (p + 1) * TopK.HEADS)
                topk.lists(0, p)
                topk.choose(0, p)
            topk.gates(dve, 0)
            for tile in range(TT):
                for start, end in segments(tile):
                    with dve.Fori(start, end) as i:
                        for b in range(2):
                            dve.wait_ge(u_in[b], (at(tile, i) + 1) * 16 * RING)
                            for r in range(RING):
                                last = nc.vector.tensor_tensor_reduce(ur[b][r][:, :], ur[b][r][:, :], xn[:, tile, :], 1.0, 0.0,
                                                                      ALU.mult, ALU.add, dot[b][:, r:r + 1])
                            last.then_inc(dotted[b], 1)
                            dve.wait_ge(gelud[b], at(tile, i) + 1)
                            nc.vector.tensor_tensor(wgt[b][:, :], gel[b][:, :], gate[:, tile, bass.ds(i * 2 * RING + b * RING, RING)],
                                                    ALU.mult).then_inc(weighed[b], 1)
                    if tile + 1 < TT:
                        if end in PIECE_AT:
                            p = PIECE_AT.index(end)
                            if tile == 0:
                                dve.wait_ge(query.kept, query.count(PH + (p + 1) * TopK.HEADS))
                            topk.lists(tile + 1, p)
                        elif end - 1 in PIECE_AT:
                            topk.choose(tile + 1, PIECE_AT.index(end - 1))
                        if end == GATES_AT:
                            topk.gates(dve, tile + 1)

        @block.scalar
        def _(act):
            def rounds(tile, start, end):
                with act.Fori(start, end) as i:
                    for b in range(2):
                        act.wait_ge(dotted[b], at(tile, i) + 2)
                        nc.scalar.activation(gel[b][:, :], dot[b][:, :], ACT.Gelu).then_inc(gelud[b], 1)
                        act.wait_ge(weighed[b], at(tile, i) + 1)
                        act.wait_ge(mixed[b], at(tile, i) + 1)
                        for r in range(RING):
                            last = nc.scalar.activation(diag[b][:, r, :], ident, ACT.Copy, scale=wgt[b][:, r:r + 1])
                        last.then_inc(spread[b], 1)

            for n in range(PH):
                query.copy_queries(act, n)
                if n:
                    query.keep_scores(act, n - 1)
            query.keep_scores(act, PH - 1)
            for n in range(PH, PH + EARLY):
                query.copy_queries(act, n)
                query.keep_scores(act, n)
            topk.exp(act, 0)
            for tile in range(TT):
                for start, end in segments(tile):
                    rounds(tile, start, end)
                    if tile == 0 and end in QUERY_AT:
                        n = PH + EARLY + QUERY_AT.index(end)
                        if n > PH + EARLY:
                            query.keep_scores(act, n - 1)
                        query.copy_queries(act, n)
                        if n == 2 * PH - 1:
                            query.keep_scores(act, n)
                    if tile + 1 < TT and end == GATES_AT:
                        topk.exp(act, tile + 1)
                act.wait_ge(closed, tile + 1)
                if tile:
                    act.wait_ge(stored, 16 * tile)
                for half in range(2):
                    last = nc.scalar.activation(ob[:, half * 512:(half + 1) * 512], acc[tile % 2][half][:, :], ACT.Copy)
                last.then_inc(copied, 1)

        @block.tensor
        def _(pe):
            for b in range(2):
                pe.sem_inc(mixed[b], 1)
            for n in range(PH):
                query.queries(pe, n)
                if n:
                    query.dots(pe, n - 1)
            query.dots(pe, PH - 1)
            for n in range(PH, PH + EARLY):
                query.queries(pe, n)
                query.dots(pe, n)
            pe.wait_ge(zeroed, 1)
            for tile in range(TT):
                if tile >= 2:
                    pe.wait_ge(copied, tile - 1)
                for half in range(2):
                    nc.tensor.matmul(acc[tile % 2][half][:, :], ident, core.x[:, tile, half * 512:(half + 1) * 512], start=True, stop=False,
                                     skip_group_check=True)
                for start, end in segments(tile):
                    with pe.Fori(start, end) as i:
                        for b in range(2):
                            pe.wait_ge(v_in[b], (at(tile, i) + 1) * 16 * RING)
                            pe.wait_ge(spread[b], at(tile, i) + 1)
                            for r in range(RING):
                                for half in range(2):
                                    last = nc.tensor.matmul(acc[tile % 2][half][:, :], diag[b][:, r, :], vr[b][r][:, half * 512:(half + 1) * 512],
                                                            start=False, stop=False, skip_group_check=True)
                            last.then_inc(mixed[b], 1)
                    if tile == 0 and end in QUERY_AT:
                        n = PH + EARLY + QUERY_AT.index(end)
                        query.queries(pe, n)
                        if n > PH + EARLY:
                            query.dots(pe, n - 1)
                        if n == 2 * PH - 1:
                            query.dots(pe, n)
                for half in range(2):
                    last = nc.tensor.matmul(acc[tile % 2][half][:, :], zero[:, :], core.x[:, tile, half * 512:(half + 1) * 512],
                                            start=False, stop=True, skip_group_check=True)
                last.then_inc(closed, 1)


def peer(nc, core, a, out):
    with ExitStack() as ctx:
        xn = sb(nc, ctx, "xn", [P, TT, D])
        h = sb(nc, ctx, "h3_t", [P, KD, T])
        ids = sb(nc, ctx, "expert_ids", [P, TT, SLOTS], U32)
        gate = sb(nc, ctx, "expert_gates", [P, TT, SLOTS])
        scores = sb(nc, ctx, "scores", [P, TT, 2 * PH, NK])
        stage_norm(nc, core, "nf", x_tiles(core), V_NORMF, None, natural=lambda i: xn[:, i, :], whole=h)
        stage_experts(nc, core, xn, h, a["norm_ffn_2"], a["keys"], scores, ids, gate, a["peer_u"], a["peer_v"], out)


def build(nc, a, scratch, out):
    with ExitStack() as stack:
        core = open_core(nc, stack, a)
        stage_load(nc, core, a)
        for part in (lambda: delta_block(nc, core, a), lambda: window_block(nc, core, a, scratch), lambda: mixers(nc, core, a), lambda: peer(nc, core, a, out)):
            before = nc.snapshot_sems()
            part()
            nc.clear_and_free_semaphores(nc.allocated_since(before))
            nc.all_engine_barrier()


def _columns(v):
    return np.reshape(v, (KD, P)).T


def _layout(i):
    consts, rows = shape_constants()
    v = np.zeros((P, V_WIDTH), np.float32)
    for name, at in (("a_norm", V_ANORM), ("kv_norm", V_KVNORM), ("b_norm", V_BNORM), ("norm_mix_2", V_NORM2), ("norm_ffn_2", V_NORMF)):
        v[:, at:at + KD] = _columns(i[name])
    for name, at in (("b_q_gain", V_QGK), ("k_gain", V_QGK + 1), ("f_q_norm_2", V_FQK), ("f_k_norm_2", V_FQK + 1)):
        v[0:HD, at] = v[HD:P, at] = np.reshape(i[name], HD)
    v[32:32 + HA, V_ALOG] = i["a_A_log"][0]
    v[32:32 + HA, V_DT] = i["a_dt_bias"][0]
    v[0:HM, V_BI] = i["b_igate_2"][0]
    v[32:32 + HM, V_BI] = i["b_fgate_m_2"][0]
    v[64:64 + HF, V_BI] = i["b_fgate_f_2"][0]
    taps = lambda w: np.transpose(np.reshape(w, (4, -1, P)), (2, 1, 0))
    return {
        "c128": consts, "c32": rows, "v128": v, "x": i["x"][0], "meta": i["meta_tokens_2"],
        "a_w_in": i["a_w_in"][0], "a_conv": taps(i["a_conv"][0]), "a_o_gain": i["a_o_gain"][0], "a_w_out": i["a_w_out"][0],
        "w_kv": i["w_kv"], "rel_bias": i["rel_bias"], "b_w_in": i["b_w_in"][0], "b_sinks": i["b_sinks"][0], "b_w_out": i["b_w_out"][0],
        "w_in_2": i["w_in_2"][0], "conv_qk_2": taps(i["conv_qk_2"][0]), "m_out_norm_2": i["m_out_norm_2"][0], "w_out_2": i["w_out_2"][0],
        "norm_ffn_2": i["norm_ffn_2"][0], "peer_query": i["peer_query_2"][0],
        "keys": np.transpose(np.reshape(i["peer_sub_keys_2"][0], (2 * PH, NK, P)), (2, 0, 1)),
        "peer_u": i["peer_u_2"][0], "peer_v": i["peer_v_2"][0],
    }


def kernel(**inputs):
    import concourse.bacc as bacc
    from concourse.bass_utils import run_bass_kernel_spmd

    nc = bacc.Bacc("TRN2", target_bir_lowering=False, num_devices=1)
    arrays, a = {}, {}
    for name, value in _layout({k: np.asarray(v) for k, v in inputs.items()}).items():
        arrays[f"in_{name}"] = np.ascontiguousarray(value)
        a[name] = nc.dram_tensor(f"in_{name}", value.shape, F32, kind="ExternalInput").ap()
    scratch = nc.dram_tensor("bias_rows", (HB, 384), F32, kind="Internal").ap()
    out = nc.dram_tensor("out_0", (T, D), F32, kind="ExternalOutput").ap()
    build(nc, a, scratch, out)
    r = run_bass_kernel_spmd(nc, [arrays], core_ids=[0])
    return r.results[0]["out_0"].reshape(1, T, D)
```
